# Optimizing a Trainium2 kernel written in Bass

```python
import jax, jax.numpy as jnp
from jax import lax
import numpy as np

D_MODEL = 1024
BATCH = 1
SEQ = 128
DEPTH = 2
DEC_BATCH = 1
DEC_SEQ = 512
PAST_LEN = 128

GRID_W = 64
N_MIXERS = 2
N_MLSTM = (DEPTH + 1) // 2
N_DELTA = DEPTH // 2
N_HEADS = 8
HEAD_DIM = D_MODEL // N_HEADS
D_INNER = N_HEADS * HEAD_DIM
N_GATE = 4 * N_HEADS
IN_DIM = 4 * D_INNER + N_GATE
CHUNK = 64
CONV_W = 5
N_EXPERTS = 16
CAP_FACTOR = 2
D_EXPERT = 1024
ADA_DIM = 6 * D_MODEL
EPS = 1e-6

kernel_name = 'hybrid_mlstm_gdn_ec_moe_diffusion_step'

def rmsnorm(x, g):
    xf = x.astype(jnp.float32)
    y = xf * lax.rsqrt(jnp.mean(xf * xf, -1, keepdims=True) + EPS)
    return (y * g.astype(jnp.float32)).astype(x.dtype)

def head_rmsnorm(x, g):
    return x * lax.rsqrt(jnp.mean(x * x, -1, keepdims=True) + EPS) * g.astype(jnp.float32)

def l2norm(x):
    return x * lax.rsqrt(jnp.sum(x * x, -1, keepdims=True) + EPS)

def to_heads(t):
    B, T, _ = t.shape
    return t.reshape(B, T, N_HEADS, HEAD_DIM).transpose(0, 2, 1, 3)

def from_heads(t):
    B, H, T, Dh = t.shape
    return t.transpose(0, 2, 1, 3).reshape(B, T, H * Dh)

def split_gates(p):
    B, T, _ = p.shape
    return jnp.moveaxis(p.reshape(B, T, 2, 2, N_HEADS), 1, -1)

def rev(t):
    return jnp.flip(t, 2)

def short_conv(x, w):
    pad = CONV_W // 2
    return lax.conv_general_dilated(x, w[:, None, :].astype(x.dtype), window_strides=(1,),
                                    padding=[(pad, pad)], dimension_numbers=('NWC', 'WIO', 'NWC'),
                                    feature_group_count=x.shape[-1])

def mlstm_dir(q, k, v, ig, lf, C0, n0, m0):
    B, H, T, _ = q.shape
    nc = T // CHUNK
    causal = jnp.tril(jnp.ones((CHUNK, CHUNK), bool))

    def split(t):
        return jnp.moveaxis(t.reshape(B, H, nc, CHUNK, *t.shape[3:]), 2, 0)

    def step(carry, xs):
        C, n, m = carry
        qc, kc, vc, ic, fc = xs
        b = jnp.cumsum(fc, -1)
        logd = jnp.where(causal, b[..., :, None] - b[..., None, :] + ic[..., None, :], -jnp.inf)
        inter = b + m[..., None]
        mt = jnp.maximum(inter, jnp.max(logd, -1))
        s = jnp.einsum('bhtd,bhsd->bhts', qc, kc) * jnp.exp(logd - mt[..., None])
        sc = jnp.exp(inter - mt)
        num = jnp.einsum('bhts,bhsv->bhtv', s, vc) + sc[..., None] * jnp.einsum('bhtd,bhdv->bhtv', qc, C)
        den = jnp.sum(s, -1) + sc * jnp.einsum('bhtd,bhd->bht', qc, n)
        h = num / jnp.maximum(jnp.abs(den), jnp.exp(-mt))[..., None]
        bl = b[..., -1]
        logw = bl[..., None] - b + ic
        m_new = jnp.maximum(bl + m, jnp.max(logw, -1))
        w = jnp.exp(logw - m_new[..., None])
        dec = jnp.exp(bl + m - m_new)
        C_new = dec[..., None, None] * C + jnp.einsum('bhs,bhsd,bhsv->bhdv', w, kc, vc)
        n_new = dec[..., None] * n + jnp.einsum('bhs,bhsd->bhd', w, kc)
        return (C_new, n_new, m_new), h

    carry0 = (C0.astype(jnp.float32), n0.astype(jnp.float32), m0.astype(jnp.float32))
    (C, n, m), h = lax.scan(step, carry0, tuple(split(t) for t in (q, k, v, ig, lf)))
    return jnp.moveaxis(h, 0, 2).reshape(B, H, T, -1), C, n, m

def delta_dir(q, k, v, g, beta, S0):
    B, H, T, _ = q.shape
    nc = T // CHUNK

    def split(t):
        return t.reshape(B, H, nc, CHUNK, *t.shape[3:])

    q, k, v, g, beta = split(q), split(k), split(v), split(g), split(beta)
    lower = jnp.tril(jnp.ones((CHUNK, CHUNK), bool))
    strict = jnp.tril(jnp.ones((CHUNK, CHUNK), bool), -1)
    G = jnp.cumsum(g, -1)
    decay = jnp.exp(jnp.where(lower, G[..., :, None] - G[..., None, :], -jnp.inf))
    kk = jnp.einsum('bhntd,bhnsd->bhnts', k, k)
    M = jnp.eye(CHUNK, dtype=jnp.float32) + jnp.where(strict, kk * decay * beta[..., :, None], 0.0)
    eG = jnp.exp(G)
    U = lax.linalg.triangular_solve(M, v * beta[..., None], left_side=True, lower=True, unit_diagonal=True)
    Wk = lax.linalg.triangular_solve(M, k * (beta * eG)[..., None], left_side=True, lower=True, unit_diagonal=True)
    qk = jnp.einsum('bhntd,bhnsd->bhnts', q, k) * decay
    kd = k * jnp.exp(G[..., -1:] - G)[..., None]
    eGl = eG[..., -1]

    def step(S, xs):
        qc, kdc, Uc, Wkc, qkc, eGc, eGlc = xs
        W = Uc - jnp.einsum('bhld,bhdv->bhlv', Wkc, S)
        o = eGc[..., None] * jnp.einsum('bhld,bhdv->bhlv', qc, S) + jnp.einsum('bhts,bhsv->bhtv', qkc, W)
        S_new = eGlc[..., None, None] * S + jnp.einsum('bhld,bhlv->bhdv', kdc, W)
        return S_new, o

    xs = tuple(jnp.moveaxis(t, 2, 0) for t in (q, kd, U, Wk, qk, eG, eGl))
    S, o = lax.scan(step, S0.astype(jnp.float32), xs)
    return jnp.moveaxis(o, 0, 2).reshape(B, H, T, -1), S

def mlstm_mixer(h, w_in, w_out, ig_b, fg_b, norm_g, C0, n0, m0):
    p = (h @ w_in).astype(jnp.float32)
    q = to_heads(p[..., :D_INNER])
    k = to_heads(p[..., D_INNER:2 * D_INNER]) * HEAD_DIM ** -0.5
    v = to_heads(p[..., 2 * D_INNER:3 * D_INNER])
    o = to_heads(p[..., 3 * D_INNER:4 * D_INNER])
    gates = split_gates(p[..., 4 * D_INNER:])
    ig = gates[:, :, 0] + ig_b.astype(jnp.float32)[None, :, :, None]
    lf = jax.nn.log_sigmoid(gates[:, :, 1] + fg_b.astype(jnp.float32)[None, :, :, None])
    hf, Cf, nf, mf = mlstm_dir(q, k, v, ig[:, 0], lf[:, 0], C0[:, 0], n0[:, 0], m0[:, 0])
    hb, Cb, nb, mb = mlstm_dir(rev(q), rev(k), rev(v), rev(ig[:, 1]), rev(lf[:, 1]), C0[:, 1], n0[:, 1], m0[:, 1])
    hn = head_rmsnorm(hf + rev(hb), norm_g.reshape(N_HEADS, 1, HEAD_DIM))
    y = from_heads(jax.nn.sigmoid(o) * hn).astype(h.dtype) @ w_out
    return y, (jnp.stack([Cf, Cb], 1), jnp.stack([nf, nb], 1), jnp.stack([mf, mb], 1))

def delta_mixer(h, w_in, w_out, conv_w, A_log, dt_bias, norm_g, S0, rows):
    B, T, _ = h.shape
    p = h @ w_in
    qkv = short_conv(p[..., :3 * D_INNER].reshape(B * rows, T // rows, 3 * D_INNER), conv_w)
    qkv = jax.nn.silu(qkv).reshape(B, T, 3 * D_INNER).astype(jnp.float32)
    q = l2norm(to_heads(qkv[..., :D_INNER])) * HEAD_DIM ** -0.5
    k = l2norm(to_heads(qkv[..., D_INNER:2 * D_INNER]))
    v = to_heads(qkv[..., 2 * D_INNER:])
    z = to_heads(p[..., 3 * D_INNER:4 * D_INNER].astype(jnp.float32))
    gates = split_gates(p[..., 4 * D_INNER:].astype(jnp.float32))
    g = -jnp.exp(A_log.astype(jnp.float32))[None, :, :, None] * jax.nn.softplus(
        gates[:, :, 0] + dt_bias.astype(jnp.float32)[None, :, :, None])
    beta = jax.nn.sigmoid(gates[:, :, 1])
    of, Sf = delta_dir(q, k, v, g[:, 0], beta[:, 0], S0[:, 0])
    ob, Sb = delta_dir(rev(q), rev(k), rev(v), rev(g[:, 1]), rev(beta[:, 1]), S0[:, 1])
    o = head_rmsnorm(of + rev(ob), norm_g) * jax.nn.silu(z)
    y = from_heads(o).astype(h.dtype) @ w_out
    return y, jnp.stack([Sf, Sb], 1)

def expert_choice_ffn(x, w_router, w_gate, w_up, w_down):
    B, T, _ = x.shape
    cap = CAP_FACTOR * T // N_EXPERTS
    aff = jax.nn.softmax((x @ w_router).astype(jnp.float32), -1)
    gsel, idx = lax.top_k(jnp.swapaxes(aff, 1, 2), cap)
    bidx = jnp.arange(B)[:, None, None]
    xs = x[bidx, idx]
    hdn = jax.nn.silu(jnp.einsum('becd,edf->becf', xs, w_gate)) * jnp.einsum('becd,edf->becf', xs, w_up)
    out = jnp.einsum('becf,efd->becd', hdn, w_down) * gsel[..., None].astype(x.dtype)
    return jnp.zeros_like(x).at[bidx, idx].add(out)

def modulation(cond, w_ada, b_ada):
    m = jax.nn.silu(cond) @ w_ada + b_ada
    return jnp.split(m[:, None, :], 6, axis=-1)

def trunk(x, cond, rows, mC, mn, mm, dS, params):
    (norm1_g, norm2_g, w_ada, b_ada, w_in, w_out, w_router, w_gate, w_up, w_down, final_g,
     mlstm_ig_b, mlstm_fg_b, mlstm_norm_g, delta_conv_w, delta_A_log, delta_dt_bias, delta_norm_g) = params
    m_states, d_states = [], []
    for i in range(DEPTH):
        sh1, sc1, g1, sh2, sc2, g2 = modulation(cond, w_ada[i], b_ada[i])
        h = rmsnorm(x, norm1_g[i]) * (1 + sc1) + sh1
        j = i // N_MIXERS
        if i % N_MIXERS == 0:
            y, st = mlstm_mixer(h, w_in[i], w_out[i], mlstm_ig_b[j], mlstm_fg_b[j], mlstm_norm_g[j],
                                mC[:, j], mn[:, j], mm[:, j])
            m_states.append(st)
        else:
            y, st = delta_mixer(h, w_in[i], w_out[i], delta_conv_w[j], delta_A_log[j], delta_dt_bias[j],
                                delta_norm_g[j], dS[:, j], rows)
            d_states.append(st)
        x = x + g1 * y
        h = rmsnorm(x, norm2_g[i]) * (1 + sc2) + sh2
        x = x + g2 * expert_choice_ffn(h, w_router[i], w_gate[i], w_up[i], w_down[i])
    new_C = jnp.stack([s[0] for s in m_states], 1)
    new_n = jnp.stack([s[1] for s in m_states], 1)
    new_m = jnp.stack([s[2] for s in m_states], 1)
    new_S = jnp.stack(d_states, 1)
    return rmsnorm(x, final_g), new_C, new_n, new_m, new_S

def setup_inputs(seed: int = 0) -> dict:
    key = jax.random.key(seed)
    ks = jax.random.split(key, 28)
    f32 = jnp.float32
    D = D_MODEL

    def nrm(k, shape, s):
        return jax.random.normal(k, shape, f32) * s

    dt = jnp.exp(jax.random.uniform(ks[25], (N_DELTA, 2, N_HEADS), f32, np.log(1e-3), np.log(1e-1)))
    return {
        'x_prompt': nrm(ks[0], (BATCH, SEQ, D), 1.0),
        'x_sample': nrm(ks[1], (DEC_BATCH, DEC_SEQ, D), 1.0),
        'state_mlstm_C': nrm(ks[2], (DEC_BATCH, N_MLSTM, 2, N_HEADS, HEAD_DIM, HEAD_DIM), 0.1),
        'state_mlstm_n': nrm(ks[3], (DEC_BATCH, N_MLSTM, 2, N_HEADS, HEAD_DIM), 0.1),
        'state_mlstm_m': nrm(ks[4], (DEC_BATCH, N_MLSTM, 2, N_HEADS), 1.0),
        'state_delta_S': nrm(ks[5], (DEC_BATCH, N_DELTA, 2, N_HEADS, HEAD_DIM, HEAD_DIM), 0.1),
        'c': nrm(ks[6], (DEC_BATCH, D), 1.0),
        'c_ctx': nrm(ks[7], (D,), 1.0),
        'norm1_g': 1.0 + nrm(ks[8], (DEPTH, D), 0.02),
        'norm2_g': 1.0 + nrm(ks[9], (DEPTH, D), 0.02),
        'w_ada': nrm(ks[10], (DEPTH, D, ADA_DIM), 0.5 * D ** -0.5),
        'b_ada': nrm(ks[11], (DEPTH, ADA_DIM), 0.02),
        'w_in': nrm(ks[12], (DEPTH, D, IN_DIM), D ** -0.5),
        'w_out': nrm(ks[13], (DEPTH, D_INNER, D), D_INNER ** -0.5),
        'w_router': nrm(ks[14], (DEPTH, D, N_EXPERTS), D ** -0.5),
        'w_gate': nrm(ks[15], (DEPTH, N_EXPERTS, D, D_EXPERT), D ** -0.5),
        'w_up': nrm(ks[16], (DEPTH, N_EXPERTS, D, D_EXPERT), D ** -0.5),
        'w_down': nrm(ks[17], (DEPTH, N_EXPERTS, D_EXPERT, D), D_EXPERT ** -0.5),
        'final_g': 1.0 + nrm(ks[18], (D,), 0.02),
        'mlstm_ig_b': nrm(ks[19], (N_MLSTM, 2, N_HEADS), 0.1),
        'mlstm_fg_b': jax.random.uniform(ks[20], (N_MLSTM, 2, N_HEADS), f32, 3.0, 6.0),
        'mlstm_norm_g': 1.0 + nrm(ks[21], (N_MLSTM, D_INNER), 0.02),
        'delta_conv_w': nrm(ks[22], (N_DELTA, CONV_W, 3 * D_INNER), CONV_W ** -0.5),
        'delta_A_log': jnp.log(jax.random.uniform(ks[23], (N_DELTA, 2, N_HEADS), f32, 1.0, 16.0)),
        'delta_dt_bias': dt + jnp.log(-jnp.expm1(-dt)),
        'delta_norm_g': 1.0 + nrm(ks[24], (N_DELTA, HEAD_DIM), 0.02),
    }

def reference(x_prompt, x_sample, state_mlstm_C, state_mlstm_n, state_mlstm_m, state_delta_S, c, c_ctx,
              norm1_g, norm2_g, w_ada, b_ada, w_in, w_out, w_router, w_gate, w_up, w_down, final_g,
              mlstm_ig_b, mlstm_fg_b, mlstm_norm_g, delta_conv_w, delta_A_log, delta_dt_bias, delta_norm_g):
    params = (norm1_g, norm2_g, w_ada, b_ada, w_in, w_out, w_router, w_gate, w_up, w_down, final_g,
              mlstm_ig_b, mlstm_fg_b, mlstm_norm_g, delta_conv_w, delta_A_log, delta_dt_bias, delta_norm_g)
    f32 = jnp.float32
    nb = x_prompt.shape[0]
    zC = jnp.zeros((nb, N_MLSTM, 2, N_HEADS, HEAD_DIM, HEAD_DIM), f32)
    zn = jnp.zeros((nb, N_MLSTM, 2, N_HEADS, HEAD_DIM), f32)
    zm = jnp.zeros((nb, N_MLSTM, 2, N_HEADS), f32)
    zS = jnp.zeros((nb, N_DELTA, 2, N_HEADS, HEAD_DIM, HEAD_DIM), f32)
    y_prompt, new_mlstm_C, new_mlstm_n, new_mlstm_m, new_delta_S = trunk(
        x_prompt, c_ctx[None, :], 1, zC, zn, zm, zS, params)
    rows = x_sample.shape[1] // GRID_W
    y_sample = trunk(x_sample, c, rows, state_mlstm_C, state_mlstm_n, state_mlstm_m, state_delta_S, params)[0]
    return (y_prompt, y_sample, new_mlstm_C, new_mlstm_n, new_mlstm_m, new_delta_S)


_drawn_inputs = setup_inputs


def setup_inputs(seed=0):
    import zlib

    import numpy as np

    out = dict(_drawn_inputs(seed))
    spreads = {}
    factors = {'state_mlstm_C': 3.483,
     'state_mlstm_n': 7.772,
     'state_mlstm_m': 5.051,
     'state_delta_S': 3.452,
     'norm2_g': 6.457,
     'final_g': 7.927,
     'mlstm_norm_g': 8.0,
     'delta_norm_g': 53.295}
    for name, (base, spread) in spreads.items():
        noise = np.random.default_rng([zlib.crc32(name.encode()), seed]).standard_normal(out[name].shape)
        drawn = base * np.exp(spread * noise) if base else spread * noise
        out[name] = __import__('jax').numpy.asarray(drawn.astype(out[name].dtype))
    for name, factor in factors.items():
        out[name] = (out[name] * factor).astype(out[name].dtype)
    return out
```

```python
from contextlib import ExitStack

import concourse.bass as bass
from concourse import mybir

F32 = mybir.dt.float32
U16 = mybir.dt.uint16
BF16 = mybir.dt.bfloat16
U32 = mybir.dt.uint32
ALU = mybir.AluOpType
ACT = mybir.ActivationFunctionType
AX = mybir.AxisListType.X

P = 128
D = 1024
KT = D // P
NT = 5
TOK = NT * P
H = 8
EX = 16
CAPS = 64
CAPP = 16
CAP = CAPS + CAPP
HC = 512
MOD = 48
EPS = 1e-6
LEVELS = 7
TAPS = 5
ROWW = 64
NROW = 8
UNITS = [(0, 1), (1, 4), (0, 2), (1, 3), (0, 3), (1, 2), (0, 4), (1, 1), (0, 0), (1, 0)]
SECOND = {(0, 3), (1, 2), (0, 4), (1, 1), (1, 0)}


PER = dict(ada_ev=12, fin_r=5, fin_i=5, ab=1, ada_mm=12, afft=1, aff=1, fin_read=5, fin_sq=10, fin_start=1, g1b=4, g1e=4, g2b=4,
           gathered=256, gexp=32, gmm=1, h_chain=32, hidden=32, idx=16, logits=1, moe_used=96, o_ready=32,
           omm=10, scattered=256, selt=1, sel=2, sme=1, sm=1, st_new=4, topk=1, x_moe=5, x_new=10, xs_a=64,
           xs_in=16, xs_turned=16, yt_ev=10, yt=5, y=5, xn=5, xt=10, hta=20, htv=5, sq=5)


def backbone(nc, a):
    ctx = ExitStack()
    sems = {}

    def S(name):
        if name not in sems:
            sems[name] = ctx.enter_context(nc.semaphore(name))
        return sems[name]

    def sb(name, shape, dt=F32):
        return ctx.enter_context(nc.sbuf_tensor(name, shape, dt))

    def bc(ap, shape):
        return ap.broadcast_to(shape)

    def heads(ap, n=P):
        return ap.unsqueeze(2).broadcast_to([ap.shape[0], ap.shape[1], n])

    with ctx:
        PS = ctx.enter_context(nc.psum_tensor("ps", [P, 8, HC], F32))

        x = sb("x", [P, NT, D])
        hT = sb("hT", [P, KT, TOK])
        acc = hT[:, :, :].rearrange("p a b -> p (a b)").rearrange("p (t d) -> p t d", t=NT)
        qkv = sb("qkv", [P, 3 * NT * D])
        qT = qkv[:, 0:NT * D].rearrange("p (k t) -> p k t", k=KT)
        kT = qkv[:, NT * D:2 * NT * D].rearrange("p (k t) -> p k t", k=KT)
        v = qkv[:, 2 * NT * D:3 * NT * D].rearrange("p (t d) -> p t d", t=NT)
        yT = qT
        og = sb("og", [P, NT * D])
        o = og[:, :].rearrange("p (t d) -> p t d", t=NT)
        slots3 = sb("slots3", [P, 3, KT * HC])
        SL = [slots3[:, j, :] for j in range(3)] + [qkv[:, j * KT * HC:(j + 1) * KT * HC] for j in range(3)]
        slot = [s.rearrange("p (k n) -> p k n", k=KT) for s in SL]
        wk = sb("wk", [P, 4608])
        half = [slots3[:, 2, j * HC:(j + 1) * HC] for j in range(8)]
        c32 = sb("c32", [P, 6, P])
        ident, TU, TL, NU, NL, ones = (c32[:, j, :] for j in range(6))
        tri = [TU, TL]
        neg_ts = [NL, NU]
        neg_st = [NU, NL]
        lmask = sb("lmask", [P, 2 * LEVELS, P], U16)
        rows = sb("rows", [P, 3, P])
        vecT = sb("vecT", [P, 264])
        norm_g = vecT[:, 0:32].rearrange("p (k l t) -> p k l t", k=2, l=2)
        biasT = vecT[:, 48:144].rearrange("p (l b) -> p l b", l=2)
        convT = vecT[:, 144:264].rearrange("p (j c) -> p j c", j=TAPS)
        cnd = sb("cnd", [P, 3, 16])
        modT = sb("modT", [P, MOD, 2])
        AB = sb("AB", [P, 2, KT, 2])
        ss = sb("ss", [P, 4, 16])
        epst = sb("epst", [P, 1])
        tick = sb("tick", [1, 1])
        wgt = sb("wgt", [P, KT, 32])
        wrt = sb("wrt", [P, KT, EX])
        gb0 = sb("gb0", [P, 2, 2, H])
        gb1 = sb("gb1", [P, 2, 2, H])
        m0 = sb("m0", [P, 2, H])
        dng = sb("dng", [P, P])
        nst = sb("nst", [P, 2, H])
        ga = sb("ga", [P, 14, NT * 2 * H])
        G3 = [ga[:, j, :].rearrange("p (t d h) -> p t d h", t=NT, d=2) for j in range(14)]
        sm = sb("sm", [P, 2, 4, 4])
        gt = sb("gt", [P, NT, 2, 2, H])
        aff = sb("aff", [P, NT, EX])
        af5 = sb("af5", [P, 2, NT])
        vals = sb("vals", [EX, CAP])
        idx = sb("idx", [EX, CAP], U32)
        idf = sb("idf", [EX, CAP])
        gsel = sb("gsel", [P, EX])
        idT = sb("idT", [P, EX], U32)
        idc = [sb(f"idc{q}", [P, 1], U32) for q in range(2)]
        gsc = [sb(f"gsc{q}", [P, 1]) for q in range(2)]

        xn_d = nc.dram_tensor("xn_d", [TOK, D], F32, kind="Internal").ap()
        moe_d = nc.dram_tensor("moe_d", [TOK, D], F32, kind="Internal").ap()

        xs = [og[:, q * D:(q + 1) * D] for q in range(2)]
        osb = [og[:, (2 + q) * D:(3 + q) * D] for q in range(2)]
        hdT = og[:, 4 * D:4 * D + KT * CAP].rearrange("p (k c) -> p k c", k=KT)
        xsT = [wk[:, q * 640:(q + 1) * 640].rearrange("p (k c) -> p k c", k=KT) for q in range(2)]
        eb = [wk[:, 1280 + q * 320:1600 + q * 320] for q in range(2)]
        affS = wk[0:EX, 2048:2560]
        affP = wk[0:EX, 2560:2688]
        zero = wk[:, 3072:4096]
        grow = wk[:, 3072:4096]
        mrow = [wk[0:2, 2048 + q * HC:2048 + (q + 1) * HC] for q in range(2)]
        Cst = wk[:, 0:2048].rearrange("p (d h v) -> p d h v", d=2, h=H)
        cpad = [wk[:, q * 676:(q + 1) * 676] for q in range(2)]
        cout = [wk[:, 1352 + q * 640:1992 + q * 640] for q in range(2)]
        cex = wk[:, 2632:3272]
        qn = wk[:, 3272:3912].rearrange("p (t c) -> p t c", t=NT)

        def four(ap):
            return ap.rearrange("p (h n) -> p h n", h=4)

        def w_ada(L):
            return a["w_ada"][L].rearrange("(k p) n -> p k n", p=P)

        def w_in(L):
            return a["w_in"][L].rearrange("(k p) n -> p k n", p=P)

        def w_out(L):
            return a["w_out"][L].rearrange("(k p) n -> p k n", p=P)

        NADA, NIN, NOUT = 12, 8, 2
        MIX = NADA + NIN + NOUT

        def mix_slot(n):
            return n % 3 if n < NADA + NIN else n - NADA - NIN

        def mix_landed(L, n):
            j = mix_slot(n)
            return 16 * (sum(mix_slot(k) == j for k in range(n + 1)) + L * (sum(mix_slot(k) == j for k in range(MIX)) + EX))

        def item_end(L, g):
            fm = (4, 6)[L]
            return 4 * (g + 1) if g < fm else 4 * fm + NT * (g + 1 - fm)

        def unit_used(L, n):
            if n < NADA:
                return S("ada_mm"), L * PER["ada_mm"] + n + 1
            if n < NADA + NIN:
                return S(f"pj_mm{L}"), item_end(L, n - NADA)
            return S("omm"), L * PER["omm"] + NT * (n - NADA - NIN + 1)

        def moe_base(L, j):
            return ((L + 1) * sum(mix_slot(k) == j for k in range(MIX)) if j < 3 else 0) + L * EX

        BETA, GC, NG, EG, EGL, EKD, BEG = G3[4], G3[5], G3[6], G3[7], G3[8], G3[9], G3[10]

        def dbuf(p):
            b = half + [wk[:, 2048 + j * HC:2048 + (j + 1) * HC] for j in range(4)]
            six = [four(z) for z in b[6 * p:6 * p + 6]]
            xb = wk[:, 4096 + 256 * p:4096 + 256 * (p + 1)].rearrange("p (h n) -> p h n", h=4)
            return dict(E=six[0], CM=six[0], nWk=six[0], AT=six[1], bv=six[1], D=six[2], kd=six[2],
                        DT=six[3], t=six[3], qk=six[4], kb=six[5], W=six[5], X=xb)

        fsq = slots3[:, 2, 0:1024]
        fex = slots3[:, 2, 1024:2048]
        g1b = slots3[:, 2, 2048:4096].rearrange("p (c j n) -> p c j n", c=2, j=2)
        ytmp = slots3[:, 2, 0:HC]
        cjunk = wk[:, 3912:4040]

        def cols(ap, l, which):
            return ap.rearrange("p h (b w s) -> p h b w s", w=2, s=2 ** l)[:, :, :, which, :]

        def cols1(ap, l, which):
            return ap.rearrange("p (b w s) -> p b w s", w=2, s=2 ** l)[:, :, which, :]

        def pack(ap, l):
            return ap.rearrange("p h (b s) -> p h b s", s=2 ** l)

        land = [S(f"landed{j}") for j in range(6)]
        block = ctx.enter_context(nc.Block())

        @block.sync
        def _(sp):
            with nc.allow_non_contiguous_dma(reason="small vectors"):
                loads = [
                    (c32[:, :, :], a["c32"]), (lmask[:, :, :], a["lmask"]),
                    (rows[0:16, 0, :], a["norm1_g"].rearrange("l (t p) -> (l t) p", p=P)),
                    (rows[16:32, 0, :], a["norm2_g"].rearrange("l (t p) -> (l t) p", p=P)),
                    (rows[32:40, 0, :], a["c_ctx"].rearrange("(t p) -> t p", p=P)),
                    (rows[40:48, 0, :], a["c"].rearrange("b (t p) -> (b t) p", p=P)),
                    (rows[0:96, 1, :], a["b_ada"].rearrange("l (t p) -> (l t) p", p=P)),
                    (rows[0:120, 2, :], a["delta_conv_w"][0].rearrange("j (t p) -> (j t) p", p=P)),
                    (gb0[:, :, 0, :], a["mlstm_ig_b"][0].partition_broadcast(P)),
                    (gb0[:, :, 1, :], a["mlstm_fg_b"][0].partition_broadcast(P)),
                    (gb1[:, :, 0, :], a["delta_A_log"][0].partition_broadcast(P)),
                    (gb1[:, :, 1, :], a["delta_dt_bias"][0].partition_broadcast(P)),
                    (m0[:, :, :], a["state_mlstm_m"][0, 0].partition_broadcast(P)),
                    (dng[:, :], a["delta_norm_g"][0].partition_broadcast(P)),
                ]
                for dst, src in loads:
                    sp.dma_start(dst, src).then_inc(S("setup"), 16)
            sp.dma_start(x[:, 0, :], a["x_prompt"][0]).then_inc(S("x_in"), 16)
            sp.dma_start(x[:, 1:5, :], a["x_sample"][0].rearrange("(t p) d -> p t d", p=P)).then_inc(S("x_in"), 16)

            for L in range(2):
                if L == 1:
                    sp.wait_ge(S("gmm"), 1)
                sp.dma_start(wgt[:, :, :], w_in(L)[:, :, 4 * D:4 * D + 32]).then_inc(S("wg_in"), 16)
                if L == 1:
                    sp.wait_ge(S("logits"), 1)
                sp.dma_start(wrt[:, :, :], a["w_router"][L].rearrange("(k p) e -> p k e", p=P)).then_inc(S("wr_in"), 16)
                for n in range(NADA + NIN):
                    j = mix_slot(n)
                    if n < 3:
                        if L:
                            sp.wait_ge(S("moe_used"), 6 * (EX - 1) + j + 1)
                    else:
                        sp.wait_ge(*unit_used(L, n - 3))
                    if n < NADA:
                        src = w_ada(L)[:, :, n * HC:(n + 1) * HC]
                    else:
                        g = n - NADA
                        src = w_in(L)[:, :, g * HC:(g + 1) * HC]
                    sp.dma_start(slot[j], src).then_inc(land[j], 16)
                st = a["state_mlstm_C" if L == 0 else "state_delta_S"][0, 0]
                if L == 1:
                    sp.wait_ge(S("tr1"), 24)
                for d in range(2):
                    sp.dma_start(Cst[:, d, :, :], st[d].rearrange("h k v -> k h v")).then_inc(S("st_in"), 16)
                if L == 0:
                    with nc.allow_non_contiguous_dma(reason="normaliser state, 2048 numbers"):
                        for d in range(2):
                            sp.dma_start(nst[:, d, :], a["state_mlstm_n"][0, 0, d].rearrange("h k -> k h")).then_inc(S("st_in"), 16)
                    sp.dma_start(grow, a["mlstm_norm_g"][0].partition_broadcast(P)).then_inc(S("grow_in"), 16)
                sp.wait_ge(S("st_new"), L * PER["st_new"] + 4)
                out = a["out_C" if L == 0 else "out_S"][0, 0]
                for d in range(2):
                    sp.dma_start(out[d].rearrange("h k v -> k h v"), Cst[:, d, :, :]).then_inc(S("st_out"), 16)
                if L == 0:
                    with nc.allow_non_contiguous_dma(reason="normaliser state, 2048 numbers"):
                        for d in range(2):
                            sp.dma_start(a["out_n"][0, 0, d].rearrange("h k -> k h"), nst[:, d, :]).then_inc(S("st_out"), 16)
                    sp.dma_start(a["out_m"][0], G3[13][0:1, 0, :, :]).then_inc(S("st_out"), 16)

                sp.wait_ge(S("fin_start"), L + 1)
                for j in range(NOUT):
                    sp.dma_start(slot[j], w_out(L)[:, :, j * HC:(j + 1) * HC]).then_inc(land[j], 16)

                for t in range(NT):
                    sp.wait_ge(S("xn"), (2 * L + 1) * PER["xn"] + t + 1)
                    sp.dma_start(xn_d[t * P:(t + 1) * P, :], o[:, t, :]).then_inc(S("xn_out"), 16)
                gv = a["w_gate"][L].rearrange("e (k p) n -> e p k n", p=P)
                uv = a["w_up"][L].rearrange("e (k p) n -> e p k n", p=P)
                dv = a["w_down"][L].rearrange("e (k p) n -> e p k n", p=P)
                six = [(gv, 0), (uv, 0), (gv, 1), (uv, 1), (dv, 0), (dv, 1)]

                def expert_loads(e, first):
                    for j, (w, hf) in enumerate(six):
                        if not first:
                            sp.wait_ge(S("moe_used"), L * PER["moe_used"] + e * 6 + (j - 5))
                        sp.dma_start(slot[j], w[e, :, :, hf * HC:(hf + 1) * HC]).then_inc(land[j], 16)

                sp.wait_ge(*unit_used(L, MIX - 1))
                sp.wait_ge(S("x_new"), L * PER["x_new"] + 10)
                expert_loads(0, True)
                with sp.Fori(1, EX) as e:
                    expert_loads(e, False)
                sp.wait_ge(S("scattered"), L * PER["scattered"] + 16 * EX)
                for t in range(NT):
                    sp.dma_start(o[:, t, :], moe_d[t * P:(t + 1) * P, :]).then_inc(S("moe_in"), 16)
            sp.dma_start(grow, a["final_g"].partition_broadcast(P)).then_inc(S("grow_in"), 16)
            for t in range(NT):
                sp.wait_ge(S("y_ready"), t + 1)
                dst = a["out_p"][0] if t == 0 else a["out_s"][0, (t - 1) * P:t * P, :]
                sp.dma_start(dst, o[:, t, :]).then_inc(S("y_out"), 16)
            sp.wait_ge(S("y_out"), 16 * NT)
            sp.wait_ge(S("st_out"), 16 * 7)

        @block.gpsimd
        def _(pool):
            pool.memset(epst[:, :], EPS).then_inc(S("epst"), 1)

            def delta_pool(pool):
                pool.wait_ge(S("tr1"), 24)
                pool.wait_ge(S("tr2"), 16)
                for u, (d, t) in enumerate(UNITS):
                    for p in range(2):
                        n = 2 * u + p
                        B = dbuf(p)
                        if u:
                            pool.wait_ge(S("dl_done"), n - 1)
                        idb = ident.unsqueeze(1).broadcast_to([P, 4, P])
                        pool.tensor_copy(B["D"], idb).then_inc(S("dl_init"), 1)
                        pool.tensor_copy(B["DT"], idb).then_inc(S("dl_init"), 1)
                    for l in range(LEVELS):
                        for p in range(2):
                            n = 2 * u + p
                            B = dbuf(p)
                            if l == 0:
                                pool.wait_ge(S("dl_at"), n + 1)
                            else:
                                pool.wait_ge(S("dl_x"), (u * LEVELS + l - 1) * 2 + p + 1)
                            mk = lmask[:, d * LEVELS + l, :].bitcast(BF16).unsqueeze(1).broadcast_to([P, 4, P])
                            pool.tensor_tensor(B["CM"], B["AT"], mk, ALU.mult).then_inc(S("dl_cm"), 1)
                    for p in range(2):
                        n = 2 * u + p
                        B = dbuf(p)
                        pool.wait_ge(S("dl_cm"), (u * LEVELS + LEVELS - 1) * 2 + p + 1)
                        pool.tensor_tensor(B["bv"], four(v[:, t, p * HC:(p + 1) * HC]),
                                           heads(BETA[:, t, d, 4 * p:4 * p + 4]), ALU.mult).then_inc(S("dl_bv"), 1)

            for L in range(2):
                if L == 1:
                    delta_pool(pool)
                if L == 1:
                    pool.wait_ge(S("moe_in"), 16 * NT)
                pool.wait_ge(S("x_new"), L * PER["x_new"] + 10)
                pool.wait_ge(S("st_out"), 16 * (5 if L == 0 else 7))
                pool.memset(zero, 0.0).then_inc(S("zeroed"), 1)
                pool.wait_ge(S("zeroed"), L + 1)
                for t in range(NT):
                    pool.dma_start(moe_d[t * P:(t + 1) * P, :], zero).then_inc(S("zero_out"), 16)

                def hold(before):
                    if not (isinstance(before, int) and before == 0):
                        pool.wait_ge(S("held"), before)
                    pool.tensor_tensor(tick[:, 0:1], epst[0:1, :], epst[0:1, :], ALU.mult).then_inc(S("held"), 1)

                def gather(e, q, first):
                    pool.wait_ge(S("idx"), L * PER["idx"] + e + 1)
                    if not first:
                        pool.wait_ge(S("xs_turned"), L * PER["xs_turned"] + e - 1)
                    hold(2 * EX * L + e if first else e * 2 + (2 * EX * L - 1))
                    pool.indirect_dma_start(xs[q][0:CAP, :], None, xn_d,
                                            bass.IndirectOffsetOnAxis(ap=idc[q][0:CAP, :], axis=0)).then_inc(S("gathered"), 16)

                def scatter(e, q, first):
                    pool.wait_ge(S("o_ready"), L * PER["o_ready"] + e * 2 + 2)
                    if not first:
                        pool.wait_ge(S("scattered"), L * PER["scattered"] + e * 16)
                    hold(2 * EX * L + (2 * EX - 1) if e is EX - 1 else e * 2 + (2 * EX * L + 2))
                    pool.indirect_dma_start(moe_d, bass.IndirectOffsetOnAxis(ap=idc[q][0:CAP, :], axis=0),
                                            osb[q][0:CAP, :], None, compute_op=ALU.add).then_inc(S("scattered"), 16)

                pool.wait_ge(S("xn_out"), 16 * NT * (L + 1))
                pool.wait_ge(S("zero_out"), 16 * NT * (L + 1))
                gather(0, 0, True)
                gather(1, 1, True)
                scatter(0, 0, True)
                gather(2, 0, False)
                scatter(1, 1, False)
                with pool.Fori(1, EX // 2 - 1) as i:
                    for q in range(2):
                        gather(i * 2 + (q + 1), 1 - q, False)
                        scatter(i * 2 + q, q, False)
                gather(EX - 1, 1, False)
                scatter(EX - 2, 0, False)
                scatter(EX - 1, 1, False)
                pool.wait_ge(S("scattered"), L * PER["scattered"] + 16 * EX)

        @block.scalar
        def _(act):
            A = nc.scalar.activation

            chain = [0]

            def link(ins):
                chain[0] += 1
                ins.then_inc(S("act_chain"), 1)
                act.wait_ge(S("act_chain"), chain[0])

            def inverse_root(dst, src, scale):
                link(A(dst, src, ACT.Ln, scale=scale, bias=epst[:, 0:1]))
                return A(dst, dst, ACT.Exp, scale=-0.5)

            act.wait_ge(S("vec"), 1)
            act.wait_ge(S("epst"), 1)
            A(cnd[:, 0, :], vecT[:, 32:48], ACT.Exp, scale=-1.0).then_inc(S("cexp"), 1)

            def norm(i):
                for t in range(NT):
                    act.wait_ge(S("x_in"), 32) if i == 0 else act.wait_ge(*x_ready(i, t))
                    link(A(o[:, t, :], x[:, t, :], ACT.Square, accum_out=ss[:, 0, t:t + 1]))
                    inverse_root(ss[:, 1, t:t + 1], ss[:, 0, t:t + 1], 1.0 / D).then_inc(S("sq"), 1)

            def x_ready(i, t):
                if i in (1, 3):
                    return S("x_new"), PER["x_new"] * (i // 2 + 1)
                return S("x_moe"), PER["x_moe"] * (i // 2 - 1) + t + 1

            def norm_evac(L, k):
                for t in range(NT):
                    act.wait_ge(S("xt"), (2 * L + k) * PER["xt"] + 2 * t + 1)
                    if t == 0:
                        act.wait_ge(S("ab"), L * PER["ab"] + 1)
                    c = int(t > 0)
                    for kt in range(4):
                        A(hT[:, kt, t * P:(t + 1) * P], PS[:, 2 * (t % 2) + 2, kt * P:(kt + 1) * P], ACT.Identity,
                          scale=AB[:, k, kt, c:c + 1], bias=modT[:, 24 * k + kt, c:c + 1]).then_inc(S("hta"), 1)

            def proj(L):
                if L == 0:
                    for i in range(36):
                        act.wait_ge(S("pj_mm0"), i + 1)
                        b = 2 * (i % 3)
                        if i < 16:
                            dst = (qT if i < 8 else kT)[:, i % 8, :]
                            sc = 1.0 if i < 8 else float(P) ** -0.5
                            A(dst[:, P:TOK], PS[:, b, :], ACT.Copy, scale=sc)
                            A(dst[:, 0:P], PS[:, b + 1, 0:P], ACT.Copy, scale=sc).then_inc(S("pj_ev0"), 1)
                        else:
                            g, t = divmod(i - 16, NT)
                            dst = (v if g < 2 else o)[:, t, (g % 2) * HC:(g % 2 + 1) * HC]
                            A(dst, PS[:, b, :], ACT.Copy).then_inc(S("pj_ev0"), 1)
                    return

                def evac(i):
                    act.wait_ge(S("pj_mm1"), i + 1)
                    b = 2 * (i % 3)
                    if i < 24:
                        if i == 0:
                            act.wait_ge(S("padded"), 2)
                        if i >= 2:
                            act.wait_ge(S("cv_done"), i - 1)
                        A(cpad[i % 2][:, 132:676].rearrange("p (r w) -> p r w", r=NROW)[:, :, 2:2 + ROWW],
                          PS[:, b, :].rearrange("p (r w) -> p r w", r=NROW), ACT.Copy)
                        A(cpad[i % 2][:, 2:130], PS[:, b + 1, 0:P], ACT.Copy).then_inc(S("pj_ev1"), 1)
                    else:
                        g, t = divmod(i - 24, NT)
                        A(o[:, t, g * HC:(g + 1) * HC], PS[:, b, :], ACT.Copy).then_inc(S("pj_ev1"), 1)

                def squares(i):
                    act.wait_ge(S("tr1"), i + 1)
                    if i >= 16:
                        c = (i - 16) * P
                        A(v[:, 0:4, c:c + P], four(PS[:, 6, :]), ACT.Copy)
                        A(v[:, 4, c:c + P], PS[:, 7, 0:P], ACT.Copy).then_inc(S("tr1_ev"), 1)
                    else:
                        if i >= 1:
                            act.wait_ge(S("qn"), i)
                        for t in range(NT):
                            src = PS[:, 6, t * P:(t + 1) * P] if t < 4 else PS[:, 7, 0:P]
                            ins = A(cjunk, src, ACT.Square, accum_out=ss[:, 0, t:t + 1])
                            link(ins)
                        inverse_root(ss[:, 1, 0:NT], ss[:, 0, 0:NT], 1.0).then_inc(S("sqj"), 1)

                def back(i):
                    act.wait_ge(S("tr2"), i + 1)
                    dst = (qT if i < 8 else kT)[:, i % 8, :]
                    A(dst[:, 0:4 * P], PS[:, 6, :], ACT.Copy)
                    A(dst[:, 4 * P:TOK], PS[:, 7, 0:P], ACT.Copy).then_inc(S("tr2_ev"), 1)

                for i in range(26):
                    if 2 <= i and i - 2 < 16:
                        back(i - 2)
                    if i < 24:
                        evac(i)
                    if 1 <= i <= 24:
                        squares(i - 1)
                    if i < 24:
                        act.wait_ge(S("cv_done"), i + 1)
                        if i:
                            act.wait_ge(S("silu"), i)
                        A(cex, cout[i % 2], ACT.Tanh).then_inc(S("cvexp"), 1)
                for i in range(24, 34):
                    evac(i)

            def gates(L):
                if L == 0:
                    act.wait_ge(S("g0"), 1)
                    A(ga[:, 1, :], ga[:, 0, :], ACT.Exp, scale=-1.0).then_inc(S("g0a"), 1)
                    act.wait_ge(S("g0a"), 1)
                    A(ga[:, 1, :], ga[:, 1, :], ACT.Ln, bias=1.0).then_inc(S("g0a"), 1)
                    act.wait_ge(S("g0"), 2)
                    for j in (9, 10, 11, 12):
                        A(ga[:, j, :], ga[:, j, :], ACT.Exp).then_inc(S("g0a"), 1)
                    return
                act.wait_ge(S("g1"), 1)
                A(ga[:, 1, :], ga[:, 0, :], ACT.Exp, scale=-1.0).then_inc(S("g1a"), 1)
                act.wait_ge(S("g1a"), 1)
                A(ga[:, 1, :], ga[:, 1, :], ACT.Ln, bias=1.0).then_inc(S("g1a"), 1)
                A(ga[:, 4, :], ga[:, 4, :], ACT.Exp, scale=-1.0).then_inc(S("g1a"), 1)
                A(gb1[:, :, 0, :], gb1[:, :, 0, :], ACT.Exp).then_inc(S("g1a"), 1)

            def gates_delta2():
                act.wait_ge(S("g1"), 2)
                for j in (7, 8, 9):
                    A(ga[:, j, :], ga[:, j, :], ACT.Exp).then_inc(S("g1a"), 1)

            def mlstm():
                def soft(n):
                    d, t = UNITS[n // 2]
                    p = n % 2
                    act.wait_ge(S("ml_bc"), n + 1)
                    if n >= 2:
                        act.wait_ge(S("ml_ps"), n - 1)
                    for h in range(4):
                        A(four(half[4 * p])[:, h, :], PS[:, 4 * p, h * P:(h + 1) * P], ACT.Exp,
                          bias=G3[3][:, t, d, 4 * p + h:4 * p + h + 1]).then_inc(S("ml_e"), 1)

                def inter(n):
                    p = n % 2
                    act.wait_ge(S("ml_den"), n + 1)
                    if n >= 2:
                        act.wait_ge(S("ml_done"), n - 1)
                    for h in range(4):
                        A(four(half[4 * p + 3])[:, h, :], PS[:, 4 * p + 1, h * P:(h + 1) * P], ACT.Copy,
                          scale=sm[:, p, 3, h:h + 1]).then_inc(S("ml_ti"), 1)

                soft(0)
                for n in range(20):
                    if n + 1 < 20:
                        soft(n + 1)
                    inter(n)

            def delta():
                for u, (d, t) in enumerate(UNITS):
                    for p in range(2):
                        n = 2 * u + p
                        act.wait_ge(S("dl_bc"), n + 1)
                        if u:
                            act.wait_ge(S("dl_w"), n - 1)
                        for h in range(4):
                            A(dbuf(p)["E"][:, h, :], PS[:, 4 * p, h * P:(h + 1) * P], ACT.Exp,
                              bias=NG[:, t, d, 4 * p + h:4 * p + h + 1]).then_inc(S("dl_e"), 1)
                    for l in range(LEVELS):
                        for p in range(2):
                            m = (u * LEVELS + l) * 2 + p
                            act.wait_ge(S("dl_tr"), m + 1)
                            off = 1 - d
                            A(cols(dbuf(p)["DT"], l, off), cols(four(PS[:, 4 * p + 2, :]), l, off), ACT.Copy).then_inc(S("dl_dt"), 1)
                    for p in range(2):
                        n = 2 * u + p
                        act.wait_ge(S("dl_wk"), n + 1)
                        A(dbuf(p)["nWk"], four(PS[:, 4 * p, :]), ACT.Copy, scale=-1.0).then_inc(S("dl_nw"), 1)
                    for p in range(2):
                        n = 2 * u + p
                        act.wait_ge(S("dl_w"), n + 1)
                        A(dbuf(p)["W"], four(PS[:, 4 * p + 1, :]), ACT.Copy).then_inc(S("dl_we"), 1)
                        for h in range(4):
                            A(dbuf(p)["t"][:, h, :], PS[:, 4 * p + 2, h * P:(h + 1) * P], ACT.Copy,
                              scale=EG[:, t, d, 4 * p + h:4 * p + h + 1]).then_inc(S("dl_t"), 1)

            def gate_out(L):
                for t in range(NT):
                    act.wait_ge(S("fin_start"), L * PER["fin_start"] + 1)
                    if t:
                        act.wait_ge(S("fin_read"), L * PER["fin_read"] + t)
                    A(fsq, acc[:, t, :], ACT.Square).then_inc(S("fin_sq"), 1)
                    A(fex, o[:, t, :], ACT.Tanh, scale=0.5).then_inc(S("fin_sq"), 1)
                    act.wait_ge(S("fin_r"), L * PER["fin_r"] + t + 1)
                    inverse_root(ss[:, 1, 0:H], ss[:, 0, 0:H], 1.0 / P).then_inc(S("fin_i"), 1)
                    if t:
                        yt_copy(L, t - 1)
                yt_copy(L, NT - 1)

            def yt_copy(L, t):
                act.wait_ge(S("yt"), L * PER["yt"] + t + 1)
                for j in range(2):
                    A(yT[:, 4 * j:4 * j + 4, t * P:(t + 1) * P], four(PS[:, 2 * (t % 2) + j, :]), ACT.Copy).then_inc(S("yt_ev"), 1)
                if t == NT - 1:
                    for c in range(2):
                        for j in range(2):
                            act.wait_ge(S("g1b"), L * PER["g1b"] + 2 * c + j + 1)
                            A(g1b[:, c, j, :], PS[:, 4 + 2 * c + j, :], ACT.Copy).then_inc(S("g1e"), 1)

            def experts(L):
                act.wait_ge(S("sm"), L * PER["sm"] + 1)
                A(aff[:, :, :], aff[:, :, :], ACT.Exp).then_inc(S("sme"), 1)

                def expert(e, q, first):
                    for hf in range(2):
                        act.wait_ge(S("moe_used"), L * PER["moe_used"] + e * 6 + (2 * hf + 1))
                        if not first:
                            act.wait_ge(S("hidden"), L * PER["hidden"] + e * 2 + (hf - 1))
                        A(eb[hf], PS[:, 2 * hf, 0:320], ACT.Tanh, scale=0.5).then_inc(S("gexp"), 1)
                    for hf in range(2):
                        act.wait_ge(S("moe_used"), L * PER["moe_used"] + e * 6 + (5 + hf))
                        if hf == 0 and not first:
                            act.wait_ge(S("scattered"), L * PER["scattered"] + (e - 1) * 16)
                        A(osb[q][0:CAP, hf * HC:(hf + 1) * HC], PS[0:CAP, 4 + hf, :], ACT.Copy,
                          scale=gsc[q][0:CAP, :]).then_inc(S("o_ready"), 1)

                expert(0, 0, True)
                expert1(expert)
                with act.Fori(1, EX // 2) as i:
                    for q in range(2):
                        expert(i * 2 + q, q, False)

            def expert1(expert):
                L = act_layer[0]
                for hf in range(2):
                    act.wait_ge(S("moe_used"), L * PER["moe_used"] + 6 + 2 * hf + 1)
                    act.wait_ge(S("hidden"), L * PER["hidden"] + hf + 1)
                    A(eb[hf], PS[:, 2 * hf, 0:320], ACT.Tanh, scale=0.5).then_inc(S("gexp"), 1)
                for hf in range(2):
                    act.wait_ge(S("moe_used"), L * PER["moe_used"] + 6 + 5 + hf)
                    A(osb[1][0:CAP, hf * HC:(hf + 1) * HC], PS[0:CAP, 4 + hf, :], ACT.Copy,
                      scale=gsc[1][0:CAP, :]).then_inc(S("o_ready"), 1)

            def modulation(L):
                for n in range(NADA):
                    act.wait_ge(S("ada_mm"), L * PER["ada_mm"] + n + 1)
                    if n >= 2:
                        act.wait_ge(S("ada_tr"), L * NADA + n - 1)
                    A(mrow[n % 2], PS[0:2, n % 2, :], ACT.Copy).then_inc(S("ada_ev"), 1)

            act_layer = [0]
            for L in range(2):
                act_layer[0] = L
                modulation(L)
                norm(2 * L)
                norm_evac(L, 0)
                if L == 0:
                    gates(0)
                    proj(0)
                    mlstm()
                else:
                    gates(1)
                    proj(1)
                    gates_delta2()
                    delta()
                gate_out(L)
                norm(2 * L + 1)
                norm_evac(L, 1)
                experts(L)
            norm(4)

        @block.tensor
        def _(pe):
            mm = nc.tensor.matmul
            tr = nc.tensor.transpose

            pe.wait_ge(S("setup"), 16 * 14)
            tr(PS[:, 0, 0:48], rows[0:48, 0, :], ident[0:48, 0:48])
            tr(PS[:, 0, 48:144], rows[0:96, 1, :], ident[0:96, 0:96])
            tr(PS[:, 0, 144:264], rows[0:120, 2, :], ident[0:120, 0:120]).then_inc(S("vect"), 1)

            def modulation(L):
                def turn(n):
                    pe.wait_ge(S("ada_ev"), L * PER["ada_ev"] + n + 1)
                    for b in range(4):
                        blk = n * 4 + b
                        ins = tr(PS[:, 2, 2 * blk:2 * blk + 2], mrow[n % 2][:, b * P:(b + 1) * P], ident[0:2, 0:2])
                    ins.then_inc(S("ada_tr"), 1)

                pe.wait_ge(S("cond"), 1)
                if L:
                    pe.wait_ge(S("x_moe"), NT)
                for n in range(NADA):
                    j = mix_slot(n)
                    pe.wait_ge(land[j], mix_landed(L, n))
                    if n >= 2:
                        pe.wait_ge(S("ada_ev"), L * PER["ada_ev"] + n - 1)
                    for kt in range(KT):
                        ins = mm(PS[0:2, n % 2, :], cnd[:, 1, kt:16:8], slot[j][:, kt, :],
                                 start=(kt == 0), stop=(kt == KT - 1))
                    ins.then_inc(S("ada_mm"), 1)
                    if n:
                        turn(n - 1)
                turn(NADA - 1)

            def norm_turn(L, k):
                for t in range(NT):
                    pe.wait_ge(S("xn"), (2 * L + k) * PER["xn"] + t + 1)
                    if t >= 2:
                        pe.wait_ge(S("hta"), (2 * L + k) * PER["hta"] + 4 * (t - 1))
                        pe.wait_ge(S("htv"), (2 * L + k) * PER["htv"] + t - 1)
                    for j in range(2):
                        for kt in range(4):
                            c = (4 * j + kt) * P
                            ins = tr(PS[:, 2 * (t % 2) + 2 + j, kt * P:(kt + 1) * P], o[:, t, c:c + P], ident)
                        ins.then_inc(S("xt"), 1)
                pe.wait_ge(S("hta"), (2 * L + k) * PER["hta"] + 4 * NT)
                pe.wait_ge(S("htv"), (2 * L + k) * PER["htv"] + NT)

            def gates(L):
                pe.wait_ge(S("wg_in"), 16 * (L + 1))
                for t in range(NT):
                    for kt in range(KT):
                        ins = mm(PS[:, 7, t * 32:(t + 1) * 32], hT[:, kt, t * P:(t + 1) * P], wgt[:, kt, :],
                                 start=(kt == 0), stop=(kt == KT - 1))
                ins.then_inc(S("gmm"), 1)

            def feature_major(L, i, sl, cb):
                b = 2 * (i % 3)
                if i >= 3:
                    pe.wait_ge(S(f"pj_ev{L}"), i - 2)
                for kt in range(KT):
                    w = slot[sl][:, kt, cb * P:(cb + 1) * P]
                    mm(PS[:, b, :], w, hT[:, kt, P:TOK], start=(kt == 0), stop=(kt == KT - 1))
                    ins = mm(PS[:, b + 1, 0:P], w, hT[:, kt, 0:P], start=(kt == 0), stop=(kt == KT - 1))
                return ins.then_inc(S(f"pj_mm{L}"), 1)

            def token_major(L, i, sl, t):
                if i >= 3:
                    pe.wait_ge(S(f"pj_ev{L}"), i - 2)
                for kt in range(KT):
                    ins = mm(PS[:, 2 * (i % 3), :], hT[:, kt, t * P:(t + 1) * P], slot[sl][:, kt, :],
                             start=(kt == 0), stop=(kt == KT - 1))
                return ins.then_inc(S(f"pj_mm{L}"), 1)

            def unit(L, g):
                n = NADA + g
                pe.wait_ge(land[mix_slot(n)], mix_landed(L, n))
                return mix_slot(n)

            def proj_mlstm():
                i = 0
                for g in range(8):
                    sl = unit(0, g)
                    for k in range(4 if g < 4 else NT):
                        feature_major(0, i, sl, k) if g < 4 else token_major(0, i, sl, k)
                        i += 1
                pe.wait_ge(S("pj_ev0"), 36)

            def proj_delta():
                def turn1(i):
                    pe.wait_ge(S("silu"), i + 1)
                    if i == 0:
                        pe.wait_ge(S("gev1"), 4)
                    elif i <= 16:
                        pe.wait_ge(S("tr2_ev"), i)
                    if i >= 17:
                        pe.wait_ge(S("tr1_ev"), i - 16)
                    for t in range(NT):
                        dst = PS[:, 6, t * P:(t + 1) * P] if t < 4 else PS[:, 7, 0:P]
                        ins = tr(dst, cout[i % 2][:, t * P:(t + 1) * P], ident)
                    ins.then_inc(S("tr1"), 1)

                def turn2(i):
                    pe.wait_ge(S("qn"), i + 1)
                    for t in range(NT):
                        dst = PS[:, 6, t * P:(t + 1) * P] if t < 4 else PS[:, 7, 0:P]
                        ins = tr(dst, qn[:, t, :], ident)
                    ins.then_inc(S("tr2"), 1)

                for i in range(26):
                    if 2 <= i and i - 2 < 16:
                        turn2(i - 2)
                    if i < 24:
                        g, k = divmod(i, 4)
                        if k == 0:
                            sl = unit(1, g)
                        feature_major(1, i, sl, k)
                    if 1 <= i <= 24:
                        turn1(i - 1)
                i = 24
                for g in range(6, 8):
                    sl = unit(1, g)
                    for t in range(NT):
                        token_major(1, i, sl, t)
                        i += 1
                pe.wait_ge(S("tr1_ev"), 8)
                pe.wait_ge(S("tr2_ev"), 16)
                pe.wait_ge(S("pj_ev1"), 34)

            def masked(bank, mask, src, neg=None):
                for h in range(4):
                    mm(PS[:, bank, h * P:(h + 1) * P], src[:, h:h + 1].broadcast_to([P, P]), ident,
                       start=(h == 0), stop=False, skip_group_check=True)
                return mm(PS[:, bank, :], ident, mask.unsqueeze(1).broadcast_to([P, 4, P]), start=False, stop=True,
                          skip_group_check=True)

            def sums(L, src, sem_in, sem_out):
                pe.wait_ge(*sem_in)
                for d in range(2):
                    mm(PS[:, 7, 40 * d:40 * d + 40].rearrange("p (t h) -> p t h", t=NT), tri[d], src[:, :, d, :], start=True, stop=True)
                mm(PS[:, 7, 80:160], ones, src[:, :, :, :].rearrange("p t d h -> p (t d h)"), start=True, stop=True).then_inc(sem_out, 1)

            def stab_mlstm():
                sums(0, G3[2], (S("lf"), 1), S("bsum"))
                pe.wait_ge(S("aready"), 1)
                for n in range(20):
                    d, t = UNITS[n // 2]
                    p = n % 2
                    if n >= 4:
                        pe.wait_ge(S("mxr"), n - 3)
                    masked(n % 4, neg_ts[d], G3[3][:, t, d, 4 * p:4 * p + 4]).then_inc(S("amm"), 1)
                pe.wait_ge(S("mxr"), 20)
                for d in range(2):
                    last = ident[:, 127:128] if d == 0 else ident[:, 0:1]
                    ins = mm(PS[:, 7, 40 * d:40 * d + 40].rearrange("p (t h) -> p t h", t=NT), last.broadcast_to([P, P]),
                             G3[6][:, :, d, :], start=True, stop=True)
                ins.then_inc(S("mlast"), 1)

            def scan_mlstm():
                def front(n):
                    d, t = UNITS[n // 2]
                    p = n % 2
                    ts = slice(t * P, (t + 1) * P)
                    if n == 0:
                        pe.wait_ge(S("nm"), 1)
                    if n >= 2:
                        pe.wait_ge(S("ml_done"), n - 1)
                    masked(4 * p, neg_st[d], G3[8][:, t, d, 4 * p:4 * p + 4]).then_inc(S("ml_bc"), 1)
                    for h in range(4):
                        ins = mm(PS[:, 4 * p + 1, h * P:(h + 1) * P], kT[:, 4 * p + h, ts], qT[:, 4 * p + h, ts], start=True, stop=True)
                    for h in range(4):
                        ins = tr(PS[:, 4 * p + 2, h * P:(h + 1) * P], kT[:, 4 * p + h, ts], ident)
                    ins.then_inc(S("ml_s"), 1)

                def back(n):
                    d, t = UNITS[n // 2]
                    p = n % 2
                    ts = slice(t * P, (t + 1) * P)
                    E, PSb, kw = (four(half[4 * p + j]) for j in range(3))
                    pe.wait_ge(S("ml_ps"), n + 1)
                    if n == 0:
                        pe.wait_ge(S("st_in"), 64)
                    if n >= 4:
                        pe.wait_ge(S("ml_c"), n - 3)
                    if n >= 16:
                        pe.wait_ge(S("ml_cz"), n - 15)
                    for h in range(4):
                        hh = 4 * p + h
                        mm(PS[:, 4 * p, h * P:(h + 1) * P], PSb[:, h, :], v[:, t, hh * P:(hh + 1) * P], start=True, stop=True)
                        mm(PS[:, 4 * p + 3, h:h + 1], PSb[:, h, :], ones[:, 0:1], start=True, stop=True)
                    for h in range(4):
                        hh = 4 * p + h
                        mm(PS[:, 4 * p + 1, h * P:(h + 1) * P], qT[:, hh, ts], Cst[:, d, hh, :], start=True, stop=True)
                        mm(PS[:, 4 * p + 3, 4 + h:5 + h], qT[:, hh, ts], nst[:, d, hh:hh + 1], start=True, stop=True)
                    for h in range(4):
                        hh = 4 * p + h
                        mm(PS[:, 4 * p + 2, h * P:(h + 1) * P], kw[:, h, :], v[:, t, hh * P:(hh + 1) * P], start=True, stop=True)
                        ins = mm(PS[:, 4 * p + 3, 8 + h:9 + h], kw[:, h, :], ones[:, 0:1], start=True, stop=True)
                    ins.then_inc(S("ml_bk"), 1)

                front(0)
                for n in range(20):
                    if n + 1 < 20:
                        front(n + 1)
                    back(n)

            def scan_delta():
                sums(1, G3[3], (S("gl"), 1), S("gsum"))
                pe.wait_ge(S("gready"), 1)
                for u, (d, t) in enumerate(UNITS):
                    ts = slice(t * P, (t + 1) * P)
                    for p in range(2):
                        n = 2 * u + p
                        if u:
                            pe.wait_ge(S("dl_done"), n - 1)
                        masked(4 * p, neg_st[d], GC[:, t, d, 4 * p:4 * p + 4]).then_inc(S("dl_bc"), 1)
                        for h in range(4):
                            mm(PS[:, 4 * p + 1, h * P:(h + 1) * P], kT[:, 4 * p + h, ts], kT[:, 4 * p + h, ts], start=True, stop=True)
                        for h in range(4):
                            mm(PS[:, 4 * p + 2, h * P:(h + 1) * P], kT[:, 4 * p + h, ts], qT[:, 4 * p + h, ts], start=True, stop=True)
                        for h in range(4):
                            ins = tr(PS[:, 4 * p + 3, h * P:(h + 1) * P], kT[:, 4 * p + h, ts], ident)
                        ins.then_inc(S("dl_kk"), 1)
                    for l in range(LEVELS):
                        for p in range(2):
                            m = (u * LEVELS + l) * 2 + p
                            n = 2 * u + p
                            B = dbuf(p)
                            pe.wait_ge(S("dl_cm"), m + 1)
                            if l == 0:
                                pe.wait_ge(S("dl_init"), 2 * n + 2)
                            else:
                                pe.wait_ge(S("dl_d"), m - 1)
                            for h in range(4):
                                ins = mm(pack(four(PS[:, 4 * p, :])[:, :, 0:64], l)[:, h], B["CM"][:, h, :],
                                         cols1(B["D"][:, h, :], l, d), start=True, stop=True)
                            ins.then_inc(S("dl_x"), 1)
                        for p in range(2):
                            m = (u * LEVELS + l) * 2 + p
                            B = dbuf(p)
                            pe.wait_ge(S("dl_xe"), m + 1)
                            if l:
                                pe.wait_ge(S("dl_dt"), m - 1)
                            for h in range(4):
                                ins = mm(four(PS[:, 4 * p + 1, :])[:, h, 0:64], B["DT"][:, h, :], B["X"][:, h, :], start=True, stop=True)
                            ins.then_inc(S("dl_dx"), 1)
                        for p in range(2):
                            m = (u * LEVELS + l) * 2 + p
                            B = dbuf(p)
                            pe.wait_ge(S("dl_d"), m + 1)
                            for h in range(4):
                                ins = tr(PS[:, 4 * p + 2, h * P:(h + 1) * P], B["D"][:, h, :], ident)
                            ins.then_inc(S("dl_tr"), 1)
                    for p in range(2):
                        n = 2 * u + p
                        B = dbuf(p)
                        pe.wait_ge(S("dl_kb"), n + 1)
                        pe.wait_ge(S("dl_dt"), (u * LEVELS + LEVELS - 1) * 2 + p + 1)
                        for h in range(4):
                            ins = mm(PS[:, 4 * p, h * P:(h + 1) * P], B["kb"][:, h, :], B["DT"][:, h, :], start=True, stop=True)
                        ins.then_inc(S("dl_wk"), 1)
                    for p in range(2):
                        n = 2 * u + p
                        B = dbuf(p)
                        pe.wait_ge(S("dl_bv"), n + 1)
                        pe.wait_ge(S("dl_nw"), n + 1)
                        if n == 0:
                            pe.wait_ge(S("st_in"), 64 + 32)
                        if n >= 4:
                            pe.wait_ge(S("dl_s"), n - 3)
                        if n >= 16:
                            pe.wait_ge(S("dl_sz"), n - 15)
                        for h in range(4):
                            hh = 4 * p + h
                            mm(PS[:, 4 * p + 2, h * P:(h + 1) * P], qT[:, hh, ts], Cst[:, d, hh, :], start=True, stop=True)
                        for h in range(4):
                            hh = 4 * p + h
                            mm(PS[:, 4 * p + 1, h * P:(h + 1) * P], B["DT"][:, h, :], B["bv"][:, h, :], start=True, stop=False)
                            ins = mm(PS[:, 4 * p + 1, h * P:(h + 1) * P], B["nWk"][:, h, :], Cst[:, d, hh, :], start=False, stop=True)
                        ins.then_inc(S("dl_w"), 1)
                    for p in range(2):
                        n = 2 * u + p
                        B = dbuf(p)
                        pe.wait_ge(S("dl_we"), n + 1)
                        pe.wait_ge(S("dl_kd"), n + 1)
                        for h in range(4):
                            mm(PS[:, 4 * p + 3, h * P:(h + 1) * P], B["kd"][:, h, :], B["W"][:, h, :], start=True, stop=True)
                        for h in range(4):
                            ins = mm(PS[:, 4 * p, h * P:(h + 1) * P], B["qk"][:, h, :], B["W"][:, h, :], start=True, stop=True)
                        ins.then_inc(S("dl_o"), 1)

            def out(L):
                for t in range(NT):
                    pe.wait_ge(S("y"), L * PER["y"] + t + 1)
                    if t >= 2:
                        pe.wait_ge(S("yt_ev"), L * PER["yt_ev"] + 2 * (t - 1))
                    for kt in range(KT):
                        ins = tr(PS[:, 2 * (t % 2) + kt // 4, (kt % 4) * P:(kt % 4 + 1) * P], acc[:, t, kt * P:(kt + 1) * P], ident)
                    ins.then_inc(S("yt"), 1)
                gate_rows(16, 4, S("g1b"))
                pe.wait_ge(S("yt_ev"), L * PER["yt_ev"] + 2 * NT)
                i = 0
                for j in range(2):
                    n = NADA + NIN + j
                    pe.wait_ge(land[j], mix_landed(L, n))
                    for t in range(NT):
                        if i >= 4:
                            pe.wait_ge(S("x_new"), L * PER["x_new"] + i - 3)
                        for kt in range(KT):
                            ins = mm(PS[:, i % 4, :], yT[:, kt, t * P:(t + 1) * P], slot[j][:, kt, :], start=(kt == 0), stop=(kt == KT - 1))
                        ins.then_inc(S("omm"), 1)
                        i += 1

            def gate_rows(first, bank, sem):
                for c in range(2):
                    for j in range(2):
                        for b in range(4):
                            ins = mm(PS[:, bank + 2 * c + j, b * P:(b + 1) * P],
                                     modT[:, first + 4 * j + b, c:c + 1].broadcast_to([P, P]), ident, start=True, stop=True)
                        ins.then_inc(sem, 1)

            def experts(L):
                pe.wait_ge(S("wr_in"), 16 * (L + 1))
                for t in range(NT):
                    for kt in range(KT):
                        ins = mm(PS[:, 0, t * EX:(t + 1) * EX], hT[:, kt, t * P:(t + 1) * P], wrt[:, kt, :],
                                 start=(kt == 0), stop=(kt == KT - 1))
                ins.then_inc(S("logits"), 1)
                pe.wait_ge(S("aff"), L * PER["aff"] + 1)
                tr(PS[0:EX, 2, 0:P], aff[:, 0, :], ident)
                for t in range(1, NT):
                    ins = tr(PS[0:EX, 1, (t - 1) * P:t * P], aff[:, t, :], ident)
                ins.then_inc(S("afft"), 1)
                pe.wait_ge(S("topk"), L * PER["topk"] + 1)
                tr(PS[0:CAP, 3, 0:EX], vals[:, :], ident[0:EX, 0:EX])
                tr(PS[0:CAP, 3, EX:2 * EX], idf[:, :], ident[0:EX, 0:EX]).then_inc(S("selt"), 1)
                pe.wait_ge(S("sel"), L * PER["sel"] + 2)

                def turn(e, q, first):
                    pe.wait_ge(S("gathered"), L * PER["gathered"] + e * 16 + 16)
                    if not first:
                        pe.wait_ge(S("xs_in"), L * PER["xs_in"] + e)
                    for kt in range(KT):
                        ins = tr(PS[:, 6 + kt // 4, (kt % 4) * CAP:(kt % 4 + 1) * CAP], xs[q][0:CAP, kt * P:(kt + 1) * P], ident[0:CAP, 0:CAP])
                    ins.then_inc(S("xs_turned"), 1)

                def hidden(e, q, first):
                    pe.wait_ge(S("xs_in"), L * PER["xs_in"] + e + 1)
                    for j in range(4):
                        pe.wait_ge(land[j], e * 16 + (16 * moe_base(L, j) + 16))
                        if not first:
                            pe.wait_ge(S("hidden"), L * PER["hidden"] + e * 2 + (j // 2 - 1))
                        for fb in range(4):
                            for kt in range(KT):
                                ins = mm(PS[:, j, fb * CAP:(fb + 1) * CAP], slot[j][:, kt, fb * P:(fb + 1) * P],
                                         xsT[q][:, kt, :], start=(kt == 0), stop=(kt == KT - 1))
                        ins.then_inc(S("moe_used"), 1)

                def down(e, q, first):
                    pe.wait_ge(S("hidden"), L * PER["hidden"] + e * 2 + 2)
                    for j in range(2):
                        pe.wait_ge(land[4 + j], e * 16 + (16 * moe_base(L, 4 + j) + 16))
                        if not first:
                            pe.wait_ge(S("o_ready"), L * PER["o_ready"] + e * 2 + (j - 1))
                        for ft in range(KT):
                            ins = mm(PS[0:CAP, 4 + j, :], hdT[:, ft, :], slot[4 + j][:, ft, :],
                                     start=(ft == 0), stop=(ft == KT - 1))
                        ins.then_inc(S("moe_used"), 1)

                turn(0, 0, True)
                hidden(0, 0, True)
                turn(1, 1, False)
                down(0, 0, True)
                hidden(1, 1, False)
                turn(2, 0, False)
                down(1, 1, False)
                with pe.Fori(1, EX // 2 - 1) as i:
                    for q in range(2):
                        e = i * 2 + q
                        hidden(e, q, False)
                        turn(i * 2 + (q + 1), 1 - q, False)
                        down(e, q, False)
                hidden(EX - 2, 0, False)
                turn(EX - 1, 1, False)
                down(EX - 2, 0, False)
                hidden(EX - 1, 1, False)
                down(EX - 1, 1, False)
                pe.wait_ge(S("hidden"), L * PER["hidden"] + 2 * EX)
                gate_rows(40, 0, S("g2b"))

            for L in range(2):
                modulation(L)
                norm_turn(L, 0)
                gates(L)
                if L == 0:
                    stab_mlstm()
                    proj_mlstm()
                    scan_mlstm()
                else:
                    proj_delta()
                    scan_delta()
                out(L)
                norm_turn(L, 1)
                experts(L)

        @block.vector
        def _(dve):
            V = nc.vector
            chain = [0]

            def link(ins):
                chain[0] += 1
                ins.then_inc(S("dve_chain"), 1)
                dve.wait_ge(S("dve_chain"), chain[0])

            dve.wait_ge(S("vect"), 1)
            V.tensor_copy(vecT[:, :], PS[:, 0, 0:264]).then_inc(S("vec"), 1)
            dve.wait_ge(S("vec"), 1)
            link(V.tensor_scalar(convT, convT, 0.5, None, ALU.mult))
            dve.wait_ge(S("cexp"), 1)
            link(V.tensor_scalar(cnd[:, 0, :], cnd[:, 0, :], 1.0, None, ALU.add))
            link(V.reciprocal(cnd[:, 0, :], cnd[:, 0, :]))
            V.tensor_tensor(cnd[:, 1, :], cnd[:, 0, :], vecT[:, 32:48], ALU.mult).then_inc(S("cond"), 1)

            def modulation(L):
                dve.wait_ge(S("ada_tr"), (L + 1) * NADA)
                link(V.tensor_tensor(modT[:, :, :], PS[:, 2, 0:96].rearrange("p (b c) -> p b c", c=2),
                                     biasT[:, L, :].unsqueeze(2).broadcast_to([P, MOD, 2]), ALU.add))
                for k in range(2):
                    ins = V.scalar_tensor_tensor(AB[:, k, :, :], modT[:, 8 + 24 * k:16 + 24 * k, :], 1.0,
                                                 norm_g[:, k, L, :].unsqueeze(2).broadcast_to([P, KT, 2]), ALU.add, ALU.mult)
                    if k == 0:
                        link(ins)
                ins.then_inc(S("ab"), 1)
                dve.wait_ge(S("ab"), L * PER["ab"] + 1)

            def sharpen(first, last, scale, gain=1.0):
                w, y, vv, tt = (ss[:, j, first:last] for j in range(4))
                link(V.tensor_scalar(vv, w, scale, EPS, ALU.mult, ALU.add))
                link(V.scalar_tensor_tensor(tt, y, -0.5 * gain, y, ALU.mult, ALU.mult))
                link(V.tensor_tensor(tt, tt, vv, ALU.mult))
                link(V.scalar_tensor_tensor(y, tt, 1.5 * gain, y, ALU.add, ALU.mult))

            def norm(i):
                L, k = divmod(i, 2)
                for t in range(NT + 1):
                    if t < NT:
                        dve.wait_ge(S("sq"), i * PER["sq"] + t + 1)
                        sharpen(t, t + 1, 1.0 / D)
                        V.tensor_scalar(o[:, t, :], x[:, t, :], ss[:, 1, t:t + 1], None, ALU.mult).then_inc(S("xn"), 1)
                    if i < 4 and t:
                        u = t - 1
                        c = int(u > 0)
                        dve.wait_ge(S("xt"), (2 * L + k) * PER["xt"] + 2 * u + 2)
                        dst = hT[:, 4:8, u * P:(u + 1) * P]
                        link(V.tensor_tensor(dst, four(PS[:, 2 * (u % 2) + 3, :]), heads(AB[:, k, 4:8, c]), ALU.mult))
                        V.tensor_tensor(dst, dst, heads(modT[:, 24 * k + 4:24 * k + 8, c]), ALU.add).then_inc(S("htv"), 1)

            def gates_mlstm():
                f, ig = gt[:, :, :, 1, :], gt[:, :, :, 0, :]
                dve.wait_ge(S("gmm"), 1)
                link(V.tensor_tensor(gt[:, :, :, :, :].rearrange("p t d k h -> p t (d k h)"),
                                     PS[:, 7, 0:160].rearrange("p (t c) -> p t c", t=NT),
                                     gb0[:, :, :, :].rearrange("p d k h -> p (d k h)").unsqueeze(1).broadcast_to([P, NT, 32]), ALU.add))
                V.scalar_tensor_tensor(G3[0], f, -1.0, f, ALU.mult, ALU.max).then_inc(S("g0"), 1)
                dve.wait_ge(S("g0a"), 2)
                V.scalar_tensor_tensor(G3[2], f, 0.0, G3[1], ALU.min, ALU.subtract).then_inc(S("lf"), 1)
                dve.wait_ge(S("bsum"), 1)
                link(V.tensor_copy(G3[4], PS[:, 7, 0:80].rearrange("p (d t h) -> p t d h", d=2, t=NT)))
                link(V.tensor_copy(ga[:, 5, :], PS[:, 7, 80:160]))
                V.tensor_tensor(G3[3], ig, G3[4], ALU.subtract).then_inc(S("aready"), 1)
                dve.wait_ge(S("aready"), 1)
                for n in range(20):
                    d, t = UNITS[n // 2]
                    p = n % 2
                    dve.wait_ge(S("amm"), n + 1)
                    V.tensor_reduce(G3[6][:, t, d, 4 * p:4 * p + 4], four(PS[:, n % 4, :]), AX, ALU.max).then_inc(S("mxr"), 1)
                dve.wait_ge(S("mxr"), 20)
                dve.wait_ge(S("mlast"), 1)
                link(V.tensor_copy(G3[7], PS[:, 7, 0:80].rearrange("p (d t h) -> p t d h", d=2, t=NT)))
                link(V.memset(G3[13][:, 0, :, :], 0.0))
                link(V.tensor_copy(G3[13][:, 1, 0, :], m0[:, 0, :]))
                link(V.tensor_copy(G3[13][:, 4, 1, :], m0[:, 1, :]))
                for s in range(4):
                    for d in range(2):
                        t = 1 + s if d == 0 else 4 - s
                        link(V.tensor_tensor(G3[7][:, t, d, :], G3[7][:, t, d, :], G3[13][:, t, d, :], ALU.max))
                        if s < 3:
                            t2 = t + 1 if d == 0 else t - 1
                            link(V.tensor_tensor(G3[13][:, t2, d, :], G3[7][:, t, d, :], G3[5][:, t, d, :], ALU.add))
                link(V.tensor_tensor(G3[7][:, 0, :, :], G3[7][:, 0, :, :], G3[13][:, 0, :, :], ALU.max))
                link(V.tensor_tensor(ga[:, 6, :], ga[:, 6, :], ga[:, 13, :], ALU.max))
                V.tensor_scalar(ga[:, 8, :], ga[:, 6, :], -1.0, None, ALU.mult).then_inc(S("nm"), 1)
                link(V.tensor_tensor(ga[:, 9, :], ga[:, 13, :], ga[:, 6, :], ALU.subtract))
                link(V.tensor_tensor(ga[:, 10, :], ga[:, 3, :], ga[:, 7, :], ALU.subtract))
                link(V.tensor_tensor(ga[:, 11, :], ga[:, 13, :], ga[:, 7, :], ALU.subtract))
                link(V.scalar_tensor_tensor(ga[:, 12, :], ga[:, 4, :], -1.0, ga[:, 6, :], ALU.mult, ALU.subtract))
                link(V.tensor_tensor(G3[13][:, 0, :, :], G3[7][:, 0, :, :], G3[5][:, 0, :, :], ALU.add))
                dve.sem_inc(S("g0"), 1)
                dve.wait_ge(S("g0a"), 6)

            def scan_mlstm():
                SC, Wt, DEC, EM = G3[9], G3[10], G3[11], G3[12]

                def mid(n):
                    d, t = UNITS[n // 2]
                    p = n % 2
                    E, PSb, kw = (four(half[4 * p + j]) for j in range(3))
                    dve.wait_ge(S("ml_s"), n + 1)
                    V.tensor_tensor(kw, four(PS[:, 4 * p + 2, :]), heads(Wt[:, t, d, 4 * p:4 * p + 4]), ALU.mult)
                    dve.wait_ge(S("ml_e"), 4 * n + 4)
                    V.tensor_tensor(PSb, four(PS[:, 4 * p + 1, :]), E, ALU.mult).then_inc(S("ml_ps"), 1)

                def end(n):
                    d, t = UNITS[n // 2]
                    p = n % 2
                    hs = slice(4 * p, 4 * p + 4)
                    last = n >= 16
                    dve.wait_ge(S("ml_bk"), n + 1)
                    b3 = PS[:, 4 * p + 3, :]
                    for h in range(4):
                        hh = 4 * p + h
                        V.scalar_tensor_tensor(Cst[:, d, hh, :], Cst[:, d, hh, :], DEC[:, t, d, hh:hh + 1],
                                               PS[:, 4 * p + 2, h * P:(h + 1) * P], ALU.mult, ALU.add)
                    link(V.tensor_tensor(nst[:, d, hs], nst[:, d, hs], DEC[:, t, d, hs], ALU.mult))
                    V.tensor_tensor(nst[:, d, hs], nst[:, d, hs], b3[:, 8:12], ALU.add).then_inc(S("ml_c"), 1)
                    den = sm[:, p, 0, :]
                    link(V.tensor_tensor(den, b3[:, 4:8], SC[:, t, d, hs], ALU.mult))
                    link(V.tensor_tensor(den, den, b3[:, 0:4], ALU.add))
                    link(V.scalar_tensor_tensor(den, den, -1.0, den, ALU.mult, ALU.max))
                    link(V.tensor_tensor(den, den, EM[:, t, d, hs], ALU.max))
                    link(V.reciprocal(sm[:, p, 1, :], den))
                    V.tensor_tensor(sm[:, p, 3, :], sm[:, p, 1, :], SC[:, t, d, hs], ALU.mult).then_inc(S("ml_den"), 1)
                    if last:
                        dve.wait_ge(S("ml_c"), n + 1)
                        dve.sem_inc(S("st_new"), 1)
                    if 12 <= n < 16:
                        dve.wait_ge(S("ml_c"), n + 1)
                        V.memset(nst[:, d, hs], 0.0)
                        V.memset(Cst[:, d, hs, :], 0.0).then_inc(S("ml_cz"), 1)
                        dve.wait_ge(S("ml_cz"), n - 11)
                    dve.wait_ge(S("ml_ti"), 4 * n + 4)
                    tI = four(half[4 * p + 3])
                    dst = acc[:, t, p * HC:(p + 1) * HC]
                    if (d, t) in SECOND:
                        link(V.tensor_tensor(half[4 * p + 3], half[4 * p + 3], dst, ALU.add))
                    for h in range(4):
                        ins = V.scalar_tensor_tensor(dst[:, h * P:(h + 1) * P], PS[:, 4 * p, h * P:(h + 1) * P],
                                                     sm[:, p, 1, h:h + 1], tI[:, h, :], ALU.mult, ALU.add)
                    ins.then_inc(S("ml_done"), 1)
                    dve.wait_ge(S("ml_done"), n + 1)

                dve.wait_ge(S("st_in"), 64)
                dve.wait_ge(S("pj_ev0"), 36)
                mid(0)
                for n in range(20):
                    if n + 1 < 20:
                        mid(n + 1)
                    end(n)
                dve.sem_inc(S("fin_start"), 1)

            def gates_delta():
                dve.wait_ge(S("gmm"), PER['gmm'] + 1)
                g4 = PS[:, 7, 0:160].rearrange("p (t d k h) -> p t d k h", t=NT, d=2, k=2)
                for d in range(2):
                    V.tensor_tensor(G3[2][:, :, d, :], g4[:, :, d, 0, :], gb1[:, d, 1, :].unsqueeze(1).broadcast_to([P, NT, H]), ALU.add).then_inc(S("gev1"), 1)
                    V.tensor_copy(G3[4][:, :, d, :], g4[:, :, d, 1, :]).then_inc(S("gev1"), 1)
                dve.wait_ge(S("gev1"), 4)
                V.scalar_tensor_tensor(ga[:, 0, :], ga[:, 2, :], -1.0, ga[:, 2, :], ALU.mult, ALU.max).then_inc(S("g1"), 1)
                dve.wait_ge(S("g1a"), 4)
                link(V.scalar_tensor_tensor(ga[:, 3, :], ga[:, 2, :], 0.0, ga[:, 1, :], ALU.max, ALU.add))
                link(V.tensor_scalar(gb1[:, :, 0, :], gb1[:, :, 0, :], -1.0, None, ALU.mult))
                for d in range(2):
                    ins = V.tensor_tensor(G3[3][:, :, d, :], G3[3][:, :, d, :], gb1[:, d, 0, :].unsqueeze(1).broadcast_to([P, NT, H]), ALU.mult)
                    ins.then_inc(S("gl0"), 1)
                dve.wait_ge(S("gl0"), 2)
                link(V.tensor_scalar(ga[:, 4, :], ga[:, 4, :], 1.0, None, ALU.add))
                V.reciprocal(ga[:, 4, :], ga[:, 4, :]).then_inc(S("gl"), 1)
                dve.wait_ge(S("gl"), 1)

            def sums_delta():
                dve.wait_ge(S("gsum"), 1)
                link(V.tensor_copy(GC, PS[:, 7, 0:80].rearrange("p (d t h) -> p t d h", d=2, t=NT)))
                link(V.tensor_copy(ga[:, 8, :], PS[:, 7, 80:160]))
                link(V.tensor_scalar(ga[:, 6, :], ga[:, 5, :], -1.0, None, ALU.mult))
                link(V.tensor_copy(ga[:, 7, :], ga[:, 5, :]))
                V.tensor_tensor(ga[:, 9, :], ga[:, 8, :], ga[:, 5, :], ALU.subtract).then_inc(S("g1"), 1)
                dve.wait_ge(S("g1"), 2)
                dve.wait_ge(S("g1a"), 7)
                V.tensor_tensor(ga[:, 10, :], ga[:, 4, :], ga[:, 7, :], ALU.mult).then_inc(S("gready"), 1)
                dve.wait_ge(S("gready"), 1)

            def proj_delta():
                for q in range(2):
                    V.memset(cpad[q], 0.0).then_inc(S("padded"), 1)
                dve.wait_ge(S("padded"), 2)

                def conv(i):
                    dve.wait_ge(S("pj_ev1"), i + 1)
                    if i >= 2:
                        dve.wait_ge(S("tr1"), i - 1)
                    src, dst = cpad[i % 2], cout[i % 2]
                    for j in range(TAPS):
                        w = convT[:, j, i:i + 1]
                        for s, o_ in ((src[:, j:j + P].unsqueeze(1), dst[:, 0:P].unsqueeze(1)),
                                      (src[:, 132:676].rearrange("p (r w) -> p r w", r=NROW)[:, :, j:j + ROWW],
                                       dst[:, P:TOK].rearrange("p (r w) -> p r w", r=NROW))):
                            if j == 0:
                                ins = V.tensor_scalar(o_, s, w, None, ALU.mult)
                            else:
                                ins = V.scalar_tensor_tensor(o_, s, w, o_, ALU.mult, ALU.add)
                            if j == TAPS - 1 and s is not None and o_.shape[1] == NROW:
                                ins.then_inc(S("cv_done"), 1)
                                dve.wait_ge(S("cv_done"), i + 1)
                            else:
                                link(ins)

                def normed(i):
                    dve.wait_ge(S("sqj"), i + 1)
                    sharpen(0, NT, 1.0, float(P) ** -0.5 if i < 8 else 1.0)
                    if i:
                        dve.wait_ge(S("tr2"), i)
                    link(V.tensor_tensor(qn[:, 0:4, :], four(PS[:, 6, :]), heads(ss[:, 1, 0:4]), ALU.mult))
                    V.tensor_scalar(qn[:, 4, :], PS[:, 7, 0:P], ss[:, 1, 4:5], None, ALU.mult).then_inc(S("qn"), 1)

                for i in range(25):
                    if i < 24:
                        conv(i)
                    if 1 <= i and i - 1 < 16:
                        normed(i - 1)
                    if i < 24:
                        dve.wait_ge(S("cvexp"), i + 1)
                        V.scalar_tensor_tensor(cout[i % 2], cex, 1.0, cout[i % 2], ALU.add, ALU.mult).then_inc(S("silu"), 1)
                        dve.wait_ge(S("silu"), i + 1)

            def scan_delta():
                dve.wait_ge(S("st_in"), 96)
                for u, (d, t) in enumerate(UNITS):
                    for p in range(2):
                        n = 2 * u + p
                        B = dbuf(p)
                        dve.wait_ge(S("dl_kk"), n + 1)
                        dve.wait_ge(S("dl_e"), 4 * n + 4)
                        V.tensor_tensor(B["AT"], four(PS[:, 4 * p + 1, :]), B["E"], ALU.mult)
                        V.tensor_tensor(B["qk"], four(PS[:, 4 * p + 2, :]), B["E"], ALU.mult).then_inc(S("dl_at"), 1)
                        V.tensor_tensor(B["kb"], four(PS[:, 4 * p + 3, :]), heads(BEG[:, t, d, 4 * p:4 * p + 4]), ALU.mult).then_inc(S("dl_kb"), 1)
                    for l in range(LEVELS):
                        for p in range(2):
                            m = (u * LEVELS + l) * 2 + p
                            B = dbuf(p)
                            dve.wait_ge(S("dl_x"), m + 1)
                            V.tensor_tensor(B["X"], four(PS[:, 4 * p, :])[:, :, 0:64], heads(BETA[:, t, d, 4 * p:4 * p + 4], 64), ALU.mult).then_inc(S("dl_xe"), 1)
                        for p in range(2):
                            m = (u * LEVELS + l) * 2 + p
                            B = dbuf(p)
                            dve.wait_ge(S("dl_dx"), m + 1)
                            for h in range(4):
                                dst = cols1(B["D"][:, h, :], l, d)
                                ins = V.tensor_tensor(dst, dst, four(PS[:, 4 * p + 1, :])[:, h, 0:64].rearrange("p (b s) -> p b s", s=2 ** l), ALU.subtract)
                            ins.then_inc(S("dl_d"), 1)
                    for p in range(2):
                        n = 2 * u + p
                        B = dbuf(p)
                        dve.wait_ge(S("dl_tr"), (u * LEVELS + LEVELS - 1) * 2 + p + 1)
                        V.tensor_tensor(B["kd"], four(PS[:, 4 * p + 3, :]), heads(EKD[:, t, d, 4 * p:4 * p + 4]), ALU.mult).then_inc(S("dl_kd"), 1)
                    for p in range(2):
                        n = 2 * u + p
                        B = dbuf(p)
                        dve.wait_ge(S("dl_o"), n + 1)
                        hs = slice(4 * p, 4 * p + 4)
                        for h in range(4):
                            hh = 4 * p + h
                            ins = V.scalar_tensor_tensor(Cst[:, d, hh, :], Cst[:, d, hh, :], EGL[:, t, d, hh:hh + 1],
                                                         PS[:, 4 * p + 3, h * P:(h + 1) * P], ALU.mult, ALU.add)
                        ins.then_inc(S("dl_s"), 1)
                        if n >= 16:
                            dve.wait_ge(S("dl_s"), n + 1)
                            dve.sem_inc(S("st_new"), 1)
                        if 12 <= n < 16:
                            dve.wait_ge(S("dl_s"), n + 1)
                            V.memset(Cst[:, d, hs, :], 0.0).then_inc(S("dl_sz"), 1)
                            dve.wait_ge(S("dl_sz"), n - 11)
                        dve.wait_ge(S("dl_t"), 4 * n + 4)
                        dst = four(acc[:, t, p * HC:(p + 1) * HC])
                        if (d, t) in SECOND:
                            link(V.tensor_tensor(B["t"], B["t"], dst, ALU.add))
                        V.tensor_tensor(dst, four(PS[:, 4 * p, :]), B["t"], ALU.add).then_inc(S("dl_done"), 1)
                        dve.wait_ge(S("dl_done"), n + 1)
                dve.sem_inc(S("fin_start"), 1)

            def gate_out(L):
                if L == 0:
                    dve.wait_ge(S("grow_in"), 16)
                for t in range(NT):
                    dve.wait_ge(S("fin_sq"), L * PER["fin_sq"] + 2 * t + 2)
                    y = acc[:, t, :]
                    y8 = y.rearrange("p (h n) -> p h n", h=H)
                    r = ss[:, 0, 0:H]
                    V.tensor_reduce(r, fsq.rearrange("p (h n) -> p h n", h=H), AX, ALU.add).then_inc(S("fin_r"), 1)
                    dve.wait_ge(S("fin_i"), L * PER["fin_i"] + t + 1)
                    sharpen(0, H, 1.0 / P, 0.5)
                    link(V.tensor_tensor(y8, y8, heads(ss[:, 1, 0:H]), ALU.mult))
                    if L == 0:
                        link(V.tensor_tensor(y, y, grow, ALU.mult))
                    else:
                        link(V.tensor_tensor(y8, y8, dng[:, :].unsqueeze(1).broadcast_to([P, H, P]), ALU.mult))
                        link(V.tensor_tensor(y, y, o[:, t, :], ALU.mult))
                    link(V.scalar_tensor_tensor(y, fex, 1.0, y, ALU.add, ALU.mult))
                    dve.sem_inc(S("y"), 1)
                    dve.sem_inc(S("fin_read"), 1)
                dve.wait_ge(S("g1e"), L * PER["g1e"] + 4)
                for i in range(10):
                    j, t = divmod(i, NT)
                    c = int(t > 0)
                    dve.wait_ge(S("omm"), L * PER["omm"] + i + 1)
                    link(V.tensor_tensor(ytmp, PS[:, i % 4, :], g1b[:, c, j, :], ALU.mult))
                    xx = x[:, t, j * HC:(j + 1) * HC]
                    V.tensor_tensor(xx, xx, ytmp, ALU.add).then_inc(S("x_new"), 1)
                    dve.wait_ge(S("x_new"), L * PER["x_new"] + i + 1)

            def experts(L):
                dve.wait_ge(S("logits"), L * PER["logits"] + 1)
                lg = PS[:, 0, 0:80].rearrange("p (t e) -> p t e", t=NT)
                link(V.tensor_reduce(af5[:, 0, :], lg, AX, ALU.max))
                V.tensor_tensor(aff[:, :, :], lg, heads(af5[:, 0, :], EX), ALU.subtract).then_inc(S("sm"), 1)
                dve.wait_ge(S("sme"), L * PER["sme"] + 1)
                link(V.tensor_reduce(af5[:, 1, :], aff[:, :, :], AX, ALU.add))
                link(V.reciprocal(af5[:, 1, :], af5[:, 1, :]))
                V.tensor_tensor(aff[:, :, :], aff[:, :, :], heads(af5[:, 1, :], EX), ALU.mult).then_inc(S("aff"), 1)
                dve.wait_ge(S("afft"), L * PER["afft"] + 1)
                link(V.tensor_copy(affP, PS[0:EX, 2, 0:P]))
                link(V.tensor_copy(affS, PS[0:EX, 1, :]))
                for src, first, cap in ((affS, 0, CAPS), (affP, CAPS, CAPP)):
                    for r in range(cap // 8):
                        s8 = slice(first + 8 * r, first + 8 * r + 8)
                        link(V.max(vals[:, s8], src))
                        link(V.max_index(idx[:, s8], vals[:, s8], src))
                        if r < cap // 8 - 1:
                            link(V.match_replace(src, vals[:, s8], src, -1.0))
                link(V.tensor_copy(idf[:, :], idx[:, :]))
                V.tensor_scalar(idf[:, 0:CAPS], idf[:, 0:CAPS], float(P), None, ALU.add).then_inc(S("topk"), 1)
                dve.wait_ge(S("selt"), L * PER["selt"] + 1)
                V.tensor_copy(gsel[0:CAP, :], PS[0:CAP, 3, 0:EX]).then_inc(S("sel"), 1)
                V.tensor_copy(idT[0:CAP, :], PS[0:CAP, 3, EX:2 * EX]).then_inc(S("sel"), 1)
                dve.wait_ge(S("sel"), L * PER["sel"] + 2)

                def pick(e, q, first):
                    if not first:
                        dve.wait_ge(S("scattered"), L * PER["scattered"] + (e - 1) * 16)
                    V.tensor_copy(idc[q][0:CAP, :], idT[0:CAP, bass.ds(e, 1)])
                    V.tensor_copy(gsc[q][0:CAP, :], gsel[0:CAP, bass.ds(e, 1)]).then_inc(S("idx"), 1)

                def tokens(e, q, first):
                    dve.wait_ge(S("xs_turned"), L * PER["xs_turned"] + e + 1)
                    for j in range(2):
                        b = PS[:, 6 + j, 0:4 * CAP].rearrange("p (k c) -> p k c", k=4)
                        for c, cs in ((1, slice(0, CAPS)), (0, slice(CAPS, CAP))):
                            V.tensor_tensor(xsT[q][:, 4 * j:4 * j + 4, cs], b[:, :, cs],
                                            heads(AB[:, 1, 4 * j:4 * j + 4, c], cs.stop - cs.start), ALU.mult).then_inc(S("xs_a"), 1)
                    dve.wait_ge(S("xs_a"), L * PER["xs_a"] + e * 4 + 4)
                    for c, cs in ((1, slice(0, CAPS)), (0, slice(CAPS, CAP))):
                        ins = V.tensor_tensor(xsT[q][:, :, cs], xsT[q][:, :, cs], heads(modT[:, 24:32, c], cs.stop - cs.start), ALU.add)
                    ins.then_inc(S("xs_in"), 1)

                def hidden(e, q, first):
                    for hf in range(2):
                        k = S("h_chain")
                        dve.wait_ge(S("gexp"), L * PER["gexp"] + e * 2 + (hf + 1))
                        V.scalar_tensor_tensor(eb[hf], eb[hf], 1.0, PS[:, 2 * hf, 0:320], ALU.add, ALU.mult).then_inc(k, 1)
                        dve.wait_ge(k, L * PER["h_chain"] + e * 2 + (hf + 1))
                        dve.wait_ge(S("moe_used"), L * PER["moe_used"] + e * 6 + (2 * hf + 2))
                        V.scalar_tensor_tensor(hdT[:, 4 * hf:4 * hf + 4, :], eb[hf].rearrange("p (k c) -> p k c", k=4), 0.5,
                                        PS[:, 2 * hf + 1, 0:320].rearrange("p (k c) -> p k c", k=4), ALU.mult, ALU.mult).then_inc(S("hidden"), 1)

                pick(0, 0, True)
                tokens(0, 0, True)
                pick(1, 1, True)
                hidden(0, 0, True)
                tokens(1, 1, False)
                pick(2, 0, False)
                hidden(1, 1, False)
                tokens(2, 0, False)
                with dve.Fori(1, EX // 2 - 1) as i:
                    for q in range(2):
                        pick(i * 2 + (q + 1), 1 - q, False)
                        hidden(i * 2 + q, q, False)
                        tokens(i * 2 + (q + 1), 1 - q, False)
                pick(EX - 1, 1, False)
                hidden(EX - 2, 0, False)
                tokens(EX - 1, 1, False)
                hidden(EX - 1, 1, False)

                dve.wait_ge(S("g2b"), L * PER["g2b"] + 4)
                dve.wait_ge(S("moe_in"), 16 * NT * (L + 1))
                for t in range(NT):
                    c = int(t > 0)
                    oo = o[:, t, :].rearrange("p (j n) -> p j n", j=2)
                    link(V.tensor_tensor(oo, oo, PS[:, 2 * c:2 * c + 2, :], ALU.mult))
                    V.tensor_tensor(x[:, t, :], x[:, t, :], o[:, t, :], ALU.add).then_inc(S("x_moe"), 1)
                    dve.wait_ge(S("x_moe"), L * PER["x_moe"] + t + 1)

            for L in range(2):
                modulation(L)
                norm(2 * L)
                if L == 0:
                    gates_mlstm()
                    scan_mlstm()
                else:
                    gates_delta()
                    proj_delta()
                    sums_delta()
                    scan_delta()
                gate_out(L)
                norm(2 * L + 1)
                experts(L)
            norm(4)
            dve.wait_ge(S("grow_in"), 32)
            for t in range(NT):
                dve.wait_ge(S("xn"), 4 * PER["xn"] + t + 1)
                V.tensor_tensor(o[:, t, :], o[:, t, :], grow, ALU.mult).then_inc(S("y_ready"), 1)


_INS = ['x_prompt', 'x_sample', 'state_mlstm_C', 'state_mlstm_n', 'state_mlstm_m', 'state_delta_S', 'c', 'c_ctx',
        'norm1_g', 'norm2_g', 'w_ada', 'b_ada', 'w_in', 'w_out', 'w_router', 'w_gate', 'w_up', 'w_down', 'final_g',
        'mlstm_ig_b', 'mlstm_fg_b', 'mlstm_norm_g', 'delta_conv_w', 'delta_A_log', 'delta_dt_bias', 'delta_norm_g']
_OUTS = [('out_p', (1, 128, 1024)), ('out_s', (1, 512, 1024)), ('out_C', (1, 1, 2, 8, 128, 128)),
         ('out_n', (1, 1, 2, 8, 128)), ('out_m', (1, 1, 2, 8)), ('out_S', (1, 1, 2, 8, 128, 128))]


def _constants():
    import numpy as np

    r, c = np.arange(128)[:, None], np.arange(128)[None, :]
    big = np.float32(-1e30)
    c32 = np.stack([r == c, r <= c, r >= c, np.where(r <= c, 0, big), np.where(r >= c, 0, big), np.ones((128, 128))], 1).astype(np.float32)
    lm = []
    for d in range(2):
        for l in range(7):
            s = 2 ** l
            br, bcol = r // s, c // s
            if d == 0:
                lm.append((br % 2 == 0) & (bcol == br + 1))
            else:
                lm.append((br % 2 == 1) & (bcol == br - 1))
    return c32, np.stack(lm, 1).astype(np.uint16) * np.uint16(0x3F80)


def kernel(**inputs):
    import numpy as _np
    import concourse.bacc as _bacc
    from concourse import mybir as _mybir
    from concourse.bass_utils import run_bass_kernel_spmd as _run

    nc = _bacc.Bacc("TRN2", target_bir_lowering=False, num_devices=1)
    arrays, args = {}, {}
    c32, lm = _constants()
    for name, arr in [(n, inputs[n]) for n in _INS] + [("c32", c32), ("lmask", lm)]:
        arr = _np.ascontiguousarray(arr)
        arrays[f"in_{name}_dram"] = arr
        args[name] = nc.dram_tensor(f"in_{name}_dram", arr.shape, _mybir.dt.from_np(arr.dtype), kind="ExternalInput").ap()
    for name, shape in _OUTS:
        args[name] = nc.dram_tensor(f"{name}_dram", shape, _mybir.dt.float32, kind="ExternalOutput").ap()
    backbone(nc, args)
    r = _run(nc, [arrays], core_ids=[0])
    return tuple(r.results[0][f"{name}_dram"] for name, _ in _OUTS)
```

```python
from contextlib import ExitStack

import concourse.bass as bass
from concourse import mybir

F32 = mybir.dt.float32
U16 = mybir.dt.uint16
BF16 = mybir.dt.bfloat16
U32 = mybir.dt.uint32
ALU = mybir.AluOpType
ACT = mybir.ActivationFunctionType
AX = mybir.AxisListType.X

P = 128
D = 1024
KT = D // P
NT = 5
TOK = NT * P
H = 8
EX = 16
CAPS = 64
CAPP = 16
CAP = CAPS + CAPP
HC = 512
MOD = 48
EPS = 1e-6
LEVELS = 7
TAPS = 5
ROWW = 64
NROW = 8
UNITS = [(0, 1), (1, 4), (0, 2), (1, 3), (0, 3), (1, 2), (0, 4), (1, 1), (0, 0), (1, 0)]
SECOND = {(0, 3), (1, 2), (0, 4), (1, 1), (1, 0)}


PER = dict(ada_ev=12, fin_r=5, fin_i=5, ab=1, ada_mm=12, afft=1, aff=1, fin_read=5, fin_sq=10, fin_start=1, g1b=4, g1e=4, g2b=4,
           gathered=256, gexp=32, gmm=1, h_chain=32, hidden=32, idx=16, logits=1, moe_used=96, o_ready=32,
           omm=10, scattered=256, selt=1, sel=2, sme=1, sm=1, st_new=4, topk=1, x_moe=5, x_new=10, xs_a=64,
           xs_in=16, xs_turned=16, yt_ev=10, yt=5, y=5, xn=5, xt=10, hta=20, htv=5, sq=5)


def backbone(nc, a):
    ctx = ExitStack()
    sems = {}

    def S(name):
        if name not in sems:
            sems[name] = ctx.enter_context(nc.semaphore(name))
        return sems[name]

    def sb(name, shape, dt=F32):
        return ctx.enter_context(nc.sbuf_tensor(name, shape, dt))

    def bc(ap, shape):
        return ap.broadcast_to(shape)

    def heads(ap, n=P):
        return ap.unsqueeze(2).broadcast_to([ap.shape[0], ap.shape[1], n])

    with ctx:
        PS = ctx.enter_context(nc.psum_tensor("ps", [P, 8, HC], F32))

        x = sb("x", [P, NT, D])
        hT = sb("hT", [P, KT, TOK])
        acc = hT[:, :, :].rearrange("p a b -> p (a b)").rearrange("p (t d) -> p t d", t=NT)
        qkv = sb("qkv", [P, 3 * NT * D])
        qT = qkv[:, 0:NT * D].rearrange("p (k t) -> p k t", k=KT)
        kT = qkv[:, NT * D:2 * NT * D].rearrange("p (k t) -> p k t", k=KT)
        v = qkv[:, 2 * NT * D:3 * NT * D].rearrange("p (t d) -> p t d", t=NT)
        yT = qT
        og = sb("og", [P, NT * D])
        o = og[:, :].rearrange("p (t d) -> p t d", t=NT)
        slots3 = sb("slots3", [P, 3, KT * HC])
        SL = [slots3[:, j, :] for j in range(3)] + [qkv[:, j * KT * HC:(j + 1) * KT * HC] for j in range(3)]
        slot = [s.rearrange("p (k n) -> p k n", k=KT) for s in SL]
        wk = sb("wk", [P, 4608])
        half = [slots3[:, 2, j * HC:(j + 1) * HC] for j in range(8)]
        lmask = sb("lmask", [P, 2 * LEVELS + 3, P], U16)
        identb, NUb, NLb = (lmask[:, 2 * LEVELS + j, :].bitcast(BF16) for j in range(3))
        c32 = sb("c32", [P, 4, P])
        ident, TU, TL, ones = (c32[:, j, :] for j in range(4))
        tri = [TU, TL]
        neg_ts = [NLb, NUb]
        neg_st = [NUb, NLb]
        rows = sb("rows", [P, 3, P])
        vecT = sb("vecT", [P, 264])
        norm_g = vecT[:, 0:32].rearrange("p (k l t) -> p k l t", k=2, l=2)
        biasT = vecT[:, 48:144].rearrange("p (l b) -> p l b", l=2)
        convT = vecT[:, 144:264].rearrange("p (j c) -> p j c", j=TAPS)
        cnd = sb("cnd", [P, 3, 16])
        modT = sb("modT", [P, MOD, 2])
        AB = sb("AB", [P, 2, KT, 2])
        ss = sb("ss", [P, 4, 16])
        epst = sb("epst", [P, 1])
        tick = sb("tick", [1, 1])
        wgt = sb("wgt", [P, KT, 32])
        wrt = sb("wrt", [P, KT, EX])
        gb0 = sb("gb0", [P, 2, 2, H])
        gb1 = sb("gb1", [P, 2, 2, H])
        m0 = sb("m0", [P, 2, H])
        dng = sb("dng", [P, P])
        nst = sb("nst", [P, 2, H])
        ga = sb("ga", [P, 14, NT * 2 * H])
        G3 = [ga[:, j, :].rearrange("p (t d h) -> p t d h", t=NT, d=2) for j in range(14)]
        sm = sb("sm", [P, 2, 4, 4])
        gt = sb("gt", [P, NT, 2, 2, H])
        aff = sb("aff", [P, NT, EX])
        af5 = sb("af5", [P, 2, NT])
        vals = sb("vals", [EX, CAP])
        idx = sb("idx", [EX, CAP], U32)
        idf = sb("idf", [EX, CAP])
        gsel = sb("gsel", [P, EX])
        idT = sb("idT", [P, EX], U32)
        idc = [sb(f"idc{q}", [P, 1], U32) for q in range(2)]
        gsc = [sb(f"gsc{q}", [P, 1]) for q in range(2)]

        xn_d = nc.dram_tensor("xn_d", [TOK, D], F32, kind="Internal").ap()
        moe_d = nc.dram_tensor("moe_d", [TOK, D], F32, kind="Internal").ap()

        xs = [og[:, q * D:(q + 1) * D] for q in range(2)]
        osb = [og[:, (2 + q) * D:(3 + q) * D] for q in range(2)]
        hdT = og[:, 4 * D:4 * D + KT * CAP].rearrange("p (k c) -> p k c", k=KT)
        xsT = [wk[:, q * 640:(q + 1) * 640].rearrange("p (k c) -> p k c", k=KT) for q in range(2)]
        eb = [wk[:, 1280 + q * 320:1600 + q * 320] for q in range(2)]
        affS = wk[0:EX, 2048:2560]
        affP = wk[0:EX, 2560:2688]
        zero = wk[:, 3072:4096]
        grow = wk[:, 3072:4096]
        mrow = [wk[0:2, 2048 + q * HC:2048 + (q + 1) * HC] for q in range(2)]
        Cst = wk[:, 0:2048].rearrange("p (d h v) -> p d h v", d=2, h=H)
        cpad = [wk[:, q * 676:(q + 1) * 676] for q in range(2)]
        cout = [wk[:, 1352 + q * 640:1992 + q * 640] for q in range(2)]
        cex = wk[:, 2632:3272]
        qn = wk[:, 3272:3912].rearrange("p (t c) -> p t c", t=NT)

        def four(ap):
            return ap.rearrange("p (h n) -> p h n", h=4)

        def w_ada(L):
            return a["w_ada"][L].rearrange("(k p) n -> p k n", p=P)

        def w_in(L):
            return a["w_in"][L].rearrange("(k p) n -> p k n", p=P)

        def w_out(L):
            return a["w_out"][L].rearrange("(k p) n -> p k n", p=P)

        NADA, NIN, NOUT = 12, 8, 2
        MIX = NADA + NIN + NOUT

        def mix_slot(n):
            return n % 3 if n < NADA + NIN else n - NADA - NIN

        def mix_landed(L, n):
            j = mix_slot(n)
            return 16 * (sum(mix_slot(k) == j for k in range(n + 1)) + L * (sum(mix_slot(k) == j for k in range(MIX)) + EX))

        def item_end(L, g):
            fm = (4, 6)[L]
            return 4 * (g + 1) if g < fm else 4 * fm + NT * (g + 1 - fm)

        def unit_used(L, n):
            if n < NADA:
                return S("ada_mm"), L * PER["ada_mm"] + n + 1
            if n < NADA + NIN:
                return S(f"pj_mm{L}"), item_end(L, n - NADA)
            return S("omm"), L * PER["omm"] + NT * (n - NADA - NIN + 1)

        def moe_base(L, j):
            return ((L + 1) * sum(mix_slot(k) == j for k in range(MIX)) if j < 3 else 0) + L * EX

        BETA, GC, NG, EG, EGL, EKD, NBETA, NEG = (G3[j] for j in range(4, 12))

        def delta_buffers(u, p):
            chunks = [four(slots3[:, j // 8, j % 8 * HC:(j % 8 + 1) * HC]) for j in range(24)]
            w = chunks[10 * (u % 2) + 5 * p:][:5]
            xb = wk[:, 4096 + 256 * p:4096 + 256 * (p + 1)].rearrange("p (h n) -> p h n", h=4)
            return dict(E=w[0], CM=(w[0], chunks[22 + p]), AT=w[1], qk=w[2], kd=w[3], DT=w[4], D=chunks[20 + p], X=xb)

        Rb, Wb, tb = (four(wk[:, 2048 + j * HC:2048 + (j + 1) * HC]) for j in range(3))

        def at_all(u, l, p):
            return (u * LEVELS + l) * 2 + p + 1

        def at_early(u, l, p):
            return (u * (LEVELS - 1) + l) * 2 + p + 1

        def at_late(u, l, p):
            return (u * (LEVELS - 1) + l - 1) * 2 + p + 1

        def at_mid(u, l, p):
            return (u * (LEVELS - 2) + l - 1) * 2 + p + 1

        def parts(d):
            return (slice(0, 64), slice(64, P)) if d == 0 else (slice(64, P), slice(0, 64))

        fsq = slots3[:, 2, 0:1024]
        fex = slots3[:, 2, 1024:2048]
        g1b = slots3[:, 2, 2048:4096].rearrange("p (c j n) -> p c j n", c=2, j=2)
        ytmp = slots3[:, 2, 0:HC]
        cjunk = wk[:, 3912:4040]

        def cols(ap, l, which):
            return ap.rearrange("p h (b w s) -> p h b w s", w=2, s=2 ** l)[:, :, :, which, :]

        def cols1(ap, l, which):
            return ap.rearrange("p (b w s) -> p b w s", w=2, s=2 ** l)[:, :, which, :]

        def pack(ap, l):
            return ap.rearrange("p h (b s) -> p h b s", s=2 ** l)

        land = [S(f"landed{j}") for j in range(6)]
        block = ctx.enter_context(nc.Block())

        @block.sync
        def _(sp):
            with nc.allow_non_contiguous_dma(reason="small vectors"):
                loads = [
                    (c32[:, :, :], a["c32"]), (lmask[:, :, :], a["lmask"]),
                    (rows[0:16, 0, :], a["norm1_g"].rearrange("l (t p) -> (l t) p", p=P)),
                    (rows[16:32, 0, :], a["norm2_g"].rearrange("l (t p) -> (l t) p", p=P)),
                    (rows[32:40, 0, :], a["c_ctx"].rearrange("(t p) -> t p", p=P)),
                    (rows[40:48, 0, :], a["c"].rearrange("b (t p) -> (b t) p", p=P)),
                    (rows[0:96, 1, :], a["b_ada"].rearrange("l (t p) -> (l t) p", p=P)),
                    (rows[0:120, 2, :], a["delta_conv_w"][0].rearrange("j (t p) -> (j t) p", p=P)),
                    (gb0[:, :, 0, :], a["mlstm_ig_b"][0].partition_broadcast(P)),
                    (gb0[:, :, 1, :], a["mlstm_fg_b"][0].partition_broadcast(P)),
                    (gb1[:, :, 0, :], a["delta_A_log"][0].partition_broadcast(P)),
                    (gb1[:, :, 1, :], a["delta_dt_bias"][0].partition_broadcast(P)),
                    (m0[:, :, :], a["state_mlstm_m"][0, 0].partition_broadcast(P)),
                    (dng[:, :], a["delta_norm_g"][0].partition_broadcast(P)),
                ]
                for dst, src in loads:
                    sp.dma_start(dst, src).then_inc(S("setup"), 16)
            sp.dma_start(x[:, 0, :], a["x_prompt"][0]).then_inc(S("x_in"), 16)
            sp.dma_start(x[:, 1:5, :], a["x_sample"][0].rearrange("(t p) d -> p t d", p=P)).then_inc(S("x_in"), 16)

            for L in range(2):
                if L == 1:
                    sp.wait_ge(S("gmm"), 1)
                sp.dma_start(wgt[:, :, :], w_in(L)[:, :, 4 * D:4 * D + 32]).then_inc(S("wg_in"), 16)
                if L == 1:
                    sp.wait_ge(S("logits"), 1)
                sp.dma_start(wrt[:, :, :], a["w_router"][L].rearrange("(k p) e -> p k e", p=P)).then_inc(S("wr_in"), 16)
                for n in range(NADA + NIN):
                    j = mix_slot(n)
                    if n < 3:
                        if L:
                            sp.wait_ge(S("moe_used"), 6 * (EX - 1) + j + 1)
                    else:
                        sp.wait_ge(*unit_used(L, n - 3))
                    if n < NADA:
                        src = w_ada(L)[:, :, n * HC:(n + 1) * HC]
                    else:
                        g = n - NADA
                        src = w_in(L)[:, :, g * HC:(g + 1) * HC]
                    sp.dma_start(slot[j], src).then_inc(land[j], 16)
                st = a["state_mlstm_C" if L == 0 else "state_delta_S"][0, 0]
                if L == 1:
                    sp.wait_ge(S("tr1"), 24)
                for d in range(2):
                    sp.dma_start(Cst[:, d, :, :], st[d].rearrange("h k v -> k h v")).then_inc(S("st_in"), 16)
                if L == 0:
                    with nc.allow_non_contiguous_dma(reason="normaliser state, 2048 numbers"):
                        for d in range(2):
                            sp.dma_start(nst[:, d, :], a["state_mlstm_n"][0, 0, d].rearrange("h k -> k h")).then_inc(S("st_in"), 16)
                    sp.dma_start(grow, a["mlstm_norm_g"][0].partition_broadcast(P)).then_inc(S("grow_in"), 16)
                sp.wait_ge(S("st_new"), L * PER["st_new"] + 4)
                out = a["out_C" if L == 0 else "out_S"][0, 0]
                for d in range(2):
                    sp.dma_start(out[d].rearrange("h k v -> k h v"), Cst[:, d, :, :]).then_inc(S("st_out"), 16)
                if L == 0:
                    with nc.allow_non_contiguous_dma(reason="normaliser state, 2048 numbers"):
                        for d in range(2):
                            sp.dma_start(a["out_n"][0, 0, d].rearrange("h k -> k h"), nst[:, d, :]).then_inc(S("st_out"), 16)
                    sp.dma_start(a["out_m"][0], G3[13][0:1, 0, :, :]).then_inc(S("st_out"), 16)

                sp.wait_ge(S("fin_start"), L + 1)
                for j in range(NOUT):
                    sp.dma_start(slot[j], w_out(L)[:, :, j * HC:(j + 1) * HC]).then_inc(land[j], 16)

                for t in range(NT):
                    sp.wait_ge(S("xn"), (2 * L + 1) * PER["xn"] + t + 1)
                    sp.dma_start(xn_d[t * P:(t + 1) * P, :], o[:, t, :]).then_inc(S("xn_out"), 16)
                gv = a["w_gate"][L].rearrange("e (k p) n -> e p k n", p=P)
                uv = a["w_up"][L].rearrange("e (k p) n -> e p k n", p=P)
                dv = a["w_down"][L].rearrange("e (k p) n -> e p k n", p=P)
                six = [(gv, 0), (uv, 0), (gv, 1), (uv, 1), (dv, 0), (dv, 1)]

                def expert_loads(e, first):
                    for j, (w, hf) in enumerate(six):
                        if not first:
                            sp.wait_ge(S("moe_used"), L * PER["moe_used"] + e * 6 + (j - 5))
                        sp.dma_start(slot[j], w[e, :, :, hf * HC:(hf + 1) * HC]).then_inc(land[j], 16)

                sp.wait_ge(*unit_used(L, MIX - 1))
                sp.wait_ge(S("x_new"), L * PER["x_new"] + 10)
                expert_loads(0, True)
                with sp.Fori(1, EX) as e:
                    expert_loads(e, False)
                sp.wait_ge(S("scattered"), L * PER["scattered"] + 16 * EX)
                for t in range(NT):
                    sp.dma_start(o[:, t, :], moe_d[t * P:(t + 1) * P, :]).then_inc(S("moe_in"), 16)
            sp.dma_start(grow, a["final_g"].partition_broadcast(P)).then_inc(S("grow_in"), 16)
            for t in range(NT):
                sp.wait_ge(S("y_ready"), t + 1)
                dst = a["out_p"][0] if t == 0 else a["out_s"][0, (t - 1) * P:t * P, :]
                sp.dma_start(dst, o[:, t, :]).then_inc(S("y_out"), 16)
            sp.wait_ge(S("y_out"), 16 * NT)
            sp.wait_ge(S("st_out"), 16 * 7)

        @block.gpsimd
        def _(pool):
            pool.memset(epst[:, :], EPS).then_inc(S("epst"), 1)

            for L in range(2):
                if L == 1:
                    pool.wait_ge(S("moe_in"), 16 * NT)
                pool.wait_ge(S("x_new"), L * PER["x_new"] + 10)
                pool.wait_ge(S("st_out"), 16 * (5 if L == 0 else 7))
                pool.memset(zero, 0.0).then_inc(S("zeroed"), 1)
                pool.wait_ge(S("zeroed"), L + 1)
                for t in range(NT):
                    pool.dma_start(moe_d[t * P:(t + 1) * P, :], zero).then_inc(S("zero_out"), 16)

                def hold(before):
                    if not (isinstance(before, int) and before == 0):
                        pool.wait_ge(S("held"), before)
                    pool.tensor_tensor(tick[:, 0:1], epst[0:1, :], epst[0:1, :], ALU.mult).then_inc(S("held"), 1)

                def gather(e, q, first):
                    pool.wait_ge(S("idx"), L * PER["idx"] + e + 1)
                    if not first:
                        pool.wait_ge(S("xs_turned"), L * PER["xs_turned"] + e - 1)
                    hold(2 * EX * L + e if first else e * 2 + (2 * EX * L - 1))
                    pool.indirect_dma_start(xs[q][0:CAP, :], None, xn_d,
                                            bass.IndirectOffsetOnAxis(ap=idc[q][0:CAP, :], axis=0)).then_inc(S("gathered"), 16)

                def scatter(e, q, first):
                    pool.wait_ge(S("o_ready"), L * PER["o_ready"] + e * 2 + 2)
                    if not first:
                        pool.wait_ge(S("scattered"), L * PER["scattered"] + e * 16)
                    hold(2 * EX * L + (2 * EX - 1) if e is EX - 1 else e * 2 + (2 * EX * L + 2))
                    pool.indirect_dma_start(moe_d, bass.IndirectOffsetOnAxis(ap=idc[q][0:CAP, :], axis=0),
                                            osb[q][0:CAP, :], None, compute_op=ALU.add).then_inc(S("scattered"), 16)

                pool.wait_ge(S("xn_out"), 16 * NT * (L + 1))
                pool.wait_ge(S("zero_out"), 16 * NT * (L + 1))
                gather(0, 0, True)
                gather(1, 1, True)
                scatter(0, 0, True)
                gather(2, 0, False)
                scatter(1, 1, False)
                with pool.Fori(1, EX // 2 - 1) as i:
                    for q in range(2):
                        gather(i * 2 + (q + 1), 1 - q, False)
                        scatter(i * 2 + q, q, False)
                gather(EX - 1, 1, False)
                scatter(EX - 2, 0, False)
                scatter(EX - 1, 1, False)
                pool.wait_ge(S("scattered"), L * PER["scattered"] + 16 * EX)

        @block.scalar
        def _(act):
            A = nc.scalar.activation

            chain = [0]

            def link(ins):
                chain[0] += 1
                ins.then_inc(S("act_chain"), 1)
                act.wait_ge(S("act_chain"), chain[0])

            def inverse_root(dst, src, scale):
                link(A(dst, src, ACT.Ln, scale=scale, bias=epst[:, 0:1]))
                return A(dst, dst, ACT.Exp, scale=-0.5)

            act.wait_ge(S("vec"), 1)
            act.wait_ge(S("epst"), 1)
            A(cnd[:, 0, :], vecT[:, 32:48], ACT.Exp, scale=-1.0).then_inc(S("cexp"), 1)

            def norm(i):
                for t in range(NT):
                    act.wait_ge(S("x_in"), 32) if i == 0 else act.wait_ge(*x_ready(i, t))
                    link(A(o[:, t, :], x[:, t, :], ACT.Square, accum_out=ss[:, 0, t:t + 1]))
                    inverse_root(ss[:, 1, t:t + 1], ss[:, 0, t:t + 1], 1.0 / D).then_inc(S("sq"), 1)

            def x_ready(i, t):
                if i in (1, 3):
                    return S("x_new"), PER["x_new"] * (i // 2 + 1)
                return S("x_moe"), PER["x_moe"] * (i // 2 - 1) + t + 1

            def norm_evac(L, k):
                for t in range(NT):
                    act.wait_ge(S("xt"), (2 * L + k) * PER["xt"] + 2 * t + 1)
                    if t == 0:
                        act.wait_ge(S("ab"), L * PER["ab"] + 1)
                    c = int(t > 0)
                    for kt in range(4):
                        A(hT[:, kt, t * P:(t + 1) * P], PS[:, 2 * (t % 2) + 2, kt * P:(kt + 1) * P], ACT.Identity,
                          scale=AB[:, k, kt, c:c + 1], bias=modT[:, 24 * k + kt, c:c + 1]).then_inc(S("hta"), 1)

            def proj(L):
                if L == 0:
                    for i in range(36):
                        act.wait_ge(S("pj_mm0"), i + 1)
                        b = 2 * (i % 3)
                        if i < 16:
                            dst = (qT if i < 8 else kT)[:, i % 8, :]
                            sc = 1.0 if i < 8 else float(P) ** -0.5
                            A(dst[:, P:TOK], PS[:, b, :], ACT.Copy, scale=sc)
                            A(dst[:, 0:P], PS[:, b + 1, 0:P], ACT.Copy, scale=sc).then_inc(S("pj_ev0"), 1)
                        else:
                            g, t = divmod(i - 16, NT)
                            dst = (v if g < 2 else o)[:, t, (g % 2) * HC:(g % 2 + 1) * HC]
                            A(dst, PS[:, b, :], ACT.Copy).then_inc(S("pj_ev0"), 1)
                    return

                def evac(i):
                    act.wait_ge(S("pj_mm1"), i + 1)
                    b = 2 * (i % 3)
                    if i < 24:
                        if i == 0:
                            act.wait_ge(S("padded"), 2)
                        if i >= 2:
                            act.wait_ge(S("cv_done"), i - 1)
                        A(cpad[i % 2][:, 132:676].rearrange("p (r w) -> p r w", r=NROW)[:, :, 2:2 + ROWW],
                          PS[:, b, :].rearrange("p (r w) -> p r w", r=NROW), ACT.Copy)
                        A(cpad[i % 2][:, 2:130], PS[:, b + 1, 0:P], ACT.Copy).then_inc(S("pj_ev1"), 1)
                    else:
                        g, t = divmod(i - 24, NT)
                        A(o[:, t, g * HC:(g + 1) * HC], PS[:, b, :], ACT.Copy).then_inc(S("pj_ev1"), 1)

                def squares(i):
                    act.wait_ge(S("tr1"), i + 1)
                    if i >= 16:
                        c = (i - 16) * P
                        A(v[:, 0:4, c:c + P], four(PS[:, 6, :]), ACT.Copy)
                        A(v[:, 4, c:c + P], PS[:, 7, 0:P], ACT.Copy).then_inc(S("tr1_ev"), 1)
                    else:
                        if i >= 1:
                            act.wait_ge(S("qn"), i)
                        for t in range(NT):
                            src = PS[:, 6, t * P:(t + 1) * P] if t < 4 else PS[:, 7, 0:P]
                            ins = A(cjunk, src, ACT.Square, accum_out=ss[:, 0, t:t + 1])
                            link(ins)
                        inverse_root(ss[:, 1, 0:NT], ss[:, 0, 0:NT], 1.0).then_inc(S("sqj"), 1)

                def back(i):
                    act.wait_ge(S("tr2"), i + 1)
                    dst = (qT if i < 8 else kT)[:, i % 8, :]
                    A(dst[:, 0:4 * P], PS[:, 6, :], ACT.Copy)
                    A(dst[:, 4 * P:TOK], PS[:, 7, 0:P], ACT.Copy).then_inc(S("tr2_ev"), 1)

                for i in range(26):
                    if 2 <= i and i - 2 < 16:
                        back(i - 2)
                    if i < 24:
                        evac(i)
                    if 1 <= i <= 24:
                        squares(i - 1)
                    if i < 24:
                        act.wait_ge(S("cv_done"), i + 1)
                        if i:
                            act.wait_ge(S("silu"), i)
                        A(cex, cout[i % 2], ACT.Tanh).then_inc(S("cvexp"), 1)
                for i in range(24, 34):
                    evac(i)

            def gates(L):
                if L == 0:
                    act.wait_ge(S("g0"), 1)
                    A(ga[:, 1, :], ga[:, 0, :], ACT.Exp, scale=-1.0).then_inc(S("g0a"), 1)
                    act.wait_ge(S("g0a"), 1)
                    A(ga[:, 1, :], ga[:, 1, :], ACT.Ln, bias=1.0).then_inc(S("g0a"), 1)
                    act.wait_ge(S("g0"), 2)
                    for j in (9, 10, 11, 12):
                        A(ga[:, j, :], ga[:, j, :], ACT.Exp).then_inc(S("g0a"), 1)
                    return
                act.wait_ge(S("g1"), 1)
                A(ga[:, 1, :], ga[:, 0, :], ACT.Exp, scale=-1.0).then_inc(S("g1a"), 1)
                act.wait_ge(S("g1a"), 1)
                A(ga[:, 1, :], ga[:, 1, :], ACT.Ln, bias=1.0).then_inc(S("g1a"), 1)
                A(ga[:, 4, :], ga[:, 4, :], ACT.Exp, scale=-1.0).then_inc(S("g1a"), 1)
                A(gb1[:, :, 0, :], gb1[:, :, 0, :], ACT.Exp).then_inc(S("g1a"), 1)

            def gates_delta2():
                act.wait_ge(S("g1"), 2)
                for j in (7, 8, 9):
                    A(ga[:, j, :], ga[:, j, :], ACT.Exp).then_inc(S("g1a"), 1)

            def mlstm():
                for n in range(20):
                    d, t = UNITS[n // 2]
                    p = n % 2
                    act.wait_ge(S("ml_bc"), n + 1)
                    if n >= 2:
                        act.wait_ge(S("ml_ps"), n - 1)
                    for h in range(4):
                        A(four(half[4 * p])[:, h, :], PS[:, n % 2, h * P:(h + 1) * P], ACT.Exp,
                          bias=G3[3][:, t, d, 4 * p + h:4 * p + h + 1]).then_inc(S("ml_e"), 1)

            def delta():
                def decay(u, p):
                    d, t = UNITS[u]
                    n = 2 * u + p
                    act.wait_ge(S("dl_bc"), n + 1)
                    if u >= 2:
                        act.wait_ge(S("dl_x"), at_all(u - 2, LEVELS - 1, p))
                    for h in range(4):
                        A(delta_buffers(u, p)["E"][:, h, :], PS[:, 4, h * P:(h + 1) * P], ACT.Exp,
                          bias=NG[:, t, d, 4 * p + h:4 * p + h + 1]).then_inc(S("dl_e"), 1)

                def inter(u, p):
                    d, t = UNITS[u]
                    n = 2 * u + p
                    act.wait_ge(S("dl_qs"), n + 1)
                    if n:
                        act.wait_ge(S("dl_done"), n)
                    for h in range(4):
                        A(tb[:, h, :], PS[:, 7, h * P:(h + 1) * P], ACT.Copy,
                          scale=EG[:, t, d, 4 * p + h:4 * p + h + 1]).then_inc(S("dl_t"), 1)

                def solved(u, p):
                    n = 2 * u + p
                    act.wait_ge(S("dl_w"), n + 1)
                    if n:
                        act.wait_ge(S("dl_o"), n)
                    A(Wb, four(PS[:, 6, :]), ACT.Copy).then_inc(S("dl_we"), 1)

                def fill(u, l):
                    if u and l in (0, 3):
                        inter(u - 1, l // 3)
                    if l in (1, 4):
                        if u:
                            solved(u - 1, l // 3)
                        if u + 1 < len(UNITS):
                            decay(u + 1, l // 3)

                for p in range(2):
                    decay(0, p)
                for u, (d, t) in enumerate(UNITS):
                    off = 1 - d
                    first, then = parts(d)
                    for l in range(LEVELS):
                        for p in range(2):
                            DT = delta_buffers(u, p)["DT"]
                            if l == 0:
                                act.wait_ge(S("dl_tr"), at_early(u, l, p))
                                if u >= 2:
                                    act.wait_ge(S("dl_w"), 2 * (u - 2) + p + 1)
                                ins = A(DT, four(PS[:, 2 * p + 1, :]), ACT.Copy)
                            elif l < LEVELS - 1:
                                act.wait_ge(S("dl_tr"), at_early(u, l, p))
                                ins = A(cols(DT, l, off), cols(four(PS[:, 2 * p + 1 - l % 2, :]), l, off), ACT.Copy)
                            else:
                                act.wait_ge(S("dl_dx"), at_late(u, l, p))
                                ins = A(DT[first, :, then], four(PS[first, 2 * p, :])[:, :, 0:64], ACT.Copy, scale=-1.0)
                            ins.then_inc(S("dl_dt"), 1)
                        fill(u, l)
                for l in range(LEVELS):
                    fill(len(UNITS), l)

            def gate_out(L):
                for t in range(NT):
                    act.wait_ge(S("fin_start"), L * PER["fin_start"] + 1)
                    if t:
                        act.wait_ge(S("fin_read"), L * PER["fin_read"] + t)
                    A(fsq, acc[:, t, :], ACT.Square).then_inc(S("fin_sq"), 1)
                    A(fex, o[:, t, :], ACT.Tanh, scale=0.5).then_inc(S("fin_sq"), 1)
                    act.wait_ge(S("fin_r"), L * PER["fin_r"] + t + 1)
                    inverse_root(ss[:, 1, 0:H], ss[:, 0, 0:H], 1.0 / P).then_inc(S("fin_i"), 1)
                    if t:
                        yt_copy(L, t - 1)
                yt_copy(L, NT - 1)

            def yt_copy(L, t):
                act.wait_ge(S("yt"), L * PER["yt"] + t + 1)
                for j in range(2):
                    A(yT[:, 4 * j:4 * j + 4, t * P:(t + 1) * P], four(PS[:, 2 * (t % 2) + j, :]), ACT.Copy).then_inc(S("yt_ev"), 1)
                if t == NT - 1:
                    for c in range(2):
                        for j in range(2):
                            act.wait_ge(S("g1b"), L * PER["g1b"] + 2 * c + j + 1)
                            A(g1b[:, c, j, :], PS[:, 4 + 2 * c + j, :], ACT.Copy).then_inc(S("g1e"), 1)

            def experts(L):
                act.wait_ge(S("sm"), L * PER["sm"] + 1)
                A(aff[:, :, :], aff[:, :, :], ACT.Exp).then_inc(S("sme"), 1)

                def expert(e, q, first):
                    for hf in range(2):
                        act.wait_ge(S("moe_used"), L * PER["moe_used"] + e * 6 + (2 * hf + 1))
                        if not first:
                            act.wait_ge(S("hidden"), L * PER["hidden"] + e * 2 + (hf - 1))
                        A(eb[hf], PS[:, 2 * hf, 0:320], ACT.Tanh, scale=0.5).then_inc(S("gexp"), 1)
                    for hf in range(2):
                        act.wait_ge(S("moe_used"), L * PER["moe_used"] + e * 6 + (5 + hf))
                        if hf == 0 and not first:
                            act.wait_ge(S("scattered"), L * PER["scattered"] + (e - 1) * 16)
                        A(osb[q][0:CAP, hf * HC:(hf + 1) * HC], PS[0:CAP, 4 + hf, :], ACT.Copy,
                          scale=gsc[q][0:CAP, :]).then_inc(S("o_ready"), 1)

                expert(0, 0, True)
                expert1(expert)
                with act.Fori(1, EX // 2) as i:
                    for q in range(2):
                        expert(i * 2 + q, q, False)

            def expert1(expert):
                L = act_layer[0]
                for hf in range(2):
                    act.wait_ge(S("moe_used"), L * PER["moe_used"] + 6 + 2 * hf + 1)
                    act.wait_ge(S("hidden"), L * PER["hidden"] + hf + 1)
                    A(eb[hf], PS[:, 2 * hf, 0:320], ACT.Tanh, scale=0.5).then_inc(S("gexp"), 1)
                for hf in range(2):
                    act.wait_ge(S("moe_used"), L * PER["moe_used"] + 6 + 5 + hf)
                    A(osb[1][0:CAP, hf * HC:(hf + 1) * HC], PS[0:CAP, 4 + hf, :], ACT.Copy,
                      scale=gsc[1][0:CAP, :]).then_inc(S("o_ready"), 1)

            def modulation(L):
                for n in range(NADA):
                    act.wait_ge(S("ada_mm"), L * PER["ada_mm"] + n + 1)
                    if n >= 2:
                        act.wait_ge(S("ada_tr"), L * NADA + n - 1)
                    A(mrow[n % 2], PS[0:2, n % 2, :], ACT.Copy).then_inc(S("ada_ev"), 1)

            act_layer = [0]
            for L in range(2):
                act_layer[0] = L
                modulation(L)
                norm(2 * L)
                norm_evac(L, 0)
                if L == 0:
                    gates(0)
                    proj(0)
                    mlstm()
                else:
                    gates(1)
                    proj(1)
                    gates_delta2()
                    delta()
                gate_out(L)
                norm(2 * L + 1)
                norm_evac(L, 1)
                experts(L)
            norm(4)

        @block.tensor
        def _(pe):
            mm = nc.tensor.matmul
            tr = nc.tensor.transpose

            pe.wait_ge(S("setup"), 16 * 14)
            tr(PS[:, 0, 0:48], rows[0:48, 0, :], ident[0:48, 0:48])
            tr(PS[:, 0, 48:144], rows[0:96, 1, :], ident[0:96, 0:96])
            tr(PS[:, 0, 144:264], rows[0:120, 2, :], ident[0:120, 0:120]).then_inc(S("vect"), 1)

            def modulation(L):
                def turn(n):
                    pe.wait_ge(S("ada_ev"), L * PER["ada_ev"] + n + 1)
                    for b in range(4):
                        blk = n * 4 + b
                        ins = tr(PS[:, 2, 2 * blk:2 * blk + 2], mrow[n % 2][:, b * P:(b + 1) * P], ident[0:2, 0:2])
                    ins.then_inc(S("ada_tr"), 1)

                pe.wait_ge(S("cond"), 1)
                if L:
                    pe.wait_ge(S("x_moe"), NT)
                for n in range(NADA):
                    j = mix_slot(n)
                    pe.wait_ge(land[j], mix_landed(L, n))
                    if n >= 2:
                        pe.wait_ge(S("ada_ev"), L * PER["ada_ev"] + n - 1)
                    for kt in range(KT):
                        ins = mm(PS[0:2, n % 2, :], cnd[:, 1, kt:16:8], slot[j][:, kt, :],
                                 start=(kt == 0), stop=(kt == KT - 1))
                    ins.then_inc(S("ada_mm"), 1)
                    if n:
                        turn(n - 1)
                turn(NADA - 1)

            def norm_turn(L, k):
                for t in range(NT):
                    pe.wait_ge(S("xn"), (2 * L + k) * PER["xn"] + t + 1)
                    if t >= 2:
                        pe.wait_ge(S("hta"), (2 * L + k) * PER["hta"] + 4 * (t - 1))
                        pe.wait_ge(S("htv"), (2 * L + k) * PER["htv"] + t - 1)
                    for j in range(2):
                        for kt in range(4):
                            c = (4 * j + kt) * P
                            ins = tr(PS[:, 2 * (t % 2) + 2 + j, kt * P:(kt + 1) * P], o[:, t, c:c + P], ident)
                        ins.then_inc(S("xt"), 1)
                pe.wait_ge(S("hta"), (2 * L + k) * PER["hta"] + 4 * NT)
                pe.wait_ge(S("htv"), (2 * L + k) * PER["htv"] + NT)

            def gates(L):
                pe.wait_ge(S("wg_in"), 16 * (L + 1))
                for t in range(NT):
                    for kt in range(KT):
                        ins = mm(PS[:, 7, t * 32:(t + 1) * 32], hT[:, kt, t * P:(t + 1) * P], wgt[:, kt, :],
                                 start=(kt == 0), stop=(kt == KT - 1))
                ins.then_inc(S("gmm"), 1)

            def feature_major(L, i, sl, cb):
                b = 2 * (i % 3)
                if i >= 3:
                    pe.wait_ge(S(f"pj_ev{L}"), i - 2)
                for kt in range(KT):
                    w = slot[sl][:, kt, cb * P:(cb + 1) * P]
                    mm(PS[:, b, :], w, hT[:, kt, P:TOK], start=(kt == 0), stop=(kt == KT - 1))
                    ins = mm(PS[:, b + 1, 0:P], w, hT[:, kt, 0:P], start=(kt == 0), stop=(kt == KT - 1))
                return ins.then_inc(S(f"pj_mm{L}"), 1)

            def token_major(L, i, sl, t):
                if i >= 3:
                    pe.wait_ge(S(f"pj_ev{L}"), i - 2)
                for kt in range(KT):
                    ins = mm(PS[:, 2 * (i % 3), :], hT[:, kt, t * P:(t + 1) * P], slot[sl][:, kt, :],
                             start=(kt == 0), stop=(kt == KT - 1))
                return ins.then_inc(S(f"pj_mm{L}"), 1)

            def unit(L, g):
                n = NADA + g
                pe.wait_ge(land[mix_slot(n)], mix_landed(L, n))
                return mix_slot(n)

            def proj_mlstm():
                i = 0
                for g in range(8):
                    sl = unit(0, g)
                    for k in range(4 if g < 4 else NT):
                        feature_major(0, i, sl, k) if g < 4 else token_major(0, i, sl, k)
                        i += 1
                pe.wait_ge(S("pj_ev0"), 36)

            def proj_delta():
                def turn1(i):
                    pe.wait_ge(S("silu"), i + 1)
                    if i == 0:
                        pe.wait_ge(S("gev1"), 4)
                    elif i <= 16:
                        pe.wait_ge(S("tr2_ev"), i)
                    if i >= 17:
                        pe.wait_ge(S("tr1_ev"), i - 16)
                    for t in range(NT):
                        dst = PS[:, 6, t * P:(t + 1) * P] if t < 4 else PS[:, 7, 0:P]
                        ins = tr(dst, cout[i % 2][:, t * P:(t + 1) * P], ident)
                    ins.then_inc(S("tr1"), 1)

                def turn2(i):
                    pe.wait_ge(S("qn"), i + 1)
                    for t in range(NT):
                        dst = PS[:, 6, t * P:(t + 1) * P] if t < 4 else PS[:, 7, 0:P]
                        ins = tr(dst, qn[:, t, :], ident)
                    ins.then_inc(S("tr2"), 1)

                for i in range(26):
                    if 2 <= i and i - 2 < 16:
                        turn2(i - 2)
                    if i < 24:
                        g, k = divmod(i, 4)
                        if k == 0:
                            sl = unit(1, g)
                        feature_major(1, i, sl, k)
                    if 1 <= i <= 24:
                        turn1(i - 1)
                i = 24
                for g in range(6, 8):
                    sl = unit(1, g)
                    for t in range(NT):
                        token_major(1, i, sl, t)
                        i += 1
                pe.wait_ge(S("tr1_ev"), 8)
                pe.wait_ge(S("tr2_ev"), 16)
                pe.wait_ge(S("pj_ev1"), 34)

            def masked(bank, mask, src, neg=None):
                for h in range(4):
                    mm(PS[:, bank, h * P:(h + 1) * P], src[:, h:h + 1].broadcast_to([P, P]), ident,
                       start=(h == 0), stop=False, skip_group_check=True)
                return mm(PS[:, bank, :], identb, mask.unsqueeze(1).broadcast_to([P, 4, P]), start=False, stop=True,
                          skip_group_check=True)

            def sums(L, src, sem_in, sem_out):
                pe.wait_ge(*sem_in)
                for d in range(2):
                    mm(PS[:, 7, 40 * d:40 * d + 40].rearrange("p (t h) -> p t h", t=NT), tri[d], src[:, :, d, :], start=True, stop=True)
                mm(PS[:, 7, 80:160], ones, src[:, :, :, :].rearrange("p t d h -> p (t d h)"), start=True, stop=True).then_inc(sem_out, 1)

            def stab_mlstm():
                sums(0, G3[2], (S("lf"), 1), S("bsum"))
                pe.wait_ge(S("aready"), 1)
                for n in range(20):
                    d, t = UNITS[n // 2]
                    p = n % 2
                    if n >= 4:
                        pe.wait_ge(S("mxr"), n - 3)
                    masked(n % 4, neg_ts[d], G3[3][:, t, d, 4 * p:4 * p + 4]).then_inc(S("amm"), 1)
                pe.wait_ge(S("mxr"), 20)
                for d in range(2):
                    last = ident[:, 127:128] if d == 0 else ident[:, 0:1]
                    ins = mm(PS[:, 7, 40 * d:40 * d + 40].rearrange("p (t h) -> p t h", t=NT), last.broadcast_to([P, P]),
                             G3[6][:, :, d, :], start=True, stop=True)
                ins.then_inc(S("mlast"), 1)

            def scan_mlstm():
                def exponents(n):
                    d, t = UNITS[n // 2]
                    p = n % 2
                    if n == 0:
                        pe.wait_ge(S("nm"), 1)
                    if n >= 2:
                        pe.wait_ge(S("ml_e"), 4 * n - 4)
                    masked(n % 2, neg_st[d], G3[8][:, t, d, 4 * p:4 * p + 4]).then_inc(S("ml_bc"), 1)

                def scores(n):
                    d, t = UNITS[n // 2]
                    p = n % 2
                    ts = slice(t * P, (t + 1) * P)
                    if n:
                        pe.wait_ge(S("ml_ps"), n)
                    for h in range(4):
                        tr(PS[:, 3, h * P:(h + 1) * P], kT[:, 4 * p + h, ts], ident)
                    for h in range(4):
                        ins = mm(PS[:, 2, h * P:(h + 1) * P], kT[:, 4 * p + h, ts], qT[:, 4 * p + h, ts], start=True, stop=True)
                    ins.then_inc(S("ml_s"), 1)

                def back(n):
                    d, t = UNITS[n // 2]
                    p = n % 2
                    ts = slice(t * P, (t + 1) * P)
                    E, PSb, kw = (four(half[4 * p + j]) for j in range(3))
                    b7 = PS[:, 7, 16 * p:16 * p + 12]
                    pe.wait_ge(S("ml_ps"), n + 1)
                    if n == 0:
                        pe.wait_ge(S("st_in"), 64)
                    if n:
                        pe.wait_ge(S("ml_c"), n)
                    for h in range(4):
                        hh = 4 * p + h
                        mm(PS[:, 4, h * P:(h + 1) * P], kw[:, h, :], v[:, t, hh * P:(hh + 1) * P], start=True, stop=True)
                        ins = mm(b7[:, 8 + h:9 + h], kw[:, h, :], ones[:, 0:1], start=True, stop=True)
                    for h in range(4):
                        mm(b7[:, h:h + 1], PSb[:, h, :], ones[:, 0:1], start=True, stop=True)
                    if n >= 16:
                        pe.wait_ge(S("ml_cz"), n - 15)
                    for h in range(4):
                        ins = mm(b7[:, 4 + h:5 + h], qT[:, 4 * p + h, ts], nst[:, d, 4 * p + h:4 * p + h + 1], start=True, stop=True)
                    ins.then_inc(S("ml_sum"), 1)
                    if n:
                        pe.wait_ge(S("ml_done"), n)
                    for h in range(4):
                        ins = mm(PS[:, 5, h * P:(h + 1) * P], qT[:, 4 * p + h, ts], Cst[:, d, 4 * p + h, :], start=True, stop=True)
                    ins.then_inc(S("ml_qc"), 1)
                    for h in range(4):
                        hh = 4 * p + h
                        ins = mm(PS[:, 6, h * P:(h + 1) * P], PSb[:, h, :], v[:, t, hh * P:(hh + 1) * P], start=True, stop=True)
                    ins.then_inc(S("ml_bk"), 1)

                exponents(0)
                exponents(1)
                scores(0)
                for n in range(20):
                    if n + 1 < 20:
                        scores(n + 1)
                    if n + 2 < 20:
                        exponents(n + 2)
                    back(n)

            def scan_delta():
                sums(1, G3[3], (S("gl"), 1), S("gsum"))
                pe.wait_ge(S("gready"), 1)

                def hb(bank, h, n=P):
                    return PS[:, bank, h * P:h * P + n]

                def front(u, p):
                    d, t = UNITS[u]
                    n = 2 * u + p
                    if n:
                        pe.wait_ge(S("dl_kd"), n)
                    masked(4, neg_st[d], GC[:, t, d, 4 * p:4 * p + 4]).then_inc(S("dl_bc"), 1)
                    for h in range(4):
                        kk = kT[:, 4 * p + h, t * P:(t + 1) * P]
                        ins = mm(hb(5, h), kk, kk, start=True, stop=True)
                    ins.then_inc(S("dl_kk"), 1)

                def keys(u, p):
                    d, t = UNITS[u]
                    ts = slice(t * P, (t + 1) * P)
                    n = 2 * u + p
                    pe.wait_ge(S("dl_at"), n + 1)
                    for h in range(4):
                        tr(hb(4, h), kT[:, 4 * p + h, ts], ident)
                    for h in range(4):
                        ins = mm(hb(5, h), kT[:, 4 * p + h, ts], qT[:, 4 * p + h, ts], start=True, stop=True)
                    ins.then_inc(S("dl_kq"), 1)

                def from_state(u, p):
                    d, t = UNITS[u]
                    ts = slice(t * P, (t + 1) * P)
                    n = 2 * u + p
                    if n == 0:
                        pe.wait_ge(S("st_in"), 64 + 32)
                    else:
                        pe.wait_ge(S("dl_done"), n)
                    if n >= 16:
                        pe.wait_ge(S("dl_sz"), n - 15)
                    for h in range(4):
                        ins = mm(hb(6, h), kT[:, 4 * p + h, ts], Cst[:, d, 4 * p + h, :], start=True, stop=True)
                    ins.then_inc(S("dl_ks"), 1)
                    for h in range(4):
                        ins = mm(hb(7, h), qT[:, 4 * p + h, ts], Cst[:, d, 4 * p + h, :], start=True, stop=True)
                    ins.then_inc(S("dl_qs"), 1)

                def solve(u, p):
                    n = 2 * u + p
                    DT = delta_buffers(u, p)["DT"]
                    pe.wait_ge(S("dl_r"), n + 1)
                    pe.wait_ge(S("dl_dt"), at_all(u, LEVELS - 1, p))
                    for h in range(4):
                        ins = mm(hb(6, h), DT[:, h, :], Rb[:, h, :], start=True, stop=True)
                    ins.then_inc(S("dl_w"), 1)

                def outputs(u, p):
                    n = 2 * u + p
                    B = delta_buffers(u, p)
                    pe.wait_ge(S("dl_we"), n + 1)
                    for h in range(4):
                        ins = mm(hb(6, h), B["kd"][:, h, :], Wb[:, h, :], start=True, stop=True)
                    ins.then_inc(S("dl_sn"), 1)
                    pe.wait_ge(S("dl_t"), 4 * n + 4)
                    for h in range(4):
                        ins = mm(hb(7, h), B["qk"][:, h, :], Wb[:, h, :], start=True, stop=True)
                    ins.then_inc(S("dl_o"), 1)

                def fill(u, l):
                    nxt = u + 1 < len(UNITS)
                    if l in (3, 6) and nxt:
                        keys(u + 1, l // 3 - 1)
                    if u and l in (0, 3):
                        from_state(u - 1, l // 3)
                    if l in (1, 4):
                        if u:
                            solve(u - 1, l // 3)
                        if nxt:
                            front(u + 1, l // 3)
                    if u and l in (2, 5):
                        outputs(u - 1, l // 3)

                for p in range(2):
                    front(0, p)
                    keys(0, p)
                for u, (d, t) in enumerate(UNITS):
                    first, then = parts(d)
                    for l in range(LEVELS):
                        for p in range(2):
                            B = delta_buffers(u, p)
                            bx = 2 * p + 1 - l % 2
                            if l == 0:
                                pe.wait_ge(S("dl_at"), 2 * u + p + 1)
                                if u:
                                    pe.wait_ge(S("dl_dt"), at_all(u - 1, LEVELS - 1, p))
                                for h in range(4):
                                    ins = tr(hb(2 * p, h), B["AT"][:, h, :], ident)
                            elif l < LEVELS - 1:
                                pe.wait_ge(S("dl_cm"), at_mid(u, l, p))
                                pe.wait_ge(S("dl_d"), at_early(u, l - 1, p))
                                for h in range(4):
                                    ins = mm(pack(four(PS[:, bx, :])[:, :, 0:64], l)[:, h], B["CM"][l % 2][:, h, :],
                                             cols1(B["D"][:, h, :], l, d), start=True, stop=True)
                            else:
                                pe.wait_ge(S("dl_d"), at_early(u, l - 1, p))
                                for h in range(4):
                                    ins = mm(PS[then, bx, h * P:h * P + 64], B["AT"][first, h, then],
                                             B["D"][first, h, first], start=True, stop=True)
                            ins.then_inc(S("dl_x"), 1)
                        for p in range(2):
                            B = delta_buffers(u, p)
                            if l == 0:
                                continue
                            pe.wait_ge(S("dl_xe"), at_late(u, l, p))
                            pe.wait_ge(S("dl_dt"), at_all(u, l - 1, p))
                            for h in range(4):
                                if l < LEVELS - 1:
                                    ins = mm(hb(2 * p + l % 2, h, 64), B["DT"][:, h, :], B["X"][:, h, :], start=True, stop=True)
                                else:
                                    ins = mm(PS[first, 2 * p, h * P:h * P + 64], B["X"][then, h, :],
                                             B["DT"][then, h, then], start=True, stop=True)
                            ins.then_inc(S("dl_dx"), 1)
                        for p in range(2):
                            if l == LEVELS - 1:
                                continue
                            pe.wait_ge(S("dl_d"), at_early(u, l, p))
                            if l == 0 and u:
                                pe.wait_ge(S("dl_xe"), at_late(u - 1, LEVELS - 1, p))
                            for h in range(4):
                                ins = tr(hb(2 * p + 1 - l % 2, h), delta_buffers(u, p)["D"][:, h, :], ident)
                            ins.then_inc(S("dl_tr"), 1)
                        fill(u, l)
                for l in range(LEVELS):
                    fill(len(UNITS), l)

            def out(L):
                for t in range(NT):
                    pe.wait_ge(S("y"), L * PER["y"] + t + 1)
                    if t >= 2:
                        pe.wait_ge(S("yt_ev"), L * PER["yt_ev"] + 2 * (t - 1))
                    for kt in range(KT):
                        ins = tr(PS[:, 2 * (t % 2) + kt // 4, (kt % 4) * P:(kt % 4 + 1) * P], acc[:, t, kt * P:(kt + 1) * P], ident)
                    ins.then_inc(S("yt"), 1)
                gate_rows(16, 4, S("g1b"))
                pe.wait_ge(S("yt_ev"), L * PER["yt_ev"] + 2 * NT)
                i = 0
                for j in range(2):
                    n = NADA + NIN + j
                    pe.wait_ge(land[j], mix_landed(L, n))
                    for t in range(NT):
                        if i >= 4:
                            pe.wait_ge(S("x_new"), L * PER["x_new"] + i - 3)
                        for kt in range(KT):
                            ins = mm(PS[:, i % 4, :], yT[:, kt, t * P:(t + 1) * P], slot[j][:, kt, :], start=(kt == 0), stop=(kt == KT - 1))
                        ins.then_inc(S("omm"), 1)
                        i += 1

            def gate_rows(first, bank, sem):
                for c in range(2):
                    for j in range(2):
                        for b in range(4):
                            ins = mm(PS[:, bank + 2 * c + j, b * P:(b + 1) * P],
                                     modT[:, first + 4 * j + b, c:c + 1].broadcast_to([P, P]), ident, start=True, stop=True)
                        ins.then_inc(sem, 1)

            def experts(L):
                pe.wait_ge(S("wr_in"), 16 * (L + 1))
                for t in range(NT):
                    for kt in range(KT):
                        ins = mm(PS[:, 0, t * EX:(t + 1) * EX], hT[:, kt, t * P:(t + 1) * P], wrt[:, kt, :],
                                 start=(kt == 0), stop=(kt == KT - 1))
                ins.then_inc(S("logits"), 1)
                pe.wait_ge(S("aff"), L * PER["aff"] + 1)
                tr(PS[0:EX, 2, 0:P], aff[:, 0, :], ident)
                for t in range(1, NT):
                    ins = tr(PS[0:EX, 1, (t - 1) * P:t * P], aff[:, t, :], ident)
                ins.then_inc(S("afft"), 1)
                pe.wait_ge(S("topk"), L * PER["topk"] + 1)
                tr(PS[0:CAP, 3, 0:EX], vals[:, :], ident[0:EX, 0:EX])
                tr(PS[0:CAP, 3, EX:2 * EX], idf[:, :], ident[0:EX, 0:EX]).then_inc(S("selt"), 1)
                pe.wait_ge(S("sel"), L * PER["sel"] + 2)

                def turn(e, q, first):
                    pe.wait_ge(S("gathered"), L * PER["gathered"] + e * 16 + 16)
                    if not first:
                        pe.wait_ge(S("xs_in"), L * PER["xs_in"] + e)
                    for kt in range(KT):
                        ins = tr(PS[:, 6 + kt // 4, (kt % 4) * CAP:(kt % 4 + 1) * CAP], xs[q][0:CAP, kt * P:(kt + 1) * P], ident[0:CAP, 0:CAP])
                    ins.then_inc(S("xs_turned"), 1)

                def hidden(e, q, first):
                    pe.wait_ge(S("xs_in"), L * PER["xs_in"] + e + 1)
                    for j in range(4):
                        pe.wait_ge(land[j], e * 16 + (16 * moe_base(L, j) + 16))
                        if not first:
                            pe.wait_ge(S("hidden"), L * PER["hidden"] + e * 2 + (j // 2 - 1))
                        for fb in range(4):
                            for kt in range(KT):
                                ins = mm(PS[:, j, fb * CAP:(fb + 1) * CAP], slot[j][:, kt, fb * P:(fb + 1) * P],
                                         xsT[q][:, kt, :], start=(kt == 0), stop=(kt == KT - 1))
                        ins.then_inc(S("moe_used"), 1)

                def down(e, q, first):
                    pe.wait_ge(S("hidden"), L * PER["hidden"] + e * 2 + 2)
                    for j in range(2):
                        pe.wait_ge(land[4 + j], e * 16 + (16 * moe_base(L, 4 + j) + 16))
                        if not first:
                            pe.wait_ge(S("o_ready"), L * PER["o_ready"] + e * 2 + (j - 1))
                        for ft in range(KT):
                            ins = mm(PS[0:CAP, 4 + j, :], hdT[:, ft, :], slot[4 + j][:, ft, :],
                                     start=(ft == 0), stop=(ft == KT - 1))
                        ins.then_inc(S("moe_used"), 1)

                turn(0, 0, True)
                hidden(0, 0, True)
                turn(1, 1, False)
                down(0, 0, True)
                hidden(1, 1, False)
                turn(2, 0, False)
                down(1, 1, False)
                with pe.Fori(1, EX // 2 - 1) as i:
                    for q in range(2):
                        e = i * 2 + q
                        hidden(e, q, False)
                        turn(i * 2 + (q + 1), 1 - q, False)
                        down(e, q, False)
                hidden(EX - 2, 0, False)
                turn(EX - 1, 1, False)
                down(EX - 2, 0, False)
                hidden(EX - 1, 1, False)
                down(EX - 1, 1, False)
                pe.wait_ge(S("hidden"), L * PER["hidden"] + 2 * EX)
                gate_rows(40, 0, S("g2b"))

            for L in range(2):
                modulation(L)
                norm_turn(L, 0)
                gates(L)
                if L == 0:
                    stab_mlstm()
                    proj_mlstm()
                    scan_mlstm()
                else:
                    proj_delta()
                    scan_delta()
                out(L)
                norm_turn(L, 1)
                experts(L)

        @block.vector
        def _(dve):
            V = nc.vector
            chain = [0]

            def link(ins):
                chain[0] += 1
                ins.then_inc(S("dve_chain"), 1)
                dve.wait_ge(S("dve_chain"), chain[0])

            dve.wait_ge(S("vect"), 1)
            V.tensor_copy(vecT[:, :], PS[:, 0, 0:264]).then_inc(S("vec"), 1)
            dve.wait_ge(S("vec"), 1)
            link(V.tensor_scalar(convT, convT, 0.5, None, ALU.mult))
            dve.wait_ge(S("cexp"), 1)
            link(V.tensor_scalar(cnd[:, 0, :], cnd[:, 0, :], 1.0, None, ALU.add))
            link(V.reciprocal(cnd[:, 0, :], cnd[:, 0, :]))
            V.tensor_tensor(cnd[:, 1, :], cnd[:, 0, :], vecT[:, 32:48], ALU.mult).then_inc(S("cond"), 1)

            def modulation(L):
                dve.wait_ge(S("ada_tr"), (L + 1) * NADA)
                link(V.tensor_tensor(modT[:, :, :], PS[:, 2, 0:96].rearrange("p (b c) -> p b c", c=2),
                                     biasT[:, L, :].unsqueeze(2).broadcast_to([P, MOD, 2]), ALU.add))
                for k in range(2):
                    ins = V.scalar_tensor_tensor(AB[:, k, :, :], modT[:, 8 + 24 * k:16 + 24 * k, :], 1.0,
                                                 norm_g[:, k, L, :].unsqueeze(2).broadcast_to([P, KT, 2]), ALU.add, ALU.mult)
                    if k == 0:
                        link(ins)
                ins.then_inc(S("ab"), 1)
                dve.wait_ge(S("ab"), L * PER["ab"] + 1)

            def sharpen(first, last, scale, gain=1.0):
                w, y, vv, tt = (ss[:, j, first:last] for j in range(4))
                link(V.tensor_scalar(vv, w, scale, EPS, ALU.mult, ALU.add))
                link(V.scalar_tensor_tensor(tt, y, -0.5 * gain, y, ALU.mult, ALU.mult))
                link(V.tensor_tensor(tt, tt, vv, ALU.mult))
                link(V.scalar_tensor_tensor(y, tt, 1.5 * gain, y, ALU.add, ALU.mult))

            def norm(i):
                L, k = divmod(i, 2)
                for t in range(NT + 1):
                    if t < NT:
                        dve.wait_ge(S("sq"), i * PER["sq"] + t + 1)
                        sharpen(t, t + 1, 1.0 / D)
                        V.tensor_scalar(o[:, t, :], x[:, t, :], ss[:, 1, t:t + 1], None, ALU.mult).then_inc(S("xn"), 1)
                    if i < 4 and t:
                        u = t - 1
                        c = int(u > 0)
                        dve.wait_ge(S("xt"), (2 * L + k) * PER["xt"] + 2 * u + 2)
                        dst = hT[:, 4:8, u * P:(u + 1) * P]
                        link(V.tensor_tensor(dst, four(PS[:, 2 * (u % 2) + 3, :]), heads(AB[:, k, 4:8, c]), ALU.mult))
                        V.tensor_tensor(dst, dst, heads(modT[:, 24 * k + 4:24 * k + 8, c]), ALU.add).then_inc(S("htv"), 1)

            def gates_mlstm():
                f, ig = gt[:, :, :, 1, :], gt[:, :, :, 0, :]
                dve.wait_ge(S("gmm"), 1)
                link(V.tensor_tensor(gt[:, :, :, :, :].rearrange("p t d k h -> p t (d k h)"),
                                     PS[:, 7, 0:160].rearrange("p (t c) -> p t c", t=NT),
                                     gb0[:, :, :, :].rearrange("p d k h -> p (d k h)").unsqueeze(1).broadcast_to([P, NT, 32]), ALU.add))
                V.scalar_tensor_tensor(G3[0], f, -1.0, f, ALU.mult, ALU.max).then_inc(S("g0"), 1)
                dve.wait_ge(S("g0a"), 2)
                V.scalar_tensor_tensor(G3[2], f, 0.0, G3[1], ALU.min, ALU.subtract).then_inc(S("lf"), 1)
                dve.wait_ge(S("bsum"), 1)
                link(V.tensor_copy(G3[4], PS[:, 7, 0:80].rearrange("p (d t h) -> p t d h", d=2, t=NT)))
                link(V.tensor_copy(ga[:, 5, :], PS[:, 7, 80:160]))
                V.tensor_tensor(G3[3], ig, G3[4], ALU.subtract).then_inc(S("aready"), 1)
                dve.wait_ge(S("aready"), 1)
                for n in range(20):
                    d, t = UNITS[n // 2]
                    p = n % 2
                    dve.wait_ge(S("amm"), n + 1)
                    V.tensor_reduce(G3[6][:, t, d, 4 * p:4 * p + 4], four(PS[:, n % 4, :]), AX, ALU.max).then_inc(S("mxr"), 1)
                dve.wait_ge(S("mxr"), 20)
                dve.wait_ge(S("mlast"), 1)
                link(V.tensor_copy(G3[7], PS[:, 7, 0:80].rearrange("p (d t h) -> p t d h", d=2, t=NT)))
                link(V.memset(G3[13][:, 0, :, :], 0.0))
                link(V.tensor_copy(G3[13][:, 1, 0, :], m0[:, 0, :]))
                link(V.tensor_copy(G3[13][:, 4, 1, :], m0[:, 1, :]))
                for s in range(4):
                    for d in range(2):
                        t = 1 + s if d == 0 else 4 - s
                        link(V.tensor_tensor(G3[7][:, t, d, :], G3[7][:, t, d, :], G3[13][:, t, d, :], ALU.max))
                        if s < 3:
                            t2 = t + 1 if d == 0 else t - 1
                            link(V.tensor_tensor(G3[13][:, t2, d, :], G3[7][:, t, d, :], G3[5][:, t, d, :], ALU.add))
                link(V.tensor_tensor(G3[7][:, 0, :, :], G3[7][:, 0, :, :], G3[13][:, 0, :, :], ALU.max))
                link(V.tensor_tensor(ga[:, 6, :], ga[:, 6, :], ga[:, 13, :], ALU.max))
                V.tensor_scalar(ga[:, 8, :], ga[:, 6, :], -1.0, None, ALU.mult).then_inc(S("nm"), 1)
                link(V.tensor_tensor(ga[:, 9, :], ga[:, 13, :], ga[:, 6, :], ALU.subtract))
                link(V.tensor_tensor(ga[:, 10, :], ga[:, 3, :], ga[:, 7, :], ALU.subtract))
                link(V.tensor_tensor(ga[:, 11, :], ga[:, 13, :], ga[:, 7, :], ALU.subtract))
                link(V.scalar_tensor_tensor(ga[:, 12, :], ga[:, 4, :], -1.0, ga[:, 6, :], ALU.mult, ALU.subtract))
                link(V.tensor_tensor(G3[13][:, 0, :, :], G3[7][:, 0, :, :], G3[5][:, 0, :, :], ALU.add))
                dve.sem_inc(S("g0"), 1)
                dve.wait_ge(S("g0a"), 6)

            def scan_mlstm():
                SC, Wt, DEC, EM = G3[9], G3[10], G3[11], G3[12]

                def mid(n):
                    d, t = UNITS[n // 2]
                    p = n % 2
                    E, PSb, kw = (four(half[4 * p + j]) for j in range(3))
                    dve.wait_ge(S("ml_s"), n + 1)
                    V.tensor_tensor(kw, four(PS[:, 3, :]), heads(Wt[:, t, d, 4 * p:4 * p + 4]), ALU.mult)
                    dve.wait_ge(S("ml_e"), 4 * n + 4)
                    V.tensor_tensor(PSb, four(PS[:, 2, :]), E, ALU.mult).then_inc(S("ml_ps"), 1)

                def end(n):
                    d, t = UNITS[n // 2]
                    p = n % 2
                    hs = slice(4 * p, 4 * p + 4)
                    b7 = PS[:, 7, 16 * p:16 * p + 12]
                    dve.wait_ge(S("ml_sum"), n + 1)
                    den = sm[:, p, 0, :]
                    link(V.tensor_tensor(den, b7[:, 4:8], SC[:, t, d, hs], ALU.mult))
                    link(V.tensor_tensor(den, den, b7[:, 0:4], ALU.add))
                    link(V.scalar_tensor_tensor(den, den, -1.0, den, ALU.mult, ALU.max))
                    link(V.tensor_tensor(den, den, EM[:, t, d, hs], ALU.max))
                    link(V.reciprocal(sm[:, p, 1, :], den))
                    link(V.tensor_tensor(sm[:, p, 3, :], sm[:, p, 1, :], SC[:, t, d, hs], ALU.mult))
                    link(V.tensor_tensor(nst[:, d, hs], nst[:, d, hs], DEC[:, t, d, hs], ALU.mult))
                    V.tensor_tensor(nst[:, d, hs], nst[:, d, hs], b7[:, 8:12], ALU.add)
                    dve.wait_ge(S("ml_qc"), n + 1)
                    for h in range(4):
                        hh = 4 * p + h
                        ins = V.scalar_tensor_tensor(Cst[:, d, hh, :], Cst[:, d, hh, :], DEC[:, t, d, hh:hh + 1],
                                                     PS[:, 4, h * P:(h + 1) * P], ALU.mult, ALU.add)
                    ins.then_inc(S("ml_c"), 1)
                    if n >= 16:
                        dve.wait_ge(S("ml_c"), n + 1)
                        dve.sem_inc(S("st_new"), 1)
                    if 12 <= n < 16:
                        dve.wait_ge(S("ml_c"), n + 1)
                        V.memset(nst[:, d, hs], 0.0)
                        V.memset(Cst[:, d, hs, :], 0.0).then_inc(S("ml_cz"), 1)
                        dve.wait_ge(S("ml_cz"), n - 11)
                    dst = acc[:, t, p * HC:(p + 1) * HC]
                    for h in range(4):
                        r = sm[:, p, 3, h:h + 1]
                        b5, o_ = PS[:, 5, h * P:(h + 1) * P], dst[:, h * P:(h + 1) * P]
                        if (d, t) in SECOND:
                            ins = V.scalar_tensor_tensor(o_, b5, r, o_, ALU.mult, ALU.add)
                        else:
                            ins = V.tensor_scalar(o_, b5, r, None, ALU.mult)
                        ins.then_inc(S("ml_ti"), 1)
                    dve.wait_ge(S("ml_bk"), n + 1)
                    dve.wait_ge(S("ml_ti"), 4 * n + 4)
                    for h in range(4):
                        o_ = dst[:, h * P:(h + 1) * P]
                        ins = V.scalar_tensor_tensor(o_, PS[:, 6, h * P:(h + 1) * P], sm[:, p, 1, h:h + 1], o_, ALU.mult, ALU.add)
                    ins.then_inc(S("ml_done"), 1)
                    dve.wait_ge(S("ml_done"), n + 1)

                dve.wait_ge(S("st_in"), 64)
                dve.wait_ge(S("pj_ev0"), 36)
                mid(0)
                for n in range(20):
                    if n + 1 < 20:
                        mid(n + 1)
                    end(n)
                dve.sem_inc(S("fin_start"), 1)

            def gates_delta():
                dve.wait_ge(S("gmm"), PER['gmm'] + 1)
                g4 = PS[:, 7, 0:160].rearrange("p (t d k h) -> p t d k h", t=NT, d=2, k=2)
                for d in range(2):
                    V.tensor_tensor(G3[2][:, :, d, :], g4[:, :, d, 0, :], gb1[:, d, 1, :].unsqueeze(1).broadcast_to([P, NT, H]), ALU.add).then_inc(S("gev1"), 1)
                    V.tensor_copy(G3[4][:, :, d, :], g4[:, :, d, 1, :]).then_inc(S("gev1"), 1)
                dve.wait_ge(S("gev1"), 4)
                V.scalar_tensor_tensor(ga[:, 0, :], ga[:, 2, :], -1.0, ga[:, 2, :], ALU.mult, ALU.max).then_inc(S("g1"), 1)
                dve.wait_ge(S("g1a"), 4)
                link(V.scalar_tensor_tensor(ga[:, 3, :], ga[:, 2, :], 0.0, ga[:, 1, :], ALU.max, ALU.add))
                link(V.tensor_scalar(gb1[:, :, 0, :], gb1[:, :, 0, :], -1.0, None, ALU.mult))
                for d in range(2):
                    ins = V.tensor_tensor(G3[3][:, :, d, :], G3[3][:, :, d, :], gb1[:, d, 0, :].unsqueeze(1).broadcast_to([P, NT, H]), ALU.mult)
                    ins.then_inc(S("gl0"), 1)
                dve.wait_ge(S("gl0"), 2)
                link(V.tensor_scalar(ga[:, 4, :], ga[:, 4, :], 1.0, None, ALU.add))
                V.reciprocal(ga[:, 4, :], ga[:, 4, :]).then_inc(S("gl"), 1)
                dve.wait_ge(S("gl"), 1)

            def sums_delta():
                dve.wait_ge(S("gsum"), 1)
                link(V.tensor_copy(GC, PS[:, 7, 0:80].rearrange("p (d t h) -> p t d h", d=2, t=NT)))
                link(V.tensor_copy(ga[:, 8, :], PS[:, 7, 80:160]))
                link(V.tensor_scalar(ga[:, 6, :], ga[:, 5, :], -1.0, None, ALU.mult))
                link(V.tensor_copy(ga[:, 7, :], ga[:, 5, :]))
                V.tensor_tensor(ga[:, 9, :], ga[:, 8, :], ga[:, 5, :], ALU.subtract).then_inc(S("g1"), 1)
                dve.wait_ge(S("g1"), 2)
                dve.wait_ge(S("g1a"), 7)
                link(V.tensor_scalar(ga[:, 10, :], ga[:, 4, :], -1.0, None, ALU.mult))
                V.tensor_scalar(ga[:, 11, :], ga[:, 7, :], -1.0, None, ALU.mult).then_inc(S("gready"), 1)
                dve.wait_ge(S("gready"), 1)

            def proj_delta():
                for q in range(2):
                    V.memset(cpad[q], 0.0).then_inc(S("padded"), 1)
                dve.wait_ge(S("padded"), 2)

                def conv(i):
                    dve.wait_ge(S("pj_ev1"), i + 1)
                    if i >= 2:
                        dve.wait_ge(S("tr1"), i - 1)
                    src, dst = cpad[i % 2], cout[i % 2]
                    for j in range(TAPS):
                        w = convT[:, j, i:i + 1]
                        for s, o_ in ((src[:, j:j + P].unsqueeze(1), dst[:, 0:P].unsqueeze(1)),
                                      (src[:, 132:676].rearrange("p (r w) -> p r w", r=NROW)[:, :, j:j + ROWW],
                                       dst[:, P:TOK].rearrange("p (r w) -> p r w", r=NROW))):
                            if j == 0:
                                ins = V.tensor_scalar(o_, s, w, None, ALU.mult)
                            else:
                                ins = V.scalar_tensor_tensor(o_, s, w, o_, ALU.mult, ALU.add)
                            if j == TAPS - 1 and s is not None and o_.shape[1] == NROW:
                                ins.then_inc(S("cv_done"), 1)
                                dve.wait_ge(S("cv_done"), i + 1)
                            else:
                                link(ins)

                def normed(i):
                    dve.wait_ge(S("sqj"), i + 1)
                    sharpen(0, NT, 1.0, float(P) ** -0.5 if i < 8 else 1.0)
                    if i:
                        dve.wait_ge(S("tr2"), i)
                    link(V.tensor_tensor(qn[:, 0:4, :], four(PS[:, 6, :]), heads(ss[:, 1, 0:4]), ALU.mult))
                    V.tensor_scalar(qn[:, 4, :], PS[:, 7, 0:P], ss[:, 1, 4:5], None, ALU.mult).then_inc(S("qn"), 1)

                for i in range(25):
                    if i < 24:
                        conv(i)
                    if 1 <= i and i - 1 < 16:
                        normed(i - 1)
                    if i < 24:
                        dve.wait_ge(S("cvexp"), i + 1)
                        V.scalar_tensor_tensor(cout[i % 2], cex, 1.0, cout[i % 2], ALU.add, ALU.mult).then_inc(S("silu"), 1)
                        dve.wait_ge(S("silu"), i + 1)

            def scan_delta():
                dve.wait_ge(S("st_in"), 96)

                def system(u, p):
                    B = delta_buffers(u, p)
                    n = 2 * u + p
                    dve.wait_ge(S("dl_kk"), n + 1)
                    dve.wait_ge(S("dl_e"), 4 * n + 4)
                    if u >= 2:
                        dve.wait_ge(S("dl_x"), at_all(u - 2, LEVELS - 1, p))
                    V.tensor_tensor(B["AT"], four(PS[:, 5, :]), B["E"], ALU.mult).then_inc(S("dl_at"), 1)

                def keys(u, p):
                    d, t = UNITS[u]
                    B = delta_buffers(u, p)
                    n = 2 * u + p
                    dve.wait_ge(S("dl_kq"), n + 1)
                    if u >= 2:
                        dve.wait_ge(S("dl_o"), 2 * (u - 2) + p + 1)
                    V.tensor_tensor(B["qk"], four(PS[:, 5, :]), B["E"], ALU.mult)
                    V.tensor_tensor(B["kd"], four(PS[:, 4, :]), heads(EKD[:, t, d, 4 * p:4 * p + 4]), ALU.mult).then_inc(S("dl_kd"), 1)

                def right_side(u, p):
                    d, t = UNITS[u]
                    n = 2 * u + p
                    dve.wait_ge(S("dl_ks"), n + 1)
                    if n:
                        dve.wait_ge(S("dl_w"), n)
                    for h in range(4):
                        hh = 4 * p + h
                        ins = V.scalar_tensor_tensor(Rb[:, h, :], PS[:, 6, h * P:(h + 1) * P], NEG[:, t, d, hh:hh + 1],
                                                     v[:, t, hh * P:(hh + 1) * P], ALU.mult, ALU.add)
                    link(ins)
                    V.tensor_tensor(Rb, Rb, heads(BETA[:, t, d, 4 * p:4 * p + 4]), ALU.mult).then_inc(S("dl_r"), 1)

                def end(u, p):
                    d, t = UNITS[u]
                    n = 2 * u + p
                    hs = slice(4 * p, 4 * p + 4)
                    dve.wait_ge(S("dl_sn"), n + 1)
                    for h in range(4):
                        hh = 4 * p + h
                        ins = V.scalar_tensor_tensor(Cst[:, d, hh, :], Cst[:, d, hh, :], EGL[:, t, d, hh:hh + 1],
                                                     PS[:, 6, h * P:(h + 1) * P], ALU.mult, ALU.add)
                    ins.then_inc(S("dl_s"), 1)
                    if n >= 16:
                        dve.wait_ge(S("dl_s"), n + 1)
                        dve.sem_inc(S("st_new"), 1)
                    if 12 <= n < 16:
                        dve.wait_ge(S("dl_s"), n + 1)
                        V.memset(Cst[:, d, hs, :], 0.0).then_inc(S("dl_sz"), 1)
                        dve.wait_ge(S("dl_sz"), n - 11)
                    dst = four(acc[:, t, p * HC:(p + 1) * HC])
                    if (d, t) in SECOND:
                        dve.wait_ge(S("dl_t"), 4 * n + 4)
                        link(V.tensor_tensor(tb, tb, dst, ALU.add))
                    dve.wait_ge(S("dl_o"), n + 1)
                    V.tensor_tensor(dst, four(PS[:, 7, :]), tb, ALU.add).then_inc(S("dl_done"), 1)
                    dve.wait_ge(S("dl_done"), n + 1)

                def mask_next(u, l, p):
                    d = UNITS[u][0]
                    if l + 1 < LEVELS - 1:
                        B = delta_buffers(u, p)
                        mk = lmask[:, d * LEVELS + l + 1, :].bitcast(BF16).unsqueeze(1).broadcast_to([P, 4, P])
                        V.tensor_tensor(B["CM"][(l + 1) % 2], B["AT"], mk, ALU.mult).then_inc(S("dl_cm"), 1)

                def fill(u, l):
                    nxt = u + 1 < len(UNITS)
                    if l in (3, 6) and nxt:
                        keys(u + 1, l // 3 - 1)
                    if u and l in (0, 3):
                        right_side(u - 1, l // 3)
                    if l in (2, 5):
                        if nxt:
                            system(u + 1, l // 3)
                        if u:
                            end(u - 1, l // 3)

                for p in range(2):
                    system(0, p)
                    keys(0, p)
                for u, (d, t) in enumerate(UNITS):
                    first, then = parts(d)
                    for l in range(LEVELS):
                        for p in range(2):
                            B = delta_buffers(u, p)
                            bx = 2 * p + 1 - l % 2
                            if l == 0:
                                dve.wait_ge(S("dl_x"), at_all(u, l, p))
                                mk = lmask[:, (1 - d) * LEVELS, :].bitcast(BF16).unsqueeze(1).broadcast_to([P, 4, P])
                                link(V.tensor_tensor(B["D"], four(PS[:, 2 * p, :]), mk, ALU.mult))
                                for h in range(4):
                                    hh = 4 * p + h
                                    ins = V.scalar_tensor_tensor(B["D"][:, h, :], B["D"][:, h, :], NBETA[:, t, d, hh:hh + 1],
                                                                 ident, ALU.mult, ALU.add)
                                ins.then_inc(S("dl_d"), 1)
                            else:
                                dve.wait_ge(S("dl_x"), at_all(u, l, p))
                                rows_ = slice(0, P) if l < LEVELS - 1 else then
                                V.tensor_tensor(B["X"][rows_], four(PS[rows_, bx, :])[:, :, 0:64],
                                                heads(BETA[rows_, t, d, 4 * p:4 * p + 4], 64), ALU.mult).then_inc(S("dl_xe"), 1)
                            mask_next(u, l, p)
                        for p in range(2):
                            if l in (0, LEVELS - 1):
                                continue
                            dst = cols(delta_buffers(u, p)["D"], l, d)
                            dve.wait_ge(S("dl_dx"), at_late(u, l, p))
                            V.tensor_tensor(dst, dst, pack(four(PS[:, 2 * p + l % 2, :])[:, :, 0:64], l), ALU.subtract).then_inc(S("dl_d"), 1)
                        fill(u, l)
                for l in range(LEVELS):
                    fill(len(UNITS), l)
                dve.sem_inc(S("fin_start"), 1)

            def gate_out(L):
                if L == 0:
                    dve.wait_ge(S("grow_in"), 16)
                for t in range(NT):
                    dve.wait_ge(S("fin_sq"), L * PER["fin_sq"] + 2 * t + 2)
                    y = acc[:, t, :]
                    y8 = y.rearrange("p (h n) -> p h n", h=H)
                    r = ss[:, 0, 0:H]
                    V.tensor_reduce(r, fsq.rearrange("p (h n) -> p h n", h=H), AX, ALU.add).then_inc(S("fin_r"), 1)
                    dve.wait_ge(S("fin_i"), L * PER["fin_i"] + t + 1)
                    sharpen(0, H, 1.0 / P, 0.5)
                    link(V.tensor_tensor(y8, y8, heads(ss[:, 1, 0:H]), ALU.mult))
                    if L == 0:
                        link(V.tensor_tensor(y, y, grow, ALU.mult))
                    else:
                        link(V.tensor_tensor(y8, y8, dng[:, :].unsqueeze(1).broadcast_to([P, H, P]), ALU.mult))
                        link(V.tensor_tensor(y, y, o[:, t, :], ALU.mult))
                    link(V.scalar_tensor_tensor(y, fex, 1.0, y, ALU.add, ALU.mult))
                    dve.sem_inc(S("y"), 1)
                    dve.sem_inc(S("fin_read"), 1)
                dve.wait_ge(S("g1e"), L * PER["g1e"] + 4)
                for i in range(10):
                    j, t = divmod(i, NT)
                    c = int(t > 0)
                    dve.wait_ge(S("omm"), L * PER["omm"] + i + 1)
                    link(V.tensor_tensor(ytmp, PS[:, i % 4, :], g1b[:, c, j, :], ALU.mult))
                    xx = x[:, t, j * HC:(j + 1) * HC]
                    V.tensor_tensor(xx, xx, ytmp, ALU.add).then_inc(S("x_new"), 1)
                    dve.wait_ge(S("x_new"), L * PER["x_new"] + i + 1)

            def experts(L):
                dve.wait_ge(S("logits"), L * PER["logits"] + 1)
                lg = PS[:, 0, 0:80].rearrange("p (t e) -> p t e", t=NT)
                link(V.tensor_reduce(af5[:, 0, :], lg, AX, ALU.max))
                V.tensor_tensor(aff[:, :, :], lg, heads(af5[:, 0, :], EX), ALU.subtract).then_inc(S("sm"), 1)
                dve.wait_ge(S("sme"), L * PER["sme"] + 1)
                link(V.tensor_reduce(af5[:, 1, :], aff[:, :, :], AX, ALU.add))
                link(V.reciprocal(af5[:, 1, :], af5[:, 1, :]))
                V.tensor_tensor(aff[:, :, :], aff[:, :, :], heads(af5[:, 1, :], EX), ALU.mult).then_inc(S("aff"), 1)
                dve.wait_ge(S("afft"), L * PER["afft"] + 1)
                link(V.tensor_copy(affP, PS[0:EX, 2, 0:P]))
                link(V.tensor_copy(affS, PS[0:EX, 1, :]))
                for src, first, cap in ((affS, 0, CAPS), (affP, CAPS, CAPP)):
                    for r in range(cap // 8):
                        s8 = slice(first + 8 * r, first + 8 * r + 8)
                        link(V.max(vals[:, s8], src))
                        link(V.max_index(idx[:, s8], vals[:, s8], src))
                        if r < cap // 8 - 1:
                            link(V.match_replace(src, vals[:, s8], src, -1.0))
                link(V.tensor_copy(idf[:, :], idx[:, :]))
                V.tensor_scalar(idf[:, 0:CAPS], idf[:, 0:CAPS], float(P), None, ALU.add).then_inc(S("topk"), 1)
                dve.wait_ge(S("selt"), L * PER["selt"] + 1)
                V.tensor_copy(gsel[0:CAP, :], PS[0:CAP, 3, 0:EX]).then_inc(S("sel"), 1)
                V.tensor_copy(idT[0:CAP, :], PS[0:CAP, 3, EX:2 * EX]).then_inc(S("sel"), 1)
                dve.wait_ge(S("sel"), L * PER["sel"] + 2)

                def pick(e, q, first):
                    if not first:
                        dve.wait_ge(S("scattered"), L * PER["scattered"] + (e - 1) * 16)
                    V.tensor_copy(idc[q][0:CAP, :], idT[0:CAP, bass.ds(e, 1)])
                    V.tensor_copy(gsc[q][0:CAP, :], gsel[0:CAP, bass.ds(e, 1)]).then_inc(S("idx"), 1)

                def tokens(e, q, first):
                    dve.wait_ge(S("xs_turned"), L * PER["xs_turned"] + e + 1)
                    for j in range(2):
                        b = PS[:, 6 + j, 0:4 * CAP].rearrange("p (k c) -> p k c", k=4)
                        for c, cs in ((1, slice(0, CAPS)), (0, slice(CAPS, CAP))):
                            V.tensor_tensor(xsT[q][:, 4 * j:4 * j + 4, cs], b[:, :, cs],
                                            heads(AB[:, 1, 4 * j:4 * j + 4, c], cs.stop - cs.start), ALU.mult).then_inc(S("xs_a"), 1)
                    dve.wait_ge(S("xs_a"), L * PER["xs_a"] + e * 4 + 4)
                    for c, cs in ((1, slice(0, CAPS)), (0, slice(CAPS, CAP))):
                        ins = V.tensor_tensor(xsT[q][:, :, cs], xsT[q][:, :, cs], heads(modT[:, 24:32, c], cs.stop - cs.start), ALU.add)
                    ins.then_inc(S("xs_in"), 1)

                def hidden(e, q, first):
                    for hf in range(2):
                        k = S("h_chain")
                        dve.wait_ge(S("gexp"), L * PER["gexp"] + e * 2 + (hf + 1))
                        V.scalar_tensor_tensor(eb[hf], eb[hf], 1.0, PS[:, 2 * hf, 0:320], ALU.add, ALU.mult).then_inc(k, 1)
                        dve.wait_ge(k, L * PER["h_chain"] + e * 2 + (hf + 1))
                        dve.wait_ge(S("moe_used"), L * PER["moe_used"] + e * 6 + (2 * hf + 2))
                        V.scalar_tensor_tensor(hdT[:, 4 * hf:4 * hf + 4, :], eb[hf].rearrange("p (k c) -> p k c", k=4), 0.5,
                                        PS[:, 2 * hf + 1, 0:320].rearrange("p (k c) -> p k c", k=4), ALU.mult, ALU.mult).then_inc(S("hidden"), 1)

                pick(0, 0, True)
                tokens(0, 0, True)
                pick(1, 1, True)
                hidden(0, 0, True)
                tokens(1, 1, False)
                pick(2, 0, False)
                hidden(1, 1, False)
                tokens(2, 0, False)
                with dve.Fori(1, EX // 2 - 1) as i:
                    for q in range(2):
                        pick(i * 2 + (q + 1), 1 - q, False)
                        hidden(i * 2 + q, q, False)
                        tokens(i * 2 + (q + 1), 1 - q, False)
                pick(EX - 1, 1, False)
                hidden(EX - 2, 0, False)
                tokens(EX - 1, 1, False)
                hidden(EX - 1, 1, False)

                dve.wait_ge(S("g2b"), L * PER["g2b"] + 4)
                dve.wait_ge(S("moe_in"), 16 * NT * (L + 1))
                for t in range(NT):
                    c = int(t > 0)
                    oo = o[:, t, :].rearrange("p (j n) -> p j n", j=2)
                    link(V.tensor_tensor(oo, oo, PS[:, 2 * c:2 * c + 2, :], ALU.mult))
                    V.tensor_tensor(x[:, t, :], x[:, t, :], o[:, t, :], ALU.add).then_inc(S("x_moe"), 1)
                    dve.wait_ge(S("x_moe"), L * PER["x_moe"] + t + 1)

            for L in range(2):
                modulation(L)
                norm(2 * L)
                if L == 0:
                    gates_mlstm()
                    scan_mlstm()
                else:
                    gates_delta()
                    proj_delta()
                    sums_delta()
                    scan_delta()
                gate_out(L)
                norm(2 * L + 1)
                experts(L)
            norm(4)
            dve.wait_ge(S("grow_in"), 32)
            for t in range(NT):
                dve.wait_ge(S("xn"), 4 * PER["xn"] + t + 1)
                V.tensor_tensor(o[:, t, :], o[:, t, :], grow, ALU.mult).then_inc(S("y_ready"), 1)


_INS = ['x_prompt', 'x_sample', 'state_mlstm_C', 'state_mlstm_n', 'state_mlstm_m', 'state_delta_S', 'c', 'c_ctx',
        'norm1_g', 'norm2_g', 'w_ada', 'b_ada', 'w_in', 'w_out', 'w_router', 'w_gate', 'w_up', 'w_down', 'final_g',
        'mlstm_ig_b', 'mlstm_fg_b', 'mlstm_norm_g', 'delta_conv_w', 'delta_A_log', 'delta_dt_bias', 'delta_norm_g']
_OUTS = [('out_p', (1, 128, 1024)), ('out_s', (1, 512, 1024)), ('out_C', (1, 1, 2, 8, 128, 128)),
         ('out_n', (1, 1, 2, 8, 128)), ('out_m', (1, 1, 2, 8)), ('out_S', (1, 1, 2, 8, 128, 128))]


def _constants():
    import numpy as np

    r, c = np.arange(128)[:, None], np.arange(128)[None, :]
    c32 = np.stack([r == c, r <= c, r >= c, np.ones((128, 128))], 1).astype(np.float32)
    lm = []
    for d in range(2):
        for l in range(7):
            s = 2 ** l
            br, bcol = r // s, c // s
            if d == 0:
                lm.append((br % 2 == 0) & (bcol == br + 1))
            else:
                lm.append((br % 2 == 1) & (bcol == br - 1))
    one, big = np.uint16(0x3F80), np.uint16(0xF149)
    bits = [m * one for m in lm] + [(r == c) * one, (r > c) * big, (r < c) * big]
    return c32, np.stack(bits, 1).astype(np.uint16)


def kernel(**inputs):
    import numpy as _np
    import concourse.bacc as _bacc
    from concourse import mybir as _mybir
    from concourse.bass_utils import run_bass_kernel_spmd as _run

    nc = _bacc.Bacc("TRN2", target_bir_lowering=False, num_devices=1)
    arrays, args = {}, {}
    c32, lm = _constants()
    for name, arr in [(n, inputs[n]) for n in _INS] + [("c32", c32), ("lmask", lm)]:
        arr = _np.ascontiguousarray(arr)
        arrays[f"in_{name}_dram"] = arr
        args[name] = nc.dram_tensor(f"in_{name}_dram", arr.shape, _mybir.dt.from_np(arr.dtype), kind="ExternalInput").ap()
    for name, shape in _OUTS:
        args[name] = nc.dram_tensor(f"{name}_dram", shape, _mybir.dt.float32, kind="ExternalOutput").ap()
    backbone(nc, args)
    r = _run(nc, [arrays], core_ids=[0])
    return tuple(r.results[0][f"{name}_dram"] for name, _ in _OUTS)
```

```python
from contextlib import ExitStack

import concourse.bass as bass
from concourse import mybir

F32 = mybir.dt.float32
U16 = mybir.dt.uint16
BF16 = mybir.dt.bfloat16
U32 = mybir.dt.uint32
ALU = mybir.AluOpType
ACT = mybir.ActivationFunctionType
AX = mybir.AxisListType.X

P = 128
D = 1024
KT = D // P
NT = 5
TOK = NT * P
H = 8
EX = 16
CAPS = 64
CAPP = 16
CAP = CAPS + CAPP
HC = 512
MOD = 48
EPS = 1e-6
LEVELS = 7
TAPS = 5
ROWW = 64
NROW = 8
UNITS = [(0, 1), (1, 4), (0, 2), (1, 3), (0, 3), (1, 2), (0, 4), (1, 1), (0, 0), (1, 0)]
SECOND = {(0, 3), (1, 2), (0, 4), (1, 1), (1, 0)}


PER = dict(ada_ev=12, fin_r=5, fin_i=5, ab=1, ada_mm=12, afft=1, aff=1, fin_sq=5, fin_start=1, g1b=4, g1e=4, g2b=4,
           gathered=256, gexp=32, gmm=1, h_chain=32, hidden=32, idx=16, logits=1, moe_used=96, o_ready=32,
           omm=10, scattered=256, selt=1, sel=2, sme=1, sm=1, st_new=4, topk=1, x_moe=5, x_new=10, xs_a=64,
           xs_in=16, xs_turned=16, yt_ev=10, yt=5, y=5, xn=5, xt=10, hta=20, htv=5, sq=5)


def backbone(nc, a):
    ctx = ExitStack()
    sems = {}

    def S(name):
        if name not in sems:
            sems[name] = ctx.enter_context(nc.semaphore(name))
        return sems[name]

    def sb(name, shape, dt=F32):
        return ctx.enter_context(nc.sbuf_tensor(name, shape, dt))

    def bc(ap, shape):
        return ap.broadcast_to(shape)

    def heads(ap, n=P):
        return ap.unsqueeze(2).broadcast_to([ap.shape[0], ap.shape[1], n])

    with ctx:
        PS = ctx.enter_context(nc.psum_tensor("ps", [P, 8, HC], F32))

        x = sb("x", [P, NT, D])
        hT = sb("hT", [P, KT, TOK])
        acc = hT[:, :, :].rearrange("p a b -> p (a b)").rearrange("p (t d) -> p t d", t=NT)
        qkv = sb("qkv", [P, 3 * NT * D])
        qT = qkv[:, 0:NT * D].rearrange("p (k t) -> p k t", k=KT)
        kT = qkv[:, NT * D:2 * NT * D].rearrange("p (k t) -> p k t", k=KT)
        v = qkv[:, 2 * NT * D:3 * NT * D].rearrange("p (t d) -> p t d", t=NT)
        yT = qT
        og = sb("og", [P, NT * D])
        o = og[:, :].rearrange("p (t d) -> p t d", t=NT)
        slots3 = sb("slots3", [P, 3, KT * HC])
        SL = [slots3[:, j, :] for j in range(3)] + [qkv[:, j * KT * HC:(j + 1) * KT * HC] for j in range(3)]
        slot = [s.rearrange("p (k n) -> p k n", k=KT) for s in SL]
        wk = sb("wk", [P, 4608])
        half = [slots3[:, 2, j * HC:(j + 1) * HC] for j in range(8)]
        lmask = sb("lmask", [P, 2 * LEVELS + 3, P], U16)
        identb, NUb, NLb = (lmask[:, 2 * LEVELS + j, :].bitcast(BF16) for j in range(3))
        c32 = sb("c32", [P, 4, P])
        ident, TU, TL, ones = (c32[:, j, :] for j in range(4))
        tri = [TU, TL]
        neg_ts = [NLb, NUb]
        neg_st = [NUb, NLb]
        rows = sb("rows", [P, 3, P])
        vecT = sb("vecT", [P, 264])
        norm_g = vecT[:, 0:32].rearrange("p (k l t) -> p k l t", k=2, l=2)
        biasT = vecT[:, 48:144].rearrange("p (l b) -> p l b", l=2)
        convT = vecT[:, 144:264].rearrange("p (j c) -> p j c", j=TAPS)
        cnd = sb("cnd", [P, 3, 16])
        modT = sb("modT", [P, MOD, 2])
        AB = sb("AB", [P, 2, KT, 2])
        ss = sb("ss", [P, 4, 16])
        epst = sb("epst", [P, 1])
        tick = sb("tick", [1, 1])
        wgt = sb("wgt", [P, KT, 32])
        wrt = sb("wrt", [P, KT, EX])
        gb0 = sb("gb0", [P, 2, 2, H])
        gb1 = sb("gb1", [P, 2, 2, H])
        m0 = sb("m0", [P, 2, H])
        dng = sb("dng", [P, P])
        nst = sb("nst", [P, 2, H])
        ga = sb("ga", [P, 14, NT * 2 * H])
        G3 = [ga[:, j, :].rearrange("p (t d h) -> p t d h", t=NT, d=2) for j in range(14)]
        sm = sb("sm", [P, 2, 4, 4])
        gt = sb("gt", [P, NT, 2, 2, H])
        aff = sb("aff", [P, NT, EX])
        af5 = sb("af5", [P, 2, NT])
        vals = sb("vals", [EX, CAP])
        idx = sb("idx", [EX, CAP], U32)
        idf = sb("idf", [EX, CAP])
        gsel = sb("gsel", [P, EX])
        idT = sb("idT", [P, EX], U32)
        idc = [sb(f"idc{q}", [P, 1], U32) for q in range(2)]
        gsc = [sb(f"gsc{q}", [P, 1]) for q in range(2)]

        xn_d = nc.dram_tensor("xn_d", [TOK, D], F32, kind="Internal").ap()
        moe_d = nc.dram_tensor("moe_d", [TOK, D], F32, kind="Internal").ap()

        xs = [og[:, q * D:(q + 1) * D] for q in range(2)]
        osb = [og[:, (2 + q) * D:(3 + q) * D] for q in range(2)]
        hdT = og[:, 4 * D:4 * D + KT * CAP].rearrange("p (k c) -> p k c", k=KT)
        xsT = [wk[:, q * 640:(q + 1) * 640].rearrange("p (k c) -> p k c", k=KT) for q in range(2)]
        eb = [wk[:, 1280 + q * 320:1600 + q * 320] for q in range(2)]
        affS = wk[0:EX, 2048:2560]
        affP = wk[0:EX, 2560:2688]
        zero = wk[:, 3072:4096]
        grow = wk[:, 3072:4096]
        mrow = [wk[0:2, 2048 + q * HC:2048 + (q + 1) * HC] for q in range(2)]
        Cst = wk[:, 0:2048].rearrange("p (d h v) -> p d h v", d=2, h=H)
        cpad = [wk[:, q * 676:(q + 1) * 676] for q in range(2)]
        cout = [wk[:, 1352 + q * 640:1992 + q * 640] for q in range(2)]
        cex = wk[:, 2632:3272]
        qn = wk[:, 3272:3912].rearrange("p (t c) -> p t c", t=NT)

        def four(ap):
            return ap.rearrange("p (h n) -> p h n", h=4)

        def w_ada(L):
            return a["w_ada"][L].rearrange("(k p) n -> p k n", p=P)

        def w_in(L):
            return a["w_in"][L].rearrange("(k p) n -> p k n", p=P)

        def w_out(L):
            return a["w_out"][L].rearrange("(k p) n -> p k n", p=P)

        def w_expert(L, e, j):
            name, hf = (("w_gate", 0), ("w_up", 0), ("w_gate", 1), ("w_up", 1), ("w_down", 0), ("w_down", 1))[j]
            return a[name][L].rearrange("e (k p) n -> e p k n", p=P)[e, :, :, hf * HC:(hf + 1) * HC]

        NADA, NIN, NOUT = 12, 8, 2
        MIX = NADA + NIN + NOUT

        def mix_slot(n):
            return n % 3 if n < NADA + NIN else n - NADA - NIN

        def mix_landed(L, n):
            j = mix_slot(n)
            return 16 * (sum(mix_slot(k) == j for k in range(n + 1)) + L * (sum(mix_slot(k) == j for k in range(MIX)) + EX))

        def item_end(L, g):
            fm = (4, 6)[L]
            return 4 * (g + 1) if g < fm else 4 * fm + NT * (g + 1 - fm)

        def unit_used(L, n):
            if n < NADA:
                return S("ada_mm"), L * PER["ada_mm"] + n + 1
            if n < NADA + NIN:
                return S(f"pj_mm{L}"), item_end(L, n - NADA)
            return S("omm"), L * PER["omm"] + NT * (n - NADA - NIN + 1)

        def moe_base(L, j):
            return ((L + 1) * sum(mix_slot(k) == j for k in range(MIX)) if j < 3 else 0) + L * EX

        BETA, GC, NG, EG, EGL, EKD, NBETA, NEG = (G3[j] for j in range(4, 12))

        def delta_buffers(u, p):
            chunks = [four(slots3[:, j // 8, j % 8 * HC:(j % 8 + 1) * HC]) for j in range(24)]
            w = chunks[10 * (u % 2) + 5 * p:][:5]
            xb = wk[:, 4096 + 256 * p:4096 + 256 * (p + 1)].rearrange("p (h n) -> p h n", h=4)
            return dict(E=w[0], CM=(w[0], chunks[22 + p]), AT=w[1], qk=w[2], kd=w[3], DT=w[4], D=chunks[20 + p], X=xb)

        Rb, Wb, tb = (four(wk[:, 2048 + j * HC:2048 + (j + 1) * HC]) for j in range(3))

        def at_all(u, l, p):
            return (u * LEVELS + l) * 2 + p + 1

        def at_early(u, l, p):
            return (u * (LEVELS - 1) + l) * 2 + p + 1

        def at_late(u, l, p):
            return (u * (LEVELS - 1) + l - 1) * 2 + p + 1

        def at_mid(u, l, p):
            return (u * (LEVELS - 2) + l - 1) * 2 + p + 1

        def parts(d):
            return (slice(0, 64), slice(64, P)) if d == 0 else (slice(64, P), slice(0, 64))

        fsq = slots3[:, 2, 0:1024]
        g1b = slots3[:, 2, 2048:4096].rearrange("p (c j n) -> p c j n", c=2, j=2)
        ytmp = wk[:, 2560:2560 + HC]
        cjunk = wk[:, 3912:4040]
        gtmp = [wk[:, 2632 + 640 * q:2632 + 640 * q + HC] for q in range(2)]

        def cols(ap, l, which):
            return ap.rearrange("p h (b w s) -> p h b w s", w=2, s=2 ** l)[:, :, :, which, :]

        def cols1(ap, l, which):
            return ap.rearrange("p (b w s) -> p b w s", w=2, s=2 ** l)[:, :, which, :]

        def pack(ap, l):
            return ap.rearrange("p h (b s) -> p h b s", s=2 ** l)

        land = [S(f"landed{j}") for j in range(6)]
        block = ctx.enter_context(nc.Block())

        @block.sync
        def _(sp):
            with nc.allow_non_contiguous_dma(reason="small vectors"):
                loads = [
                    (c32[:, :, :], a["c32"]), (lmask[:, :, :], a["lmask"]),
                    (rows[0:16, 0, :], a["norm1_g"].rearrange("l (t p) -> (l t) p", p=P)),
                    (rows[16:32, 0, :], a["norm2_g"].rearrange("l (t p) -> (l t) p", p=P)),
                    (rows[32:40, 0, :], a["c_ctx"].rearrange("(t p) -> t p", p=P)),
                    (rows[40:48, 0, :], a["c"].rearrange("b (t p) -> (b t) p", p=P)),
                    (rows[0:96, 1, :], a["b_ada"].rearrange("l (t p) -> (l t) p", p=P)),
                    (rows[0:120, 2, :], a["delta_conv_w"][0].rearrange("j (t p) -> (j t) p", p=P)),
                    (gb0[:, :, 0, :], a["mlstm_ig_b"][0].partition_broadcast(P)),
                    (gb0[:, :, 1, :], a["mlstm_fg_b"][0].partition_broadcast(P)),
                    (gb1[:, :, 0, :], a["delta_A_log"][0].partition_broadcast(P)),
                    (gb1[:, :, 1, :], a["delta_dt_bias"][0].partition_broadcast(P)),
                    (m0[:, :, :], a["state_mlstm_m"][0, 0].partition_broadcast(P)),
                    (dng[:, :], a["delta_norm_g"][0].partition_broadcast(P)),
                ]
                for dst, src in loads:
                    sp.dma_start(dst, src).then_inc(S("setup"), 16)

            sp.dma_start(x[:, 0, :], a["x_prompt"][0]).then_inc(S("x_in"), 16)
            sp.dma_start(x[:, 1:5, :], a["x_sample"][0].rearrange("(t p) d -> p t d", p=P)).then_inc(S("x_in"), 16)

            for L in range(2):
                for n in range(NADA + NIN):
                    j = mix_slot(n)
                    if n < 3:
                        if L:
                            sp.wait_ge(S("moe_used"), 6 * (EX - 1) + j + 1)
                    else:
                        sp.wait_ge(*unit_used(L, n - 3))
                    if n < NADA:
                        src = w_ada(L)[:, :, n * HC:(n + 1) * HC]
                    else:
                        g = n - NADA
                        src = w_in(L)[:, :, g * HC:(g + 1) * HC]
                    sp.dma_start(slot[j], src).then_inc(land[j], 16)
                    if n == 2:
                        if L == 1:
                            sp.wait_ge(S("gmm"), 1)
                        sp.dma_start(wgt[:, :, :], w_in(L)[:, :, 4 * D:4 * D + 32]).then_inc(S("wg_in"), 16)
                        if L == 1:
                            sp.wait_ge(S("logits"), 1)
                        sp.dma_start(wrt[:, :, :], a["w_router"][L].rearrange("(k p) e -> p k e", p=P)).then_inc(S("wr_in"), 16)
                st = a["state_mlstm_C" if L == 0 else "state_delta_S"][0, 0]
                if L == 1:
                    sp.wait_ge(S("tr1"), 24)
                for d in range(2):
                    sp.dma_start(Cst[:, d, :, :], st[d].rearrange("h k v -> k h v")).then_inc(S("st_in"), 16)
                if L == 0:
                    with nc.allow_non_contiguous_dma(reason="normaliser state, 2048 numbers"):
                        for d in range(2):
                            sp.dma_start(nst[:, d, :], a["state_mlstm_n"][0, 0, d].rearrange("h k -> k h")).then_inc(S("st_in"), 16)
                    sp.dma_start(grow, a["mlstm_norm_g"][0].partition_broadcast(P)).then_inc(S("grow_in"), 16)
                sp.wait_ge(S("st_new"), L * PER["st_new"] + 4)
                out = a["out_C" if L == 0 else "out_S"][0, 0]
                for d in range(2):
                    sp.dma_start(out[d].rearrange("h k v -> k h v"), Cst[:, d, :, :]).then_inc(S("st_out"), 16)
                if L == 0:
                    with nc.allow_non_contiguous_dma(reason="normaliser state, 2048 numbers"):
                        for d in range(2):
                            sp.dma_start(a["out_n"][0, 0, d].rearrange("h k -> k h"), nst[:, d, :]).then_inc(S("st_out"), 16)
                    sp.dma_start(a["out_m"][0], G3[13][0:1, 0, :, :]).then_inc(S("st_out"), 16)

                sp.wait_ge(S("fin_start"), L + 1)
                for j in range(NOUT):
                    sp.dma_start(slot[j], w_out(L)[:, :, j * HC:(j + 1) * HC]).then_inc(land[j], 16)

                for t in range(NT):
                    sp.wait_ge(S("xn"), (2 * L + 1) * PER["xn"] + t + 1)
                    sp.dma_start(xn_d[t * P:(t + 1) * P, :], o[:, t, :]).then_inc(S("xn_out"), 16)
                def expert_loads(e, first):
                    for j in range(6) if first else (1, 3, 5):
                        if not first:
                            sp.wait_ge(S("moe_used"), L * PER["moe_used"] + e * 6 + (j - 5))
                        sp.dma_start(slot[j], w_expert(L, e, j)).then_inc(land[j], 16)

                sp.wait_ge(*unit_used(L, MIX - 1))
                sp.wait_ge(S("x_new"), L * PER["x_new"] + 10)
                expert_loads(0, True)
                with sp.Fori(1, EX) as e:
                    expert_loads(e, False)
                sp.wait_ge(S("scattered"), L * PER["scattered"] + 16 * EX)
                for t in range(NT):
                    sp.dma_start(o[:, t, :], moe_d[t * P:(t + 1) * P, :]).then_inc(S("moe_in"), 16)
            sp.dma_start(grow, a["final_g"].partition_broadcast(P)).then_inc(S("grow_in"), 16)
            for t in range(NT):
                sp.wait_ge(S("y_ready"), t + 1)
                dst = a["out_p"][0] if t == 0 else a["out_s"][0, (t - 1) * P:t * P, :]
                sp.dma_start(dst, o[:, t, :]).then_inc(S("y_out"), 16)
            sp.wait_ge(S("y_out"), 16 * NT)
            sp.wait_ge(S("st_out"), 16 * 7)

        @block.gpsimd
        def _(pool):
            pool.memset(epst[:, :], EPS).then_inc(S("epst"), 1)

            for L in range(2):
                if L == 1:
                    pool.wait_ge(S("moe_in"), 16 * NT)
                pool.wait_ge(S("x_new"), L * PER["x_new"] + 10)
                pool.wait_ge(S("st_out"), 16 * (5 if L == 0 else 7))
                pool.memset(zero, 0.0).then_inc(S("zeroed"), 1)
                pool.wait_ge(S("zeroed"), L + 1)
                for t in range(NT):
                    pool.dma_start(moe_d[t * P:(t + 1) * P, :], zero).then_inc(S("zero_out"), 16)

                def hold(before):
                    if not (isinstance(before, int) and before == 0):
                        pool.wait_ge(S("held"), before)
                    pool.tensor_tensor(tick[:, 0:1], epst[0:1, :], epst[0:1, :], ALU.mult).then_inc(S("held"), 1)

                def gather(e, q, first):
                    pool.wait_ge(S("idx"), L * PER["idx"] + e + 1)
                    if not first:
                        pool.wait_ge(S("xs_turned"), L * PER["xs_turned"] + e - 1)
                    hold(2 * EX * L + e if first else e * 2 + (2 * EX * L - 1))
                    pool.indirect_dma_start(xs[q][0:CAP, :], None, xn_d,
                                            bass.IndirectOffsetOnAxis(ap=idc[q][0:CAP, :], axis=0)).then_inc(S("gathered"), 16)

                def scatter(e, q, first):
                    pool.wait_ge(S("o_ready"), L * PER["o_ready"] + e * 2 + 2)
                    if not first:
                        pool.wait_ge(S("scattered"), L * PER["scattered"] + e * 16)
                    hold(2 * EX * L + (2 * EX - 1) if e is EX - 1 else e * 2 + (2 * EX * L + 2))
                    pool.indirect_dma_start(moe_d, bass.IndirectOffsetOnAxis(ap=idc[q][0:CAP, :], axis=0),
                                            osb[q][0:CAP, :], None, compute_op=ALU.add).then_inc(S("scattered"), 16)

                pool.wait_ge(S("xn_out"), 16 * NT * (L + 1))
                pool.wait_ge(S("zero_out"), 16 * NT * (L + 1))
                gather(0, 0, True)
                gather(1, 1, True)
                scatter(0, 0, True)
                gather(2, 0, False)
                scatter(1, 1, False)
                with pool.Fori(1, EX // 2 - 1) as i:
                    for q in range(2):
                        gather(i * 2 + (q + 1), 1 - q, False)
                        scatter(i * 2 + q, q, False)
                gather(EX - 1, 1, False)
                scatter(EX - 2, 0, False)
                scatter(EX - 1, 1, False)
                pool.wait_ge(S("scattered"), L * PER["scattered"] + 16 * EX)

        @block.scalar
        def _(act):
            A = nc.scalar.activation

            chain = [0]

            def link(ins):
                chain[0] += 1
                ins.then_inc(S("act_chain"), 1)
                act.wait_ge(S("act_chain"), chain[0])

            def inverse_root(dst, src, scale):
                link(A(dst, src, ACT.Ln, scale=scale, bias=epst[:, 0:1]))
                return A(dst, dst, ACT.Exp, scale=-0.5)

            act.wait_ge(S("vec"), 1)
            act.wait_ge(S("epst"), 1)
            A(cnd[:, 0, :], vecT[:, 32:48], ACT.Exp, scale=-1.0).then_inc(S("cexp"), 1)

            def norm(i):
                for t in range(NT):
                    norm_tile(i, t)

            def norm_tile(i, t):
                act.wait_ge(S("x_in"), 32) if i == 0 else act.wait_ge(*x_ready(i, t))
                link(A(o[:, t, :], x[:, t, :], ACT.Square, accum_out=ss[:, 0, t:t + 1]))
                inverse_root(ss[:, 1, t:t + 1], ss[:, 0, t:t + 1], 1.0 / D).then_inc(S("sq"), 1)

            def x_ready(i, t):
                if i in (1, 3):
                    return S("x_new"), PER["x_new"] * (i // 2) + 2 * (t + 1)
                return S("x_moe"), PER["x_moe"] * (i // 2 - 1) + t + 1

            def norm_evac(L, k):
                for t in range(NT):
                    evac_tile(L, k, t)

            def evac_tile(L, k, t):
                act.wait_ge(S("xt"), (2 * L + k) * PER["xt"] + 2 * t + 1)
                if t == 0:
                    act.wait_ge(S("ab"), L * PER["ab"] + 1)
                c = int(t > 0)
                for kt in range(4):
                    A(hT[:, kt, t * P:(t + 1) * P], PS[:, 2 * (t % 2) + 2, kt * P:(kt + 1) * P], ACT.Identity,
                      scale=AB[:, k, kt, c:c + 1], bias=modT[:, 24 * k + kt, c:c + 1]).then_inc(S("hta"), 1)

            def proj(L):
                if L == 0:
                    for i in range(36):
                        act.wait_ge(S("pj_mm0"), i + 1)
                        b = 2 * (i % 3)
                        if i < 16:
                            dst = (qT if i < 8 else kT)[:, i % 8, :]
                            sc = 1.0 if i < 8 else float(P) ** -0.5
                            A(dst[:, P:TOK], PS[:, b, :], ACT.Copy, scale=sc)
                            A(dst[:, 0:P], PS[:, b + 1, 0:P], ACT.Copy, scale=sc).then_inc(S("pj_ev0"), 1)
                        else:
                            g, t = divmod(i - 16, NT)
                            if g == 2 and t == 0:
                                gates_mlstm2()
                            dst = (v if g < 2 else o)[:, t, (g % 2) * HC:(g % 2 + 1) * HC]
                            if g < 2:
                                A(dst, PS[:, b, :], ACT.Copy).then_inc(S("pj_ev0"), 1)
                            else:
                                A(dst, PS[:, b, :], ACT.Tanh, scale=0.5).then_inc(S("pj_ev0"), 1)
                    return

                def evac(i):
                    act.wait_ge(S("pj_mm1"), i + 1)
                    b = 2 * (i % 2)
                    if i < 24:
                        if i == 0:
                            act.wait_ge(S("padded"), 2)
                        if i >= 2:
                            act.wait_ge(S("cv_done"), i - 1)
                        A(cpad[i % 2][:, 132:676].rearrange("p (r w) -> p r w", r=NROW)[:, :, 2:2 + ROWW],
                          PS[:, b, :].rearrange("p (r w) -> p r w", r=NROW), ACT.Copy)
                        A(cpad[i % 2][:, 2:130], PS[:, b + 1, 0:P], ACT.Copy).then_inc(S("pj_ev1"), 1)
                    else:
                        g, t = divmod(i - 24, NT)
                        A(o[:, t, g * HC:(g + 1) * HC], PS[:, b, :], ACT.Copy)
                        if i == 24:
                            act.wait_ge(S("silu"), 24)
                            act.wait_ge(S("tr2"), 16)
                        elif i >= 26:
                            act.wait_ge(S("og"), 10 + i - 25)
                        A(gtmp[i % 2], PS[:, b, :], ACT.Tanh, scale=0.5).then_inc(S("pj_ev1"), 1)

                def squares(i):
                    act.wait_ge(S("tr1"), i + 1)
                    if i >= 16:
                        c = (i - 16) * P
                        A(v[:, 0:4, c:c + P], four(PS[:, 4, :]), ACT.Copy)
                        A(v[:, 4, c:c + P], PS[:, 5, 0:P], ACT.Copy).then_inc(S("tr1_ev"), 1)
                    else:
                        if i >= 1:
                            act.wait_ge(S("qn"), i)
                        for t in range(NT):
                            src = PS[:, 4, t * P:(t + 1) * P] if t < 4 else PS[:, 5, 0:P]
                            ins = A(cjunk, src, ACT.Square, accum_out=ss[:, 0, t:t + 1])
                            link(ins)
                        inverse_root(ss[:, 1, 0:NT], ss[:, 0, 0:NT], 1.0).then_inc(S("sqj"), 1)

                def back(i):
                    act.wait_ge(S("tr2"), i + 1)
                    dst = (qT if i < 8 else kT)[:, i % 8, :]
                    A(dst[:, 0:4 * P], PS[:, 6, :], ACT.Copy)
                    A(dst[:, 4 * P:TOK], PS[:, 7, 0:P], ACT.Copy).then_inc(S("tr2_ev"), 1)

                for i in range(26):
                    if i < 24:
                        evac(i)
                    if 2 <= i and i - 2 < 16:
                        back(i - 2)
                    if 1 <= i <= 24:
                        squares(i - 1)
                    if i < 24:
                        act.wait_ge(S("cv_done"), i + 1)
                        if i:
                            act.wait_ge(S("silu"), i)
                        A(cex, cout[i % 2], ACT.Tanh).then_inc(S("cvexp"), 1)
                for i in range(24, 34):
                    evac(i)

            def gates(L):
                if L == 0:
                    act.wait_ge(S("g0"), 1)
                    A(ga[:, 1, :], ga[:, 0, :], ACT.Exp, scale=-1.0).then_inc(S("g0a"), 1)
                    act.wait_ge(S("g0a"), 1)
                    A(ga[:, 1, :], ga[:, 1, :], ACT.Ln, bias=1.0).then_inc(S("g0a"), 1)
                    return
                act.wait_ge(S("g1"), 1)
                A(ga[:, 1, :], ga[:, 0, :], ACT.Exp, scale=-1.0).then_inc(S("g1a"), 1)
                act.wait_ge(S("g1a"), 1)
                A(ga[:, 1, :], ga[:, 1, :], ACT.Ln, bias=1.0).then_inc(S("g1a"), 1)
                A(ga[:, 4, :], ga[:, 4, :], ACT.Exp, scale=-1.0).then_inc(S("g1a"), 1)
                A(gb1[:, :, 0, :], gb1[:, :, 0, :], ACT.Exp).then_inc(S("g1a"), 1)

            def gates_mlstm2():
                act.wait_ge(S("g0"), 2)
                for j in (9, 10, 11, 12):
                    A(ga[:, j, :], ga[:, j, :], ACT.Exp).then_inc(S("g0a"), 1)

            def gates_delta2():
                act.wait_ge(S("g1"), 2)
                for j in (7, 8, 9):
                    A(ga[:, j, :], ga[:, j, :], ACT.Exp).then_inc(S("g1a"), 1)

            def mlstm():
                for n in range(20):
                    d, t = UNITS[n // 2]
                    p = n % 2
                    act.wait_ge(S("ml_bc"), n + 1)
                    if n >= 2:
                        act.wait_ge(S("ml_ps"), n - 1)
                    for h in range(4):
                        A(four(half[4 * p])[:, h, :], PS[:, n % 2, h * P:(h + 1) * P], ACT.Exp,
                          bias=G3[3][:, t, d, 4 * p + h:4 * p + h + 1]).then_inc(S("ml_e"), 1)

            def delta():
                def decay(u, p):
                    d, t = UNITS[u]
                    n = 2 * u + p
                    act.wait_ge(S("dl_bc"), n + 1)
                    if u >= 2:
                        act.wait_ge(S("dl_x"), at_all(u - 2, LEVELS - 1, p))
                    for h in range(4):
                        A(delta_buffers(u, p)["E"][:, h, :], PS[:, 4, h * P:(h + 1) * P], ACT.Exp,
                          bias=NG[:, t, d, 4 * p + h:4 * p + h + 1]).then_inc(S("dl_e"), 1)

                def inter(u, p):
                    d, t = UNITS[u]
                    n = 2 * u + p
                    act.wait_ge(S("dl_qs"), n + 1)
                    if n:
                        act.wait_ge(S("dl_done"), n)
                    for h in range(4):
                        A(tb[:, h, :], PS[:, 7, h * P:(h + 1) * P], ACT.Copy,
                          scale=EG[:, t, d, 4 * p + h:4 * p + h + 1]).then_inc(S("dl_t"), 1)

                def solved(u, p):
                    n = 2 * u + p
                    act.wait_ge(S("dl_w"), n + 1)
                    if n:
                        act.wait_ge(S("dl_o"), n)
                    A(Wb, four(PS[:, 6, :]), ACT.Copy).then_inc(S("dl_we"), 1)

                def fill(u, l):
                    if u and l in (0, 3):
                        inter(u - 1, l // 3)
                    if l in (1, 4):
                        if u:
                            solved(u - 1, l // 3)
                        if u + 1 < len(UNITS):
                            decay(u + 1, l // 3)

                for p in range(2):
                    decay(0, p)
                for u, (d, t) in enumerate(UNITS):
                    off = 1 - d
                    first, then = parts(d)
                    for l in range(LEVELS):
                        for p in range(2):
                            DT = delta_buffers(u, p)["DT"]
                            if l == 0:
                                act.wait_ge(S("dl_tr"), at_early(u, l, p))
                                if u >= 2:
                                    act.wait_ge(S("dl_w"), 2 * (u - 2) + p + 1)
                                ins = A(DT, four(PS[:, 2 * p + 1, :]), ACT.Copy)
                            elif l < LEVELS - 1:
                                act.wait_ge(S("dl_tr"), at_early(u, l, p))
                                ins = A(cols(DT, l, off), cols(four(PS[:, 2 * p + 1 - l % 2, :]), l, off), ACT.Copy)
                            else:
                                act.wait_ge(S("dl_dx"), at_late(u, l, p))
                                ins = A(DT[first, :, then], four(PS[first, 2 * p, :])[:, :, 0:64], ACT.Copy, scale=-1.0)
                            ins.then_inc(S("dl_dt"), 1)
                        fill(u, l)
                for l in range(LEVELS):
                    fill(len(UNITS), l)

            def gate_tile(L, t):
                act.wait_ge(S("fin_start"), L * PER["fin_start"] + 1)
                A(fsq, acc[:, t, :], ACT.Square).then_inc(S("fin_sq"), 1)
                act.wait_ge(S("fin_r"), L * PER["fin_r"] + t + 1)
                inverse_root(ss[:, 1, 8:16], ss[:, 0, 8:16], 1.0 / P).then_inc(S("fin_i"), 1)

            def yt_copy(L, t):
                act.wait_ge(S("yt"), L * PER["yt"] + t + 1)
                for j in range(2):
                    A(yT[:, 4 * j:4 * j + 4, t * P:(t + 1) * P], four(PS[:, j, :]), ACT.Copy).then_inc(S("yt_ev"), 1)

            def mixer_tail(L):
                i = 2 * L + 1
                gate_tile(L, 0)
                gate_tile(L, 1)
                yt_copy(L, 0)
                for c in range(2):
                    for j in range(2):
                        act.wait_ge(S("g1b"), L * PER["g1b"] + 2 * c + j + 1)
                        A(g1b[:, c, j, :], PS[:, 2 + 2 * c + j, :], ACT.Copy).then_inc(S("g1e"), 1)
                for t in range(2, NT):
                    gate_tile(L, t)
                    yt_copy(L, t - 1)
                yt_copy(L, NT - 1)
                for t in range(NT - 1):
                    norm_tile(i, t)
                evac_tile(L, 1, 0)
                evac_tile(L, 1, 1)
                norm_tile(i, NT - 1)
                for t in range(2, NT):
                    evac_tile(L, 1, t)

            def experts(L):
                act.wait_ge(S("sm"), L * PER["sm"] + 1)
                A(aff[:, :, :], aff[:, :, :], ACT.Exp).then_inc(S("sme"), 1)

                def expert(e, q, first, last=False):
                    def load(j):
                        if not last:
                            act.dma_start(slot[j], w_expert(L, e + 1, j)).then_inc(land[j], 16)

                    for hf in range(2):
                        act.wait_ge(S("moe_used"), L * PER["moe_used"] + e * 6 + (2 * hf + 1))
                        if first != 0:
                            act.wait_ge(S("hidden"), L * PER["hidden"] + e * 2 + (hf - 1))
                        A(eb[hf], PS[:, 2 * hf, 0:320], ACT.Tanh, scale=0.5).then_inc(S("gexp"), 1)
                        load(2 * hf)
                    for hf in range(2):
                        act.wait_ge(S("moe_used"), L * PER["moe_used"] + e * 6 + (5 + hf))
                        if hf == 0 and first is None:
                            act.wait_ge(S("scattered"), L * PER["scattered"] + (e - 1) * 16)
                        A(osb[q][0:CAP, hf * HC:(hf + 1) * HC], PS[0:CAP, 4 + hf, :], ACT.Copy,
                          scale=gsc[q][0:CAP, :]).then_inc(S("o_ready"), 1)
                        if hf == 0:
                            load(4)

                expert(0, 0, 0)
                expert(1, 1, 1)
                with act.Fori(1, EX // 2 - 1) as i:
                    for q in range(2):
                        expert(i * 2 + q, q, None)
                expert(EX - 2, 0, None)
                expert(EX - 1, 1, None, last=True)

            def modulation(L):
                for n in range(NADA):
                    act.wait_ge(S("ada_mm"), L * PER["ada_mm"] + n + 1)
                    if n >= 2:
                        act.wait_ge(S("ada_tr"), L * NADA + n - 1)
                    A(mrow[n % 2], PS[0:2, n % 2, :], ACT.Copy).then_inc(S("ada_ev"), 1)

            for L in range(2):
                norm(2 * L)
                modulation(L)
                norm_evac(L, 0)
                if L == 0:
                    gates(0)
                    proj(0)
                    mlstm()
                else:
                    gates(1)
                    proj(1)
                    gates_delta2()
                    act.wait_ge(S("og"), 20)
                    delta()
                mixer_tail(L)
                experts(L)
            norm(4)

        @block.tensor
        def _(pe):
            mm = nc.tensor.matmul
            tr = nc.tensor.transpose

            pe.wait_ge(S("setup"), 16 * 14)
            tr(PS[:, 0, 0:48], rows[0:48, 0, :], ident[0:48, 0:48])
            tr(PS[:, 0, 48:144], rows[0:96, 1, :], ident[0:96, 0:96])
            tr(PS[:, 0, 144:264], rows[0:120, 2, :], ident[0:120, 0:120]).then_inc(S("vect"), 1)

            def modulation(L):
                def turn(n):
                    pe.wait_ge(S("ada_ev"), L * PER["ada_ev"] + n + 1)
                    for b in range(4):
                        blk = n * 4 + b
                        ins = tr(PS[:, 6, 2 * blk:2 * blk + 2], mrow[n % 2][:, b * P:(b + 1) * P], ident[0:2, 0:2])
                    ins.then_inc(S("ada_tr"), 1)

                pe.wait_ge(S("cond"), 1)
                if L:
                    pe.wait_ge(S("x_moe"), NT)
                for n in range(NADA):
                    j = mix_slot(n)
                    pe.wait_ge(land[j], mix_landed(L, n))
                    if n >= 2:
                        pe.wait_ge(S("ada_ev"), L * PER["ada_ev"] + n - 1)
                    for kt in range(KT):
                        ins = mm(PS[0:2, n % 2, :], cnd[:, 1, kt:16:8], slot[j][:, kt, :],
                                 start=(kt == 0), stop=(kt == KT - 1))
                    ins.then_inc(S("ada_mm"), 1)
                    if n:
                        turn(n - 1)
                turn(NADA - 1)

            def turn_tile(L, k, t):
                pe.wait_ge(S("xn"), (2 * L + k) * PER["xn"] + t + 1)
                if t >= 2:
                    turned(L, k, t - 2)
                for j in range(2):
                    for kt in range(4):
                        c = (4 * j + kt) * P
                        ins = tr(PS[:, 2 * (t % 2) + 2 + j, kt * P:(kt + 1) * P], o[:, t, c:c + P], ident)
                    ins.then_inc(S("xt"), 1)

            def turned(L, k, t):
                pe.wait_ge(S("hta"), (2 * L + k) * PER["hta"] + 4 * (t + 1))
                pe.wait_ge(S("htv"), (2 * L + k) * PER["htv"] + t + 1)

            def norm_turn(L, k):
                for t in range(NT):
                    turn_tile(L, k, t)
                turned(L, k, NT - 1)

            def gates(L):
                pe.wait_ge(S("wg_in"), 16 * (L + 1))
                for t in range(NT):
                    for kt in range(KT):
                        ins = mm(PS[:, 7, t * 32:(t + 1) * 32], hT[:, kt, t * P:(t + 1) * P], wgt[:, kt, :],
                                 start=(kt == 0), stop=(kt == KT - 1))
                ins.then_inc(S("gmm"), 1)

            def feature_major(L, i, sl, cb):
                n = 3 - L
                b = 2 * (i % n)
                if i >= n:
                    pe.wait_ge(S(f"pj_ev{L}"), i - n + 1)
                for kt in range(KT):
                    w = slot[sl][:, kt, cb * P:(cb + 1) * P]
                    mm(PS[:, b, :], w, hT[:, kt, P:TOK], start=(kt == 0), stop=(kt == KT - 1))
                    ins = mm(PS[:, b + 1, 0:P], w, hT[:, kt, 0:P], start=(kt == 0), stop=(kt == KT - 1))
                return ins.then_inc(S(f"pj_mm{L}"), 1)

            def token_major(L, i, sl, t):
                n = 3 - L
                if i >= n:
                    pe.wait_ge(S(f"pj_ev{L}"), i - n + 1)
                for kt in range(KT):
                    ins = mm(PS[:, 2 * (i % n), :], hT[:, kt, t * P:(t + 1) * P], slot[sl][:, kt, :],
                             start=(kt == 0), stop=(kt == KT - 1))
                return ins.then_inc(S(f"pj_mm{L}"), 1)

            def unit(L, g):
                n = NADA + g
                pe.wait_ge(land[mix_slot(n)], mix_landed(L, n))
                return mix_slot(n)

            def proj_mlstm():
                i = 0
                for g in range(8):
                    sl = unit(0, g)
                    for k in range(4 if g < 4 else NT):
                        feature_major(0, i, sl, k) if g < 4 else token_major(0, i, sl, k)
                        gates(0) if i == 0 else stab_mlstm(i - 1)
                        i += 1
                pe.wait_ge(S("pj_ev0"), 36)

            def proj_delta():
                def turn1(i):
                    pe.wait_ge(S("silu"), i + 1)
                    if i >= 17:
                        pe.wait_ge(S("tr1_ev"), i - 16)
                    elif i:
                        pe.wait_ge(S("qn"), i)
                    for t in range(NT):
                        dst = PS[:, 4, t * P:(t + 1) * P] if t < 4 else PS[:, 5, 0:P]
                        ins = tr(dst, cout[i % 2][:, t * P:(t + 1) * P], ident)
                    ins.then_inc(S("tr1"), 1)

                def turn2(i):
                    pe.wait_ge(S("qn"), i + 1)
                    if i == 0:
                        pe.wait_ge(S("gev1"), 4)
                    else:
                        pe.wait_ge(S("tr2_ev"), i)
                    for t in range(NT):
                        dst = PS[:, 6, t * P:(t + 1) * P] if t < 4 else PS[:, 7, 0:P]
                        ins = tr(dst, qn[:, t, :], ident)
                    ins.then_inc(S("tr2"), 1)

                for i in range(26):
                    if i < 24:
                        g, k = divmod(i, 4)
                        if k == 0:
                            sl = unit(1, g)
                        feature_major(1, i, sl, k)
                    if i == 0:
                        gates(1)
                    if 2 <= i and i - 2 < 16:
                        turn2(i - 2)
                    if 1 <= i <= 24:
                        turn1(i - 1)
                i = 24
                for g in range(6, 8):
                    sl = unit(1, g)
                    for t in range(NT):
                        token_major(1, i, sl, t)
                        i += 1
                pe.wait_ge(S("tr1_ev"), 8)
                pe.wait_ge(S("tr2_ev"), 16)
                pe.wait_ge(S("pj_ev1"), 34)

            def masked(bank, mask, src, neg=None):
                for h in range(4):
                    mm(PS[:, bank, h * P:(h + 1) * P], src[:, h:h + 1].broadcast_to([P, P]), ident,
                       start=(h == 0), stop=False, skip_group_check=True)
                return mm(PS[:, bank, :], identb, mask.unsqueeze(1).broadcast_to([P, 4, P]), start=False, stop=True,
                          skip_group_check=True)

            def sums(L, src, sem_in, sem_out):
                pe.wait_ge(*sem_in)
                for d in range(2):
                    mm(PS[:, 7, 40 * d:40 * d + 40].rearrange("p (t h) -> p t h", t=NT), tri[d], src[:, :, d, :], start=True, stop=True)
                mm(PS[:, 7, 80:160], ones, src[:, :, :, :].rearrange("p t d h -> p (t d h)"), start=True, stop=True).then_inc(sem_out, 1)

            def stab_mlstm(i):
                if i == 0:
                    sums(0, G3[2], (S("lf"), 1), S("bsum"))
                elif i <= 20:
                    n = i - 1
                    d, t = UNITS[n // 2]
                    p = n % 2
                    if n == 0:
                        pe.wait_ge(S("aready"), 1)
                    else:
                        pe.wait_ge(S("mxr"), n)
                    masked(6, neg_ts[d], G3[3][:, t, d, 4 * p:4 * p + 4]).then_inc(S("amm"), 1)
                elif i == 21:
                    pe.wait_ge(S("mxr"), 20)
                    for d in range(2):
                        last = ident[:, 127:128] if d == 0 else ident[:, 0:1]
                        ins = mm(PS[:, 7, 40 * d:40 * d + 40].rearrange("p (t h) -> p t h", t=NT), last.broadcast_to([P, P]),
                                 G3[6][:, :, d, :], start=True, stop=True)
                    ins.then_inc(S("mlast"), 1)

            def scan_mlstm():
                def exponents(n):
                    d, t = UNITS[n // 2]
                    p = n % 2
                    if n == 0:
                        pe.wait_ge(S("nm"), 1)
                    if n >= 2:
                        pe.wait_ge(S("ml_e"), 4 * n - 4)
                    masked(n % 2, neg_st[d], G3[8][:, t, d, 4 * p:4 * p + 4]).then_inc(S("ml_bc"), 1)

                def scores(n):
                    d, t = UNITS[n // 2]
                    p = n % 2
                    ts = slice(t * P, (t + 1) * P)
                    if n:
                        pe.wait_ge(S("ml_ps"), n)
                    for h in range(4):
                        tr(PS[:, 3, h * P:(h + 1) * P], kT[:, 4 * p + h, ts], ident)
                    for h in range(4):
                        ins = mm(PS[:, 2, h * P:(h + 1) * P], kT[:, 4 * p + h, ts], qT[:, 4 * p + h, ts], start=True, stop=True)
                    ins.then_inc(S("ml_s"), 1)

                def back(n):
                    d, t = UNITS[n // 2]
                    p = n % 2
                    ts = slice(t * P, (t + 1) * P)
                    E, PSb, kw = (four(half[4 * p + j]) for j in range(3))
                    b7 = PS[:, 7, 16 * p:16 * p + 12]
                    pe.wait_ge(S("ml_ps"), n + 1)
                    if n == 0:
                        pe.wait_ge(S("st_in"), 64)
                    if n:
                        pe.wait_ge(S("ml_c"), n)
                    for h in range(4):
                        hh = 4 * p + h
                        mm(PS[:, 4, h * P:(h + 1) * P], kw[:, h, :], v[:, t, hh * P:(hh + 1) * P], start=True, stop=True)
                        ins = mm(b7[:, 8 + h:9 + h], kw[:, h, :], ones[:, 0:1], start=True, stop=True)
                    for h in range(4):
                        mm(b7[:, h:h + 1], PSb[:, h, :], ones[:, 0:1], start=True, stop=True)
                    if n >= 16:
                        pe.wait_ge(S("ml_cz"), n - 15)
                    for h in range(4):
                        ins = mm(b7[:, 4 + h:5 + h], qT[:, 4 * p + h, ts], nst[:, d, 4 * p + h:4 * p + h + 1], start=True, stop=True)
                    ins.then_inc(S("ml_sum"), 1)
                    if n:
                        pe.wait_ge(S("ml_done"), n)
                    for h in range(4):
                        ins = mm(PS[:, 5, h * P:(h + 1) * P], qT[:, 4 * p + h, ts], Cst[:, d, 4 * p + h, :], start=True, stop=True)
                    ins.then_inc(S("ml_qc"), 1)
                    for h in range(4):
                        hh = 4 * p + h
                        ins = mm(PS[:, 6, h * P:(h + 1) * P], PSb[:, h, :], v[:, t, hh * P:(hh + 1) * P], start=True, stop=True)
                    ins.then_inc(S("ml_bk"), 1)

                exponents(0)
                exponents(1)
                scores(0)
                for n in range(20):
                    if n + 1 < 20:
                        scores(n + 1)
                    if n + 2 < 20:
                        exponents(n + 2)
                    back(n)

            def scan_delta():
                sums(1, G3[3], (S("gl"), 1), S("gsum"))
                pe.wait_ge(S("gready"), 1)

                def hb(bank, h, n=P):
                    return PS[:, bank, h * P:h * P + n]

                def front(u, p):
                    d, t = UNITS[u]
                    n = 2 * u + p
                    if n:
                        pe.wait_ge(S("dl_kd"), n)
                    masked(4, neg_st[d], GC[:, t, d, 4 * p:4 * p + 4]).then_inc(S("dl_bc"), 1)
                    for h in range(4):
                        kk = kT[:, 4 * p + h, t * P:(t + 1) * P]
                        ins = mm(hb(5, h), kk, kk, start=True, stop=True)
                    ins.then_inc(S("dl_kk"), 1)

                def keys(u, p):
                    d, t = UNITS[u]
                    ts = slice(t * P, (t + 1) * P)
                    n = 2 * u + p
                    pe.wait_ge(S("dl_at"), n + 1)
                    for h in range(4):
                        tr(hb(4, h), kT[:, 4 * p + h, ts], ident)
                    for h in range(4):
                        ins = mm(hb(5, h), kT[:, 4 * p + h, ts], qT[:, 4 * p + h, ts], start=True, stop=True)
                    ins.then_inc(S("dl_kq"), 1)

                def from_state(u, p):
                    d, t = UNITS[u]
                    ts = slice(t * P, (t + 1) * P)
                    n = 2 * u + p
                    if n == 0:
                        pe.wait_ge(S("st_in"), 64 + 32)
                    else:
                        pe.wait_ge(S("dl_done"), n)
                    if n >= 16:
                        pe.wait_ge(S("dl_sz"), n - 15)
                    for h in range(4):
                        ins = mm(hb(6, h), kT[:, 4 * p + h, ts], Cst[:, d, 4 * p + h, :], start=True, stop=True)
                    ins.then_inc(S("dl_ks"), 1)
                    for h in range(4):
                        ins = mm(hb(7, h), qT[:, 4 * p + h, ts], Cst[:, d, 4 * p + h, :], start=True, stop=True)
                    ins.then_inc(S("dl_qs"), 1)

                def solve(u, p):
                    n = 2 * u + p
                    DT = delta_buffers(u, p)["DT"]
                    pe.wait_ge(S("dl_r"), n + 1)
                    pe.wait_ge(S("dl_dt"), at_all(u, LEVELS - 1, p))
                    for h in range(4):
                        ins = mm(hb(6, h), DT[:, h, :], Rb[:, h, :], start=True, stop=True)
                    ins.then_inc(S("dl_w"), 1)

                def outputs(u, p):
                    n = 2 * u + p
                    B = delta_buffers(u, p)
                    pe.wait_ge(S("dl_we"), n + 1)
                    for h in range(4):
                        ins = mm(hb(6, h), B["kd"][:, h, :], Wb[:, h, :], start=True, stop=True)
                    ins.then_inc(S("dl_sn"), 1)
                    pe.wait_ge(S("dl_t"), 4 * n + 4)
                    for h in range(4):
                        ins = mm(hb(7, h), B["qk"][:, h, :], Wb[:, h, :], start=True, stop=True)
                    ins.then_inc(S("dl_o"), 1)

                def fill(u, l):
                    nxt = u + 1 < len(UNITS)
                    if l in (3, 6) and nxt:
                        keys(u + 1, l // 3 - 1)
                    if u and l in (0, 3):
                        from_state(u - 1, l // 3)
                    if l in (0, 4) and nxt:
                        front(u + 1, l // 4)
                    if u and l in (1, 4):
                        solve(u - 1, l // 3)
                    if u and l in (2, 5):
                        outputs(u - 1, l // 3)

                for p in range(2):
                    front(0, p)
                    keys(0, p)
                for u, (d, t) in enumerate(UNITS):
                    first, then = parts(d)
                    for l in range(LEVELS):
                        for p in range(2):
                            B = delta_buffers(u, p)
                            bx = 2 * p + 1 - l % 2
                            if l == 0:
                                pe.wait_ge(S("dl_at"), 2 * u + p + 1)
                                if u:
                                    pe.wait_ge(S("dl_dt"), at_all(u - 1, LEVELS - 1, p))
                                for h in range(4):
                                    ins = tr(hb(2 * p, h), B["AT"][:, h, :], ident)
                            elif l < LEVELS - 1:
                                pe.wait_ge(S("dl_cm"), at_mid(u, l, p))
                                pe.wait_ge(S("dl_d"), at_early(u, l - 1, p))
                                for h in range(4):
                                    ins = mm(pack(four(PS[:, bx, :])[:, :, 0:64], l)[:, h], B["CM"][l % 2][:, h, :],
                                             cols1(B["D"][:, h, :], l, d), start=True, stop=True)
                            else:
                                pe.wait_ge(S("dl_d"), at_early(u, l - 1, p))
                                for h in range(4):
                                    ins = mm(PS[then, bx, h * P:h * P + 64], B["AT"][first, h, then],
                                             B["D"][first, h, first], start=True, stop=True)
                            ins.then_inc(S("dl_x"), 1)
                        if l == LEVELS - 1:
                            fill(u, l)
                        for p in range(2):
                            B = delta_buffers(u, p)
                            if l == 0:
                                continue
                            pe.wait_ge(S("dl_xe"), at_late(u, l, p))
                            pe.wait_ge(S("dl_dt"), at_all(u, l - 1, p))
                            for h in range(4):
                                if l < LEVELS - 1:
                                    ins = mm(hb(2 * p + l % 2, h, 64), B["DT"][:, h, :], B["X"][:, h, :], start=True, stop=True)
                                else:
                                    ins = mm(PS[first, 2 * p, h * P:h * P + 64], B["X"][then, h, :],
                                             B["DT"][then, h, then], start=True, stop=True)
                            ins.then_inc(S("dl_dx"), 1)
                        if l < LEVELS - 1:
                            fill(u, l)
                        for p in range(2):
                            if l == LEVELS - 1:
                                continue
                            pe.wait_ge(S("dl_d"), at_early(u, l, p))
                            if l == 0 and u:
                                pe.wait_ge(S("dl_xe"), at_late(u - 1, LEVELS - 1, p))
                            for h in range(4):
                                ins = tr(hb(2 * p + 1 - l % 2, h), delta_buffers(u, p)["D"][:, h, :], ident)
                            ins.then_inc(S("dl_tr"), 1)
                for l in range(LEVELS):
                    fill(len(UNITS), l)

            def mixer_tail(L):
                def turn_y(t):
                    pe.wait_ge(S("y"), L * PER["y"] + t + 1)
                    if t:
                        pe.wait_ge(S("yt_ev"), L * PER["yt_ev"] + 2 * t)
                    for kt in range(KT):
                        ins = tr(PS[:, kt // 4, (kt % 4) * P:(kt % 4 + 1) * P], acc[:, t, kt * P:(kt + 1) * P], ident)
                    ins.then_inc(S("yt"), 1)

                def out(t):
                    pe.wait_ge(S("yt_ev"), L * PER["yt_ev"] + 2 * t + 2)
                    for j in range(2):
                        i = 2 * t + j
                        if t == 0:
                            pe.wait_ge(land[j], mix_landed(L, NADA + NIN + j))
                        else:
                            pe.wait_ge(S("x_new"), L * PER["x_new"] + i - 1)
                        for kt in range(KT):
                            ins = mm(PS[:, 6 + j, :], yT[:, kt, t * P:(t + 1) * P], slot[j][:, kt, :], start=(kt == 0), stop=(kt == KT - 1))
                        ins.then_inc(S("omm"), 1)

                def logits(t):
                    turned(L, 1, t)
                    for kt in range(KT):
                        ins = mm(PS[:, 0, t * EX:(t + 1) * EX], hT[:, kt, t * P:(t + 1) * P], wrt[:, kt, :],
                                 start=(kt == 0), stop=(kt == KT - 1))
                    return ins

                turn_y(0)
                gate_rows(16, 2, S("g1b"))
                for t in range(1, NT):
                    turn_y(t)
                    out(t - 1)
                pe.wait_ge(S("g1e"), L * PER["g1e"] + 4)
                turn_tile(L, 1, 0)
                turn_tile(L, 1, 1)
                out(NT - 1)
                turn_tile(L, 1, 2)
                turn_tile(L, 1, 3)
                pe.wait_ge(S("wr_in"), 16 * (L + 1))
                logits(0)
                logits(1)
                turn_tile(L, 1, 4)
                for t in range(2, NT):
                    ins = logits(t)
                ins.then_inc(S("logits"), 1)

            def gate_rows(first, bank, sem):
                for c in range(2):
                    for j in range(2):
                        for b in range(4):
                            ins = mm(PS[:, bank + 2 * c + j, b * P:(b + 1) * P],
                                     modT[:, first + 4 * j + b, c:c + 1].broadcast_to([P, P]), ident, start=True, stop=True)
                        ins.then_inc(sem, 1)

            def experts(L):
                pe.wait_ge(S("aff"), L * PER["aff"] + 1)
                tr(PS[0:EX, 2, 0:P], aff[:, 0, :], ident)
                for t in range(1, NT):
                    ins = tr(PS[0:EX, 1, (t - 1) * P:t * P], aff[:, t, :], ident)
                ins.then_inc(S("afft"), 1)
                pe.wait_ge(S("topk"), L * PER["topk"] + 1)
                tr(PS[0:CAP, 3, 0:EX], vals[:, :], ident[0:EX, 0:EX])
                tr(PS[0:CAP, 3, EX:2 * EX], idf[:, :], ident[0:EX, 0:EX]).then_inc(S("selt"), 1)
                pe.wait_ge(S("sel"), L * PER["sel"] + 2)

                def turn(e, q, first):
                    pe.wait_ge(S("gathered"), L * PER["gathered"] + e * 16 + 16)
                    if not first:
                        pe.wait_ge(S("xs_in"), L * PER["xs_in"] + e)
                    for kt in range(KT):
                        ins = tr(PS[:, 6 + kt // 4, (kt % 4) * CAP:(kt % 4 + 1) * CAP], xs[q][0:CAP, kt * P:(kt + 1) * P], ident[0:CAP, 0:CAP])
                    ins.then_inc(S("xs_turned"), 1)

                def hidden(e, q, first):
                    pe.wait_ge(S("xs_in"), L * PER["xs_in"] + e + 1)
                    for j in range(4):
                        pe.wait_ge(land[j], e * 16 + (16 * moe_base(L, j) + 16))
                        if not first:
                            pe.wait_ge(S("hidden"), L * PER["hidden"] + e * 2 + (j // 2 - 1))
                        for fb in range(4):
                            for kt in range(KT):
                                ins = mm(PS[:, j, fb * CAP:(fb + 1) * CAP], slot[j][:, kt, fb * P:(fb + 1) * P],
                                         xsT[q][:, kt, :], start=(kt == 0), stop=(kt == KT - 1))
                        ins.then_inc(S("moe_used"), 1)

                def down(e, q, first):
                    pe.wait_ge(S("hidden"), L * PER["hidden"] + e * 2 + 2)
                    for j in range(2):
                        pe.wait_ge(land[4 + j], e * 16 + (16 * moe_base(L, 4 + j) + 16))
                        if not first:
                            pe.wait_ge(S("o_ready"), L * PER["o_ready"] + e * 2 + (j - 1))
                        for ft in range(KT):
                            ins = mm(PS[0:CAP, 4 + j, :], hdT[:, ft, :], slot[4 + j][:, ft, :],
                                     start=(ft == 0), stop=(ft == KT - 1))
                        ins.then_inc(S("moe_used"), 1)

                def keep_clock(n):
                    for _ in range(n):
                        mm(PS[:, 4, :], ident, hT[:, 0, 0:HC], start=True, stop=True)

                keep_clock(5)
                turn(0, 0, True)
                keep_clock(3)
                hidden(0, 0, True)
                turn(1, 1, False)
                down(0, 0, True)
                hidden(1, 1, False)
                turn(2, 0, False)
                down(1, 1, False)
                with pe.Fori(1, EX // 2 - 1) as i:
                    for q in range(2):
                        e = i * 2 + q
                        hidden(e, q, False)
                        turn(i * 2 + (q + 1), 1 - q, False)
                        down(e, q, False)
                hidden(EX - 2, 0, False)
                turn(EX - 1, 1, False)
                down(EX - 2, 0, False)
                hidden(EX - 1, 1, False)
                down(EX - 1, 1, False)
                pe.wait_ge(S("hidden"), L * PER["hidden"] + 2 * EX)
                gate_rows(40, 0, S("g2b"))

            for L in range(2):
                modulation(L)
                norm_turn(L, 0)
                if L == 0:
                    proj_mlstm()
                    scan_mlstm()
                else:
                    proj_delta()
                    scan_delta()
                mixer_tail(L)
                experts(L)

        @block.vector
        def _(dve):
            V = nc.vector
            chain = [0]

            def link(ins):
                chain[0] += 1
                ins.then_inc(S("dve_chain"), 1)
                dve.wait_ge(S("dve_chain"), chain[0])

            dve.wait_ge(S("vect"), 1)
            V.tensor_copy(vecT[:, :], PS[:, 0, 0:264]).then_inc(S("vec"), 1)
            dve.wait_ge(S("vec"), 1)
            link(V.tensor_scalar(convT, convT, 0.5, None, ALU.mult))
            dve.wait_ge(S("cexp"), 1)
            link(V.tensor_scalar(cnd[:, 0, :], cnd[:, 0, :], 1.0, None, ALU.add))
            link(V.reciprocal(cnd[:, 0, :], cnd[:, 0, :]))
            V.tensor_tensor(cnd[:, 1, :], cnd[:, 0, :], vecT[:, 32:48], ALU.mult).then_inc(S("cond"), 1)

            def modulation(L):
                dve.wait_ge(S("ada_tr"), (L + 1) * NADA)
                link(V.tensor_tensor(modT[:, :, :], PS[:, 6, 0:96].rearrange("p (b c) -> p b c", c=2),
                                     biasT[:, L, :].unsqueeze(2).broadcast_to([P, MOD, 2]), ALU.add))
                for k in range(2):
                    ins = V.scalar_tensor_tensor(AB[:, k, :, :], modT[:, 8 + 24 * k:16 + 24 * k, :], 1.0,
                                                 norm_g[:, k, L, :].unsqueeze(2).broadcast_to([P, KT, 2]), ALU.add, ALU.mult)
                    if k == 0:
                        link(ins)
                ins.then_inc(S("ab"), 1)
                dve.wait_ge(S("ab"), L * PER["ab"] + 1)

            def sharpen(first, last, scale, gain=1.0):
                w, y, vv, tt = (ss[:, j, first:last] for j in range(4))
                link(V.tensor_scalar(vv, w, scale, EPS, ALU.mult, ALU.add))
                link(V.scalar_tensor_tensor(tt, y, -0.5 * gain, y, ALU.mult, ALU.mult))
                link(V.tensor_tensor(tt, tt, vv, ALU.mult))
                link(V.scalar_tensor_tensor(y, tt, 1.5 * gain, y, ALU.add, ALU.mult))

            def norm_tile(i, t):
                dve.wait_ge(S("sq"), i * PER["sq"] + t + 1)
                sharpen(t, t + 1, 1.0 / D)
                r = ss[:, 1, t:t + 1]
                if i < 4:
                    V.tensor_scalar(o[:, t, :], x[:, t, :], r, None, ALU.mult).then_inc(S("xn"), 1)
                else:
                    V.scalar_tensor_tensor(o[:, t, :], x[:, t, :], r, grow, ALU.mult, ALU.mult).then_inc(S("y_ready"), 1)

            def evac_tile(i, t):
                k = i % 2
                c = int(t > 0)
                dve.wait_ge(S("xt"), i * PER["xt"] + 2 * t + 2)
                dst = hT[:, 4:8, t * P:(t + 1) * P]
                link(V.tensor_tensor(dst, four(PS[:, 2 * (t % 2) + 3, :]), heads(AB[:, k, 4:8, c]), ALU.mult))
                V.tensor_tensor(dst, dst, heads(modT[:, 24 * k + 4:24 * k + 8, c]), ALU.add).then_inc(S("htv"), 1)

            def gates_mlstm():
                f, ig = gt[:, :, :, 1, :], gt[:, :, :, 0, :]
                dve.wait_ge(S("gmm"), 1)
                link(V.tensor_tensor(gt[:, :, :, :, :].rearrange("p t d k h -> p t (d k h)"),
                                     PS[:, 7, 0:160].rearrange("p (t c) -> p t c", t=NT),
                                     gb0[:, :, :, :].rearrange("p d k h -> p (d k h)").unsqueeze(1).broadcast_to([P, NT, 32]), ALU.add))
                V.scalar_tensor_tensor(G3[0], f, -1.0, f, ALU.mult, ALU.max).then_inc(S("g0"), 1)
                dve.wait_ge(S("g0a"), 2)
                V.scalar_tensor_tensor(G3[2], f, 0.0, G3[1], ALU.min, ALU.subtract).then_inc(S("lf"), 1)
                dve.wait_ge(S("bsum"), 1)
                link(V.tensor_copy(G3[4], PS[:, 7, 0:80].rearrange("p (d t h) -> p t d h", d=2, t=NT)))
                link(V.tensor_copy(ga[:, 5, :], PS[:, 7, 80:160]))
                V.tensor_tensor(G3[3], ig, G3[4], ALU.subtract).then_inc(S("aready"), 1)
                dve.wait_ge(S("aready"), 1)
                for n in range(20):
                    d, t = UNITS[n // 2]
                    p = n % 2
                    dve.wait_ge(S("amm"), n + 1)
                    V.tensor_reduce(G3[6][:, t, d, 4 * p:4 * p + 4], four(PS[:, 6, :]), AX, ALU.max).then_inc(S("mxr"), 1)
                dve.wait_ge(S("mxr"), 20)
                dve.wait_ge(S("mlast"), 1)
                link(V.tensor_copy(G3[7], PS[:, 7, 0:80].rearrange("p (d t h) -> p t d h", d=2, t=NT)))
                link(V.memset(G3[13][:, 0, :, :], 0.0))
                link(V.tensor_copy(G3[13][:, 1, 0, :], m0[:, 0, :]))
                link(V.tensor_copy(G3[13][:, 4, 1, :], m0[:, 1, :]))
                for s in range(4):
                    for d in range(2):
                        t = 1 + s if d == 0 else 4 - s
                        link(V.tensor_tensor(G3[7][:, t, d, :], G3[7][:, t, d, :], G3[13][:, t, d, :], ALU.max))
                        if s < 3:
                            t2 = t + 1 if d == 0 else t - 1
                            link(V.tensor_tensor(G3[13][:, t2, d, :], G3[7][:, t, d, :], G3[5][:, t, d, :], ALU.add))
                link(V.tensor_tensor(G3[7][:, 0, :, :], G3[7][:, 0, :, :], G3[13][:, 0, :, :], ALU.max))
                link(V.tensor_tensor(ga[:, 6, :], ga[:, 6, :], ga[:, 13, :], ALU.max))
                V.tensor_scalar(ga[:, 8, :], ga[:, 6, :], -1.0, None, ALU.mult).then_inc(S("nm"), 1)
                link(V.tensor_tensor(ga[:, 9, :], ga[:, 13, :], ga[:, 6, :], ALU.subtract))
                link(V.tensor_tensor(ga[:, 10, :], ga[:, 3, :], ga[:, 7, :], ALU.subtract))
                link(V.tensor_tensor(ga[:, 11, :], ga[:, 13, :], ga[:, 7, :], ALU.subtract))
                link(V.scalar_tensor_tensor(ga[:, 12, :], ga[:, 4, :], -1.0, ga[:, 6, :], ALU.mult, ALU.subtract))
                link(V.tensor_tensor(G3[13][:, 0, :, :], G3[7][:, 0, :, :], G3[5][:, 0, :, :], ALU.add))
                dve.sem_inc(S("g0"), 1)
                dve.wait_ge(S("g0a"), 6)

            def scan_mlstm():
                SC, Wt, DEC, EM = G3[9], G3[10], G3[11], G3[12]

                def mid(n):
                    d, t = UNITS[n // 2]
                    p = n % 2
                    E, PSb, kw = (four(half[4 * p + j]) for j in range(3))
                    dve.wait_ge(S("ml_s"), n + 1)
                    V.tensor_tensor(kw, four(PS[:, 3, :]), heads(Wt[:, t, d, 4 * p:4 * p + 4]), ALU.mult)
                    dve.wait_ge(S("ml_e"), 4 * n + 4)
                    V.tensor_tensor(PSb, four(PS[:, 2, :]), E, ALU.mult).then_inc(S("ml_ps"), 1)

                def end(n):
                    d, t = UNITS[n // 2]
                    p = n % 2
                    hs = slice(4 * p, 4 * p + 4)
                    b7 = PS[:, 7, 16 * p:16 * p + 12]
                    dve.wait_ge(S("ml_sum"), n + 1)
                    den = sm[:, p, 0, :]
                    link(V.tensor_tensor(den, b7[:, 4:8], SC[:, t, d, hs], ALU.mult))
                    link(V.tensor_tensor(den, den, b7[:, 0:4], ALU.add))
                    link(V.scalar_tensor_tensor(den, den, -1.0, den, ALU.mult, ALU.max))
                    link(V.tensor_tensor(den, den, EM[:, t, d, hs], ALU.max))
                    link(V.reciprocal(sm[:, p, 1, :], den))
                    link(V.tensor_tensor(sm[:, p, 3, :], sm[:, p, 1, :], SC[:, t, d, hs], ALU.mult))
                    link(V.tensor_tensor(nst[:, d, hs], nst[:, d, hs], DEC[:, t, d, hs], ALU.mult))
                    V.tensor_tensor(nst[:, d, hs], nst[:, d, hs], b7[:, 8:12], ALU.add)
                    dve.wait_ge(S("ml_qc"), n + 1)
                    for h in range(4):
                        hh = 4 * p + h
                        ins = V.scalar_tensor_tensor(Cst[:, d, hh, :], Cst[:, d, hh, :], DEC[:, t, d, hh:hh + 1],
                                                     PS[:, 4, h * P:(h + 1) * P], ALU.mult, ALU.add)
                    ins.then_inc(S("ml_c"), 1)
                    if n >= 16:
                        dve.wait_ge(S("ml_c"), n + 1)
                        dve.sem_inc(S("st_new"), 1)
                    if 12 <= n < 16:
                        dve.wait_ge(S("ml_c"), n + 1)
                        V.memset(nst[:, d, hs], 0.0)
                        V.memset(Cst[:, d, hs, :], 0.0).then_inc(S("ml_cz"), 1)
                        dve.wait_ge(S("ml_cz"), n - 11)
                    dst = acc[:, t, p * HC:(p + 1) * HC]
                    for h in range(4):
                        r = sm[:, p, 3, h:h + 1]
                        b5, o_ = PS[:, 5, h * P:(h + 1) * P], dst[:, h * P:(h + 1) * P]
                        if (d, t) in SECOND:
                            ins = V.scalar_tensor_tensor(o_, b5, r, o_, ALU.mult, ALU.add)
                        else:
                            ins = V.tensor_scalar(o_, b5, r, None, ALU.mult)
                        ins.then_inc(S("ml_ti"), 1)
                    dve.wait_ge(S("ml_bk"), n + 1)
                    dve.wait_ge(S("ml_ti"), 4 * n + 4)
                    for h in range(4):
                        o_ = dst[:, h * P:(h + 1) * P]
                        ins = V.scalar_tensor_tensor(o_, PS[:, 6, h * P:(h + 1) * P], sm[:, p, 1, h:h + 1], o_, ALU.mult, ALU.add)
                    ins.then_inc(S("ml_done"), 1)
                    dve.wait_ge(S("ml_done"), n + 1)

                dve.wait_ge(S("st_in"), 64)
                dve.wait_ge(S("pj_ev0"), 36)
                mid(0)
                for n in range(20):
                    if n + 1 < 20:
                        mid(n + 1)
                    end(n)
                dve.sem_inc(S("fin_start"), 1)

            def gates_delta():
                dve.wait_ge(S("gmm"), PER['gmm'] + 1)
                g4 = PS[:, 7, 0:160].rearrange("p (t d k h) -> p t d k h", t=NT, d=2, k=2)
                for d in range(2):
                    V.tensor_tensor(G3[2][:, :, d, :], g4[:, :, d, 0, :], gb1[:, d, 1, :].unsqueeze(1).broadcast_to([P, NT, H]), ALU.add).then_inc(S("gev1"), 1)
                    V.tensor_copy(G3[4][:, :, d, :], g4[:, :, d, 1, :]).then_inc(S("gev1"), 1)
                dve.wait_ge(S("gev1"), 4)
                V.scalar_tensor_tensor(ga[:, 0, :], ga[:, 2, :], -1.0, ga[:, 2, :], ALU.mult, ALU.max).then_inc(S("g1"), 1)
                dve.wait_ge(S("g1a"), 4)
                link(V.scalar_tensor_tensor(ga[:, 3, :], ga[:, 2, :], 0.0, ga[:, 1, :], ALU.max, ALU.add))
                link(V.tensor_scalar(gb1[:, :, 0, :], gb1[:, :, 0, :], -1.0, None, ALU.mult))
                for d in range(2):
                    ins = V.tensor_tensor(G3[3][:, :, d, :], G3[3][:, :, d, :], gb1[:, d, 0, :].unsqueeze(1).broadcast_to([P, NT, H]), ALU.mult)
                    ins.then_inc(S("gl0"), 1)
                dve.wait_ge(S("gl0"), 2)
                link(V.tensor_scalar(ga[:, 4, :], ga[:, 4, :], 1.0, None, ALU.add))
                V.reciprocal(ga[:, 4, :], ga[:, 4, :]).then_inc(S("gl"), 1)
                dve.wait_ge(S("gl"), 1)

            def sums_delta():
                dve.wait_ge(S("gsum"), 1)
                link(V.tensor_copy(GC, PS[:, 7, 0:80].rearrange("p (d t h) -> p t d h", d=2, t=NT)))
                link(V.tensor_copy(ga[:, 8, :], PS[:, 7, 80:160]))
                link(V.tensor_scalar(ga[:, 6, :], ga[:, 5, :], -1.0, None, ALU.mult))
                link(V.tensor_copy(ga[:, 7, :], ga[:, 5, :]))
                V.tensor_tensor(ga[:, 9, :], ga[:, 8, :], ga[:, 5, :], ALU.subtract).then_inc(S("g1"), 1)
                dve.wait_ge(S("g1"), 2)
                dve.wait_ge(S("g1a"), 7)
                link(V.tensor_scalar(ga[:, 10, :], ga[:, 4, :], -1.0, None, ALU.mult))
                V.tensor_scalar(ga[:, 11, :], ga[:, 7, :], -1.0, None, ALU.mult).then_inc(S("gready"), 1)
                dve.wait_ge(S("gready"), 1)

            def proj_delta():
                for q in range(2):
                    V.memset(cpad[q], 0.0).then_inc(S("padded"), 1)
                dve.wait_ge(S("padded"), 2)

                def conv(i):
                    dve.wait_ge(S("pj_ev1"), i + 1)
                    if i >= 2:
                        dve.wait_ge(S("tr1"), i - 1)
                    src, dst = cpad[i % 2], cout[i % 2]
                    for j in range(TAPS):
                        w = convT[:, j, i:i + 1]
                        for s, o_ in ((src[:, j:j + P].unsqueeze(1), dst[:, 0:P].unsqueeze(1)),
                                      (src[:, 132:676].rearrange("p (r w) -> p r w", r=NROW)[:, :, j:j + ROWW],
                                       dst[:, P:TOK].rearrange("p (r w) -> p r w", r=NROW))):
                            if j == 0:
                                ins = V.tensor_scalar(o_, s, w, None, ALU.mult)
                            else:
                                ins = V.scalar_tensor_tensor(o_, s, w, o_, ALU.mult, ALU.add)
                            if j == TAPS - 1 and s is not None and o_.shape[1] == NROW:
                                ins.then_inc(S("cv_done"), 1)
                                dve.wait_ge(S("cv_done"), i + 1)
                            else:
                                link(ins)

                def normed(i):
                    dve.wait_ge(S("sqj"), i + 1)
                    sharpen(0, NT, 1.0, float(P) ** -0.5 if i < 8 else 1.0)
                    if i:
                        dve.wait_ge(S("tr2"), i)
                    link(V.tensor_tensor(qn[:, 0:4, :], four(PS[:, 4, :]), heads(ss[:, 1, 0:4]), ALU.mult))
                    V.tensor_scalar(qn[:, 4, :], PS[:, 5, 0:P], ss[:, 1, 4:5], None, ALU.mult).then_inc(S("qn"), 1)

                for i in range(25):
                    if i < 24:
                        conv(i)
                    if 1 <= i and i - 1 < 16:
                        normed(i - 1)
                    if i < 24:
                        dve.wait_ge(S("cvexp"), i + 1)
                        V.scalar_tensor_tensor(cout[i % 2], cex, 1.0, cout[i % 2], ALU.add, ALU.mult).then_inc(S("silu"), 1)
                        dve.wait_ge(S("silu"), i + 1)

            def scan_delta():
                dve.wait_ge(S("st_in"), 96)

                def system(u, p):
                    B = delta_buffers(u, p)
                    n = 2 * u + p
                    dve.wait_ge(S("dl_kk"), n + 1)
                    dve.wait_ge(S("dl_e"), 4 * n + 4)
                    if u >= 2:
                        dve.wait_ge(S("dl_x"), at_all(u - 2, LEVELS - 1, p))
                    V.tensor_tensor(B["AT"], four(PS[:, 5, :]), B["E"], ALU.mult).then_inc(S("dl_at"), 1)

                def keys(u, p):
                    d, t = UNITS[u]
                    B = delta_buffers(u, p)
                    n = 2 * u + p
                    dve.wait_ge(S("dl_kq"), n + 1)
                    if u >= 2:
                        dve.wait_ge(S("dl_o"), 2 * (u - 2) + p + 1)
                    V.tensor_tensor(B["qk"], four(PS[:, 5, :]), B["E"], ALU.mult)
                    V.tensor_tensor(B["kd"], four(PS[:, 4, :]), heads(EKD[:, t, d, 4 * p:4 * p + 4]), ALU.mult).then_inc(S("dl_kd"), 1)

                def right_side(u, p):
                    d, t = UNITS[u]
                    n = 2 * u + p
                    dve.wait_ge(S("dl_ks"), n + 1)
                    if n:
                        dve.wait_ge(S("dl_w"), n)
                    for h in range(4):
                        hh = 4 * p + h
                        ins = V.scalar_tensor_tensor(Rb[:, h, :], PS[:, 6, h * P:(h + 1) * P], NEG[:, t, d, hh:hh + 1],
                                                     v[:, t, hh * P:(hh + 1) * P], ALU.mult, ALU.add)
                    link(ins)
                    V.tensor_tensor(Rb, Rb, heads(BETA[:, t, d, 4 * p:4 * p + 4]), ALU.mult).then_inc(S("dl_r"), 1)

                def end(u, p):
                    d, t = UNITS[u]
                    n = 2 * u + p
                    hs = slice(4 * p, 4 * p + 4)
                    dve.wait_ge(S("dl_sn"), n + 1)
                    for h in range(4):
                        hh = 4 * p + h
                        ins = V.scalar_tensor_tensor(Cst[:, d, hh, :], Cst[:, d, hh, :], EGL[:, t, d, hh:hh + 1],
                                                     PS[:, 6, h * P:(h + 1) * P], ALU.mult, ALU.add)
                    ins.then_inc(S("dl_s"), 1)
                    if n >= 16:
                        dve.wait_ge(S("dl_s"), n + 1)
                        dve.sem_inc(S("st_new"), 1)
                    if 12 <= n < 16:
                        dve.wait_ge(S("dl_s"), n + 1)
                        V.memset(Cst[:, d, hs, :], 0.0).then_inc(S("dl_sz"), 1)
                        dve.wait_ge(S("dl_sz"), n - 11)
                    dst = four(acc[:, t, p * HC:(p + 1) * HC])
                    if (d, t) in SECOND:
                        dve.wait_ge(S("dl_t"), 4 * n + 4)
                        link(V.tensor_tensor(tb, tb, dst, ALU.add))
                    dve.wait_ge(S("dl_o"), n + 1)
                    V.tensor_tensor(dst, four(PS[:, 7, :]), tb, ALU.add).then_inc(S("dl_done"), 1)
                    dve.wait_ge(S("dl_done"), n + 1)

                def mask_next(u, l, p):
                    d = UNITS[u][0]
                    if l + 1 < LEVELS - 1:
                        B = delta_buffers(u, p)
                        mk = lmask[:, d * LEVELS + l + 1, :].bitcast(BF16).unsqueeze(1).broadcast_to([P, 4, P])
                        V.tensor_tensor(B["CM"][(l + 1) % 2], B["AT"], mk, ALU.mult).then_inc(S("dl_cm"), 1)

                def fill(u, l):
                    nxt = u + 1 < len(UNITS)
                    if l in (3, 6) and nxt:
                        keys(u + 1, l // 3 - 1)
                    if u and l in (0, 3):
                        right_side(u - 1, l // 3)
                    if l in (2, 5):
                        if nxt:
                            system(u + 1, l // 3)
                        if u:
                            end(u - 1, l // 3)

                for p in range(2):
                    system(0, p)
                    keys(0, p)
                for u, (d, t) in enumerate(UNITS):
                    first, then = parts(d)
                    for l in range(LEVELS):
                        for p in range(2):
                            B = delta_buffers(u, p)
                            bx = 2 * p + 1 - l % 2
                            if l == 0:
                                dve.wait_ge(S("dl_x"), at_all(u, l, p))
                                mk = lmask[:, (1 - d) * LEVELS, :].bitcast(BF16).unsqueeze(1).broadcast_to([P, 4, P])
                                link(V.tensor_tensor(B["D"], four(PS[:, 2 * p, :]), mk, ALU.mult))
                                for h in range(4):
                                    hh = 4 * p + h
                                    ins = V.scalar_tensor_tensor(B["D"][:, h, :], B["D"][:, h, :], NBETA[:, t, d, hh:hh + 1],
                                                                 ident, ALU.mult, ALU.add)
                                ins.then_inc(S("dl_d"), 1)
                            else:
                                dve.wait_ge(S("dl_x"), at_all(u, l, p))
                                rows_ = slice(0, P) if l < LEVELS - 1 else then
                                V.tensor_tensor(B["X"][rows_], four(PS[rows_, bx, :])[:, :, 0:64],
                                                heads(BETA[rows_, t, d, 4 * p:4 * p + 4], 64), ALU.mult).then_inc(S("dl_xe"), 1)
                            if l:
                                mask_next(u, l, p)
                        for p in range(2):
                            if l == 0:
                                mask_next(u, l, p)
                            if l in (0, LEVELS - 1):
                                continue
                            dst = cols(delta_buffers(u, p)["D"], l, d)
                            dve.wait_ge(S("dl_dx"), at_late(u, l, p))
                            V.tensor_tensor(dst, dst, pack(four(PS[:, 2 * p + l % 2, :])[:, :, 0:64], l), ALU.subtract).then_inc(S("dl_d"), 1)
                        fill(u, l)
                for l in range(LEVELS):
                    fill(len(UNITS), l)
                dve.sem_inc(S("fin_start"), 1)

            def gate_tile(L, t):
                dve.wait_ge(S("fin_sq"), L * PER["fin_sq"] + t + 1)
                y = acc[:, t, :]
                y8 = y.rearrange("p (h n) -> p h n", h=H)
                r = ss[:, 0, 8:16]
                V.tensor_reduce(r, fsq.rearrange("p (h n) -> p h n", h=H), AX, ALU.add).then_inc(S("fin_r"), 1)
                dve.wait_ge(S("fin_i"), L * PER["fin_i"] + t + 1)
                sharpen(8, 16, 1.0 / P, 0.5)
                link(V.tensor_tensor(y8, y8, heads(ss[:, 1, 8:16]), ALU.mult))
                V.tensor_tensor(y, y, o[:, t, :], ALU.mult).then_inc(S("y"), 1)

            def output_gates(L):
                if L == 0:
                    dve.wait_ge(S("grow_in"), 16)
                for k in range(2 * NT):
                    j, t = divmod(k, NT)
                    dst = o[:, t, j * HC:(j + 1) * HC]
                    dve.wait_ge(S(f"pj_ev{L}"), (26, 24)[L] + k + 1)
                    if L == 0:
                        V.scalar_tensor_tensor(dst, dst, 1.0, grow[:, j * HC:(j + 1) * HC], ALU.add, ALU.mult).then_inc(S("og"), 1)
                    else:
                        link(V.scalar_tensor_tensor(dst, gtmp[k % 2], 1.0, dst, ALU.add, ALU.mult))
                        V.tensor_tensor(four(dst), four(dst), dng[:, :].unsqueeze(1).broadcast_to([P, 4, P]), ALU.mult).then_inc(S("og"), 1)
                dve.wait_ge(S("og"), 10 * (L + 1))

            def x_tile(L, t):
                c = int(t > 0)
                for j in range(2):
                    i = 2 * t + j
                    dve.wait_ge(S("omm"), L * PER["omm"] + i + 1)
                    if i == 0:
                        dve.wait_ge(S("g1e"), L * PER["g1e"] + 4)
                    link(V.tensor_tensor(ytmp, PS[:, 6 + j, :], g1b[:, c, j, :], ALU.mult))
                    xx = x[:, t, j * HC:(j + 1) * HC]
                    V.tensor_tensor(xx, xx, ytmp, ALU.add).then_inc(S("x_new"), 1)
                    dve.wait_ge(S("x_new"), L * PER["x_new"] + i + 1)

            def mixer_tail(L):
                n = 2 * L + 1
                gate_tile(L, 0)
                gate_tile(L, 1)
                for t in range(2, NT):
                    gate_tile(L, t)
                    x_tile(L, t - 2)
                for t in range(3):
                    norm_tile(n, t)
                x_tile(L, 3)
                norm_tile(n, 3)
                evac_tile(n, 0)
                evac_tile(n, 1)
                x_tile(L, 4)
                norm_tile(n, 4)
                for t in range(2, NT):
                    evac_tile(n, t)

            def experts(L):
                dve.wait_ge(S("logits"), L * PER["logits"] + 1)
                lg = PS[:, 0, 0:80].rearrange("p (t e) -> p t e", t=NT)
                link(V.tensor_reduce(af5[:, 0, :], lg, AX, ALU.max))
                V.tensor_tensor(aff[:, :, :], lg, heads(af5[:, 0, :], EX), ALU.subtract).then_inc(S("sm"), 1)
                dve.wait_ge(S("sme"), L * PER["sme"] + 1)
                link(V.tensor_reduce(af5[:, 1, :], aff[:, :, :], AX, ALU.add))
                link(V.reciprocal(af5[:, 1, :], af5[:, 1, :]))
                V.tensor_tensor(aff[:, :, :], aff[:, :, :], heads(af5[:, 1, :], EX), ALU.mult).then_inc(S("aff"), 1)
                dve.wait_ge(S("afft"), L * PER["afft"] + 1)
                link(V.tensor_copy(affP, PS[0:EX, 2, 0:P]))
                link(V.tensor_copy(affS, PS[0:EX, 1, :]))
                for src, first, cap in ((affS, 0, CAPS), (affP, CAPS, CAPP)):
                    for r in range(cap // 8):
                        s8 = slice(first + 8 * r, first + 8 * r + 8)
                        link(V.max(vals[:, s8], src))
                        link(V.max_index(idx[:, s8], vals[:, s8], src))
                        if r < cap // 8 - 1:
                            link(V.match_replace(src, vals[:, s8], src, -1.0))
                link(V.tensor_copy(idf[:, :], idx[:, :]))
                V.tensor_scalar(idf[:, 0:CAPS], idf[:, 0:CAPS], float(P), None, ALU.add).then_inc(S("topk"), 1)
                dve.wait_ge(S("selt"), L * PER["selt"] + 1)
                V.tensor_copy(gsel[0:CAP, :], PS[0:CAP, 3, 0:EX]).then_inc(S("sel"), 1)
                V.tensor_copy(idT[0:CAP, :], PS[0:CAP, 3, EX:2 * EX]).then_inc(S("sel"), 1)
                dve.wait_ge(S("sel"), L * PER["sel"] + 2)

                def pick(e, q, first):
                    if not first:
                        dve.wait_ge(S("scattered"), L * PER["scattered"] + (e - 1) * 16)
                    V.tensor_copy(idc[q][0:CAP, :], idT[0:CAP, bass.ds(e, 1)])
                    V.tensor_copy(gsc[q][0:CAP, :], gsel[0:CAP, bass.ds(e, 1)]).then_inc(S("idx"), 1)

                def tokens(e, q, first):
                    dve.wait_ge(S("xs_turned"), L * PER["xs_turned"] + e + 1)
                    for j in range(2):
                        b = PS[:, 6 + j, 0:4 * CAP].rearrange("p (k c) -> p k c", k=4)
                        for c, cs in ((1, slice(0, CAPS)), (0, slice(CAPS, CAP))):
                            V.tensor_tensor(xsT[q][:, 4 * j:4 * j + 4, cs], b[:, :, cs],
                                            heads(AB[:, 1, 4 * j:4 * j + 4, c], cs.stop - cs.start), ALU.mult).then_inc(S("xs_a"), 1)
                    dve.wait_ge(S("xs_a"), L * PER["xs_a"] + e * 4 + 4)
                    for c, cs in ((1, slice(0, CAPS)), (0, slice(CAPS, CAP))):
                        ins = V.tensor_tensor(xsT[q][:, :, cs], xsT[q][:, :, cs], heads(modT[:, 24:32, c], cs.stop - cs.start), ALU.add)
                    ins.then_inc(S("xs_in"), 1)

                def hidden(e, q, first):
                    for hf in range(2):
                        k = S("h_chain")
                        dve.wait_ge(S("gexp"), L * PER["gexp"] + e * 2 + (hf + 1))
                        V.scalar_tensor_tensor(eb[hf], eb[hf], 1.0, PS[:, 2 * hf, 0:320], ALU.add, ALU.mult).then_inc(k, 1)
                        dve.wait_ge(k, L * PER["h_chain"] + e * 2 + (hf + 1))
                        dve.wait_ge(S("moe_used"), L * PER["moe_used"] + e * 6 + (2 * hf + 2))
                        V.scalar_tensor_tensor(hdT[:, 4 * hf:4 * hf + 4, :], eb[hf].rearrange("p (k c) -> p k c", k=4), 0.5,
                                        PS[:, 2 * hf + 1, 0:320].rearrange("p (k c) -> p k c", k=4), ALU.mult, ALU.mult).then_inc(S("hidden"), 1)

                pick(0, 0, True)
                tokens(0, 0, True)
                pick(1, 1, True)
                hidden(0, 0, True)
                tokens(1, 1, False)
                pick(2, 0, False)
                hidden(1, 1, False)
                tokens(2, 0, False)
                with dve.Fori(1, EX // 2 - 1) as i:
                    for q in range(2):
                        pick(i * 2 + (q + 1), 1 - q, False)
                        hidden(i * 2 + q, q, False)
                        tokens(i * 2 + (q + 1), 1 - q, False)
                pick(EX - 1, 1, False)
                hidden(EX - 2, 0, False)
                tokens(EX - 1, 1, False)
                hidden(EX - 1, 1, False)

                dve.wait_ge(S("g2b"), L * PER["g2b"] + 4)
                dve.wait_ge(S("moe_in"), 16 * NT * (L + 1))
                for t in range(NT):
                    c = int(t > 0)
                    oo = o[:, t, :].rearrange("p (j n) -> p j n", j=2)
                    link(V.tensor_tensor(oo, oo, PS[:, 2 * c:2 * c + 2, :], ALU.mult))
                    V.tensor_tensor(x[:, t, :], x[:, t, :], o[:, t, :], ALU.add).then_inc(S("x_moe"), 1)
                    dve.wait_ge(S("x_moe"), L * PER["x_moe"] + t + 1)

            for L in range(2):
                for t in range(NT):
                    norm_tile(2 * L, t)
                modulation(L)
                for t in range(NT):
                    evac_tile(2 * L, t)
                if L == 0:
                    gates_mlstm()
                    output_gates(0)
                    scan_mlstm()
                else:
                    gates_delta()
                    proj_delta()
                    output_gates(1)
                    sums_delta()
                    scan_delta()
                mixer_tail(L)
                experts(L)
            dve.wait_ge(S("grow_in"), 32)
            for t in range(NT):
                norm_tile(4, t)


_INS = ['x_prompt', 'x_sample', 'state_mlstm_C', 'state_mlstm_n', 'state_mlstm_m', 'state_delta_S', 'c', 'c_ctx',
        'norm1_g', 'norm2_g', 'w_ada', 'b_ada', 'w_in', 'w_out', 'w_router', 'w_gate', 'w_up', 'w_down', 'final_g',
        'mlstm_ig_b', 'mlstm_fg_b', 'mlstm_norm_g', 'delta_conv_w', 'delta_A_log', 'delta_dt_bias', 'delta_norm_g']
_OUTS = [('out_p', (1, 128, 1024)), ('out_s', (1, 512, 1024)), ('out_C', (1, 1, 2, 8, 128, 128)),
         ('out_n', (1, 1, 2, 8, 128)), ('out_m', (1, 1, 2, 8)), ('out_S', (1, 1, 2, 8, 128, 128))]


def _constants():
    import numpy as np

    r, c = np.arange(128)[:, None], np.arange(128)[None, :]
    c32 = np.stack([r == c, r <= c, r >= c, np.ones((128, 128))], 1).astype(np.float32)
    lm = []
    for d in range(2):
        for l in range(7):
            s = 2 ** l
            br, bcol = r // s, c // s
            if d == 0:
                lm.append((br % 2 == 0) & (bcol == br + 1))
            else:
                lm.append((br % 2 == 1) & (bcol == br - 1))
    one, big = np.uint16(0x3F80), np.uint16(0xF149)
    bits = [m * one for m in lm] + [(r == c) * one, (r > c) * big, (r < c) * big]
    return c32, np.stack(bits, 1).astype(np.uint16)


def kernel(**inputs):
    import numpy as _np
    import concourse.bacc as _bacc
    from concourse import mybir as _mybir
    from concourse.bass_utils import run_bass_kernel_spmd as _run

    nc = _bacc.Bacc("TRN2", target_bir_lowering=False, num_devices=1)
    arrays, args = {}, {}
    c32, lm = _constants()
    for name, arr in [(n, inputs[n]) for n in _INS] + [("c32", c32), ("lmask", lm)]:
        arr = _np.ascontiguousarray(arr)
        arrays[f"in_{name}_dram"] = arr
        args[name] = nc.dram_tensor(f"in_{name}_dram", arr.shape, _mybir.dt.from_np(arr.dtype), kind="ExternalInput").ap()
    for name, shape in _OUTS:
        args[name] = nc.dram_tensor(f"{name}_dram", shape, _mybir.dt.float32, kind="ExternalOutput").ap()
    backbone(nc, args)
    r = _run(nc, [arrays], core_ids=[0])
    return tuple(r.results[0][f"{name}_dram"] for name, _ in _OUTS)
```
